# Optimizing a Trainium2 kernel written in Bass

```python
import math
import jax
import jax.numpy as jnp
from jax import lax
import numpy as np

D_MODEL = 1024
BATCH = 1
SEQ = 256
DEPTH = 2

N_Q_HEADS = 16
N_KV_HEADS = 4
HEAD_DIM = D_MODEL // N_Q_HEADS
Q_PER_KV = N_Q_HEADS // N_KV_HEADS
WINDOW = 128
ATTN_BLOCK = 128
QKV_WIDTH = (N_Q_HEADS + 2 * N_KV_HEADS) * HEAD_DIM
N_BUCKETS = 32
MAX_DISTANCE = 128
SSM_EXPAND = 2
D_INNER = SSM_EXPAND * D_MODEL
SSM_HEAD_DIM = 64
N_SSM_HEADS = D_INNER // SSM_HEAD_DIM
N_SSM_GROUPS = 4
SSM_HEADS_PER_GROUP = N_SSM_HEADS // N_SSM_GROUPS
D_STATE = 128
CONV_WIDTH = 4
SSM_CHUNK = 128
D_XBC = D_INNER + 2 * N_SSM_GROUPS * D_STATE
D_IN_PROJ = D_INNER + D_XBC + N_SSM_HEADS
D_FF = 7 * D_MODEL // 2
N_EXPERTS = 8
TOP_K = 2
N_ATTN_LAYERS = (DEPTH + 1) // 2
N_SSM_LAYERS = DEPTH // 2
NORM_EPS = 1e-6

kernel_name = 'swa_sink_ssd_moe_hybrid'

def rms_norm(x, w, eps=NORM_EPS):
    xf = x.astype(jnp.float32)
    y = xf * lax.rsqrt(jnp.mean(xf * xf, axis=-1, keepdims=True) + eps)
    return (y * w.astype(jnp.float32)).astype(x.dtype)

def modulate(x, gain, shift, scale):
    return rms_norm(x, gain) * (1 + scale[:, None, :]) + shift[:, None, :]

def t5_causal_bucket(dist):
    max_exact = N_BUCKETS // 2
    d = jnp.maximum(dist, 0)
    df = jnp.maximum(d, 1).astype(jnp.float32)
    large = max_exact + (jnp.log(df / max_exact) / math.log(MAX_DISTANCE / max_exact)
                         * (N_BUCKETS - max_exact)).astype(jnp.int32)
    large = jnp.minimum(large, N_BUCKETS - 1)
    return jnp.where(d < max_exact, d, large)

def band_bias_and_mask(rel_bias, n_blocks):
    qi = jnp.arange(ATTN_BLOCK)[:, None]
    kj = jnp.arange(2 * ATTN_BLOCK)[None, :]
    dist = qi + ATTN_BLOCK - kj
    bias = rel_bias.astype(jnp.float32)[t5_causal_bucket(dist)]
    bias = jnp.transpose(bias, (2, 0, 1)).reshape(N_KV_HEADS, Q_PER_KV, ATTN_BLOCK, 2 * ATTN_BLOCK)
    key_pos = jnp.arange(n_blocks)[:, None, None] * ATTN_BLOCK - ATTN_BLOCK + kj[None]
    mask = (dist >= 0) & (dist < WINDOW) & (key_pos >= 0)
    return bias, mask

def swa_sink_attention(h, w_qkv, q_gain, k_gain, sinks, w_o, bias, mask):
    b, s, _ = h.shape
    nb = s // ATTN_BLOCK
    qkv = h @ w_qkv
    q, k, v = jnp.split(qkv, [N_Q_HEADS * HEAD_DIM, (N_Q_HEADS + N_KV_HEADS) * HEAD_DIM], axis=-1)
    q = rms_norm(q.reshape(b, s, N_Q_HEADS, HEAD_DIM), q_gain)
    k = rms_norm(k.reshape(b, s, N_KV_HEADS, HEAD_DIM), k_gain)
    v = v.reshape(b, s, N_KV_HEADS, HEAD_DIM)
    q = q.reshape(b, nb, ATTN_BLOCK, N_KV_HEADS, Q_PER_KV, HEAD_DIM)

    def band(t):
        t = t.reshape(b, nb, ATTN_BLOCK, N_KV_HEADS, HEAD_DIM)
        prev = jnp.pad(t, ((0, 0), (1, 0), (0, 0), (0, 0), (0, 0)))[:, :-1]
        return jnp.concatenate([prev, t], axis=2)

    kb, vb = band(k), band(v)
    scores = jnp.einsum('bnqhgd,bnkhd->bnhgqk', q, kb).astype(jnp.float32) * (HEAD_DIM ** -0.5) + bias
    scores = jnp.where(mask[None, :, None, None], scores, -jnp.inf)
    sink = sinks.astype(jnp.float32).reshape(1, 1, N_KV_HEADS, Q_PER_KV, 1, 1)
    m = jnp.maximum(jnp.max(scores, axis=-1, keepdims=True), sink)
    p = jnp.exp(scores - m)
    probs = p / (jnp.sum(p, axis=-1, keepdims=True) + jnp.exp(sink - m))
    out = jnp.einsum('bnhgqk,bnkhd->bnqhgd', probs.astype(vb.dtype), vb)
    return out.reshape(b, s, N_Q_HEADS * HEAD_DIM) @ w_o

def causal_depthwise_conv(u, w, bias):
    ch = u.shape[-1]
    y = lax.conv_general_dilated(u, w[:, None, :].astype(u.dtype), window_strides=(1,),
                                 padding=[(CONV_WIDTH - 1, 0)],
                                 dimension_numbers=('NWC', 'WIO', 'NWC'),
                                 feature_group_count=ch)
    return y + bias

def ssd_chunked_scan(x, dt, a, bmat, cmat):
    b, s = x.shape[:2]
    L = SSM_CHUNK
    nc = s // L
    G, HG = N_SSM_GROUPS, SSM_HEADS_PER_GROUP
    xd = (x * dt[..., None]).reshape(b, nc, L, G, HG, SSM_HEAD_DIM)
    a_cs = jnp.cumsum((dt * a).reshape(b, nc, L, G, HG), axis=2)
    bc = bmat.reshape(b, nc, L, G, D_STATE)
    cc = cmat.reshape(b, nc, L, G, D_STATE)
    causal = jnp.tril(jnp.ones((L, L), dtype=bool))
    a_t = jnp.moveaxis(a_cs, 2, -1)
    decay = jnp.exp(jnp.where(causal, a_t[..., :, None] - a_t[..., None, :], -jnp.inf))
    cb = jnp.einsum('bclgn,bcsgn->bcgls', cc, bc)
    y_diag = jnp.einsum('bcghls,bcsghp->bclghp', cb[:, :, :, None] * decay, xd)
    decay_to_end = jnp.exp(a_cs[:, :, -1:] - a_cs)
    states = jnp.einsum('bclgn,bclghp->bcghpn', bc, xd * decay_to_end[..., None])
    chunk_decay = jnp.exp(a_cs[:, :, -1])

    def step(hstate, inp):
        st, dec = inp
        return dec[..., None, None] * hstate + st, hstate

    h0 = jnp.zeros((b, G, HG, SSM_HEAD_DIM, D_STATE), states.dtype)
    _, prev = lax.scan(step, h0, (jnp.moveaxis(states, 1, 0), jnp.moveaxis(chunk_decay, 1, 0)))
    prev = jnp.moveaxis(prev, 0, 1)
    y_off = jnp.einsum('bclgn,bcghpn->bclghp', cc, prev) * jnp.exp(a_cs)[..., None]
    return (y_diag + y_off).reshape(b, s, N_SSM_HEADS, SSM_HEAD_DIM)

def mamba2_mixer(h, w_in, conv_w, conv_b, dt_bias, a_log, d_skip, norm_w, w_out):
    b, s, _ = h.shape
    f32 = jnp.float32
    zxbcdt = h @ w_in
    z, xbc, dt = jnp.split(zxbcdt, [D_INNER, D_INNER + D_XBC], axis=-1)
    xbc = jax.nn.silu(causal_depthwise_conv(xbc, conv_w, conv_b))
    xs, bmat, cmat = jnp.split(xbc, [D_INNER, D_INNER + N_SSM_GROUPS * D_STATE], axis=-1)
    xs = xs.reshape(b, s, N_SSM_HEADS, SSM_HEAD_DIM).astype(f32)
    bmat = bmat.reshape(b, s, N_SSM_GROUPS, D_STATE).astype(f32)
    cmat = cmat.reshape(b, s, N_SSM_GROUPS, D_STATE).astype(f32)
    dt = jax.nn.softplus((dt + dt_bias).astype(f32))
    a = -jnp.exp(a_log.astype(f32))
    y = ssd_chunked_scan(xs, dt, a, bmat, cmat) + d_skip.astype(f32)[:, None] * xs
    y = y.reshape(b, s, D_INNER).astype(h.dtype)
    y = rms_norm(y * jax.nn.silu(z), norm_w)
    return y @ w_out

def swiglu(h, w_gu, w_down):
    g, u = jnp.split(h @ w_gu, 2, axis=-1)
    return (jax.nn.silu(g) * u) @ w_down

def moe_swiglu(h, w_router, w_gu, w_down):
    logits = (h @ w_router).astype(jnp.float32)
    top_vals, top_idx = lax.top_k(logits, TOP_K)
    top_w = jax.nn.softmax(top_vals, axis=-1)
    combine = jnp.sum(jax.nn.one_hot(top_idx, N_EXPERTS, dtype=jnp.float32) * top_w[..., None], axis=-2)
    combine = combine.astype(h.dtype)
    out = jnp.zeros_like(h)
    for e in range(N_EXPERTS):
        out = out + combine[..., e:e + 1] * swiglu(h, w_gu[e], w_down[e])
    return out

def setup_inputs(seed: int = 0) -> dict:
    key = jax.random.key(seed)
    ks = jax.random.split(key, 24)
    f32 = jnp.float32
    nrm = lambda k, shape, sc: jax.random.normal(k, shape, f32) * sc
    na, nm = N_ATTN_LAYERS, N_SSM_LAYERS
    dt0 = jnp.exp(jax.random.uniform(ks[13], (nm, N_SSM_HEADS), f32)
                  * (math.log(0.1) - math.log(0.001)) + math.log(0.001))
    dt0 = jnp.maximum(dt0, 1e-4)
    return {
        'x': nrm(ks[0], (BATCH, SEQ, D_MODEL), 1.0),
        'c': nrm(ks[1], (BATCH, D_MODEL), 1.0),
        'ada_w': nrm(ks[2], (DEPTH, D_MODEL, 6 * D_MODEL), D_MODEL ** -0.5),
        'ada_b': nrm(ks[3], (DEPTH, 6 * D_MODEL), 0.02),
        'norm_gain': 1.0 + nrm(ks[4], (DEPTH, 2, D_MODEL), 0.1),
        'rel_bias': nrm(ks[5], (N_BUCKETS, N_Q_HEADS), 0.5),
        'attn_w_qkv': nrm(ks[6], (na, D_MODEL, QKV_WIDTH), D_MODEL ** -0.5),
        'attn_q_gain': 1.0 + nrm(ks[7], (na, HEAD_DIM), 0.1),
        'attn_k_gain': 1.0 + nrm(ks[8], (na, HEAD_DIM), 0.1),
        'attn_sinks': nrm(ks[9], (na, N_Q_HEADS), 0.5),
        'attn_w_o': nrm(ks[10], (na, N_Q_HEADS * HEAD_DIM, D_MODEL), (N_Q_HEADS * HEAD_DIM) ** -0.5),
        'ssm_w_in': nrm(ks[11], (nm, D_MODEL, D_IN_PROJ), D_MODEL ** -0.5),
        'ssm_conv_w': nrm(ks[12], (nm, CONV_WIDTH, D_XBC), CONV_WIDTH ** -0.5),
        'ssm_conv_b': nrm(ks[14], (nm, D_XBC), 0.02),
        'ssm_dt_bias': dt0 + jnp.log(-jnp.expm1(-dt0)),
        'ssm_a_log': jnp.log(jax.random.uniform(ks[15], (nm, N_SSM_HEADS), f32, 1.0, 16.0)),
        'ssm_d': 1.0 + nrm(ks[16], (nm, N_SSM_HEADS), 0.1),
        'ssm_norm_w': 1.0 + nrm(ks[17], (nm, D_INNER), 0.1),
        'ssm_w_out': nrm(ks[18], (nm, D_INNER, D_MODEL), D_INNER ** -0.5),
        'ffn_w_gu': nrm(ks[19], (na, D_MODEL, 2 * D_FF), D_MODEL ** -0.5),
        'ffn_w_down': nrm(ks[20], (na, D_FF, D_MODEL), D_FF ** -0.5),
        'moe_w_router': nrm(ks[21], (nm, D_MODEL, N_EXPERTS), D_MODEL ** -0.5),
        'moe_w_gu': nrm(ks[22], (nm, N_EXPERTS, D_MODEL, 2 * D_FF), D_MODEL ** -0.5),
        'moe_w_down': nrm(ks[23], (nm, N_EXPERTS, D_FF, D_MODEL), D_FF ** -0.5),
    }

def reference(x, c, ada_w, ada_b, norm_gain, rel_bias, attn_w_qkv, attn_q_gain, attn_k_gain,
              attn_sinks, attn_w_o, ssm_w_in, ssm_conv_w, ssm_conv_b, ssm_dt_bias, ssm_a_log,
              ssm_d, ssm_norm_w, ssm_w_out, ffn_w_gu, ffn_w_down, moe_w_router, moe_w_gu,
              moe_w_down):
    s = x.shape[1]
    bias, mask = band_bias_and_mask(rel_bias, s // ATTN_BLOCK)
    cond = jax.nn.silu(c)
    for i in range(DEPTH):
        j = i // 2
        mod = cond @ ada_w[i] + ada_b[i]
        sh1, sc1, g1, sh2, sc2, g2 = jnp.split(mod, 6, axis=-1)
        hm = modulate(x, norm_gain[i, 0], sh1, sc1)
        if i % 2 == 0:
            mix = swa_sink_attention(hm, attn_w_qkv[j], attn_q_gain[j], attn_k_gain[j],
                                     attn_sinks[j], attn_w_o[j], bias, mask)
        else:
            mix = mamba2_mixer(hm, ssm_w_in[j], ssm_conv_w[j], ssm_conv_b[j], ssm_dt_bias[j],
                               ssm_a_log[j], ssm_d[j], ssm_norm_w[j], ssm_w_out[j])
        x = x + g1[:, None, :] * mix
        hf = modulate(x, norm_gain[i, 1], sh2, sc2)
        if i % 2 == 0:
            ffn = swiglu(hf, ffn_w_gu[j], ffn_w_down[j])
        else:
            ffn = moe_swiglu(hf, moe_w_router[j], moe_w_gu[j], moe_w_down[j])
        x = x + g2[:, None, :] * ffn
    return x


_drawn_inputs = setup_inputs


def setup_inputs(seed=0):
    import zlib

    import numpy as np

    out = dict(_drawn_inputs(seed))
    spreads = {}
    factors = {'ssm_conv_b': 3.14, 'attn_sinks': 2.727}
    for name, (base, spread) in spreads.items():
        noise = np.random.default_rng([zlib.crc32(name.encode()), seed]).standard_normal(out[name].shape)
        drawn = base * np.exp(spread * noise) if base else spread * noise
        out[name] = jnp.asarray(drawn.astype(out[name].dtype))
    for name, factor in factors.items():
        out[name] = (out[name] * factor).astype(out[name].dtype)
    return out
```

```python
import math

import numpy as np
import concourse.bass as bass
from concourse import mybir

P = 128
D = 1024
SEQ = 256
T = SEQ // P
KD = D // P
HEADS, KV, HD = 16, 4, 64
GQ = HEADS // KV
QKV = (HEADS + 2 * KV) * HD
WINDOW, BUCKETS, MAXDIST = 128, 32, 128
DI = 2 * D
SH, SHD, SG, NS = 32, 64, 4, 128
HG = SH // SG
XBC = DI + 2 * SG * NS
NPROJ = DI + XBC + SH
TAPS = 4
CH = XBC // P
FF = 7 * D // 2
EXPERTS = 8
EPS = 1e-6
MASKED = -1e30

HALF = 512
TW = 1024
RAW = 12
SPLIT = 4
FJ = FF // HALF
FK = FF // P
BODY = FJ * KD + FK
LEAD = 3
assert BODY % RAW == 0 and BODY % SPLIT == 0

IS_SCALE = (0, 1, 0, 0, 1, 0)
MOD_SLOT = ((0, 1, 2, 3, 4, 5), (0, 1, 2, 3, 4, 6))


def bucket_of(dist):
    exact = BUCKETS // 2
    if dist < exact:
        return dist
    return min(BUCKETS - 1, exact + int(math.log(dist / exact) / math.log(MAXDIST / exact) * (BUCKETS - exact)))


def shape_constants():
    i = np.arange(P)
    square = np.zeros((P, 6, P), np.float32)
    square[:, 5] = np.eye(P)[::-1]
    square[:, 0] = np.eye(P)
    square[:, 1] = 1
    square[:, 2] = i[:, None] <= i[None]
    square[:, 3] = i[:, None] < i[None]
    square[:, 4] = i[None]
    table = np.zeros((BUCKETS + 1, 3 * P), np.float32)
    for j in range(3 * P):
        dist = 2 * P - 1 - j
        table[bucket_of(dist) if 0 <= dist < WINDOW else BUCKETS, j] = 1
    return square.reshape(P, 6 * P), table


def build(nc, A, out, square_in, table_in, overflow_at=P):
    f32, f32r, i32, u32 = mybir.dt.float32, mybir.dt.float32r, mybir.dt.int32, mybir.dt.uint32
    ACT = mybir.ActivationFunctionType
    ALU = mybir.AluOpType
    AX = mybir.AxisListType

    top = [(nc.sbuf_base + 31) // 32 * 32]

    def place(name, shape, dtype=f32, at=None):
        size = int(np.prod(shape[1:])) * 4
        if at is None:
            at = top[0]
            top[0] += (size + 31) // 32 * 32
        return nc.alloc_sbuf_tensor_at(name, shape, dtype, offset=at)

    def area(size):
        top[0] += size
        return top[0] - size

    raw = place("raw", [P, RAW, TW])
    w_hi = place("w_hi", [P, SPLIT, TW], f32r)
    w_lo = place("w_lo", [P, SPLIT, TW], f32r)
    x = place("x", [P, T, D])
    A_AT = area(2 * KD * SEQ * 4)
    U_AT = area(2 * FK * SEQ * 4)
    mod = place("mod", [P, 7, D])
    S_AT = area(2 * D * 4)
    square = place("square", [P, 5, P])
    F_AT = area(4096)
    rows16 = place("rows16", [16, D])
    vecs = place("vecs", [P, P])
    cond = place("cond", [P, KD])
    ss, ms, rs = (place(n, [P, 2]) for n in ("ss", "ms", "rs"))
    flag = place("flag", [1, 1], i32)
    w_r = place("w_r", [P, KD, EXPERTS])
    comb = place("comb", [P, T, EXPERTS + 1])
    slot_of = place("slot_of", [P, T, EXPERTS + 1])
    assert top[0] <= nc.sbuf_usable_end, top[0]
    ident, ones, tri, tri_strict, column = (square[:, n, :] for n in range(5))

    rel_rows = place("rel_rows", [BUCKETS, HEADS], f32, A_AT + 512)
    vec_rows = place("vec_rows", [P, P], f32, A_AT)
    a_hi = place("a_hi", [P, KD, SEQ], f32r, A_AT)
    a_lo = place("a_lo", [P, KD, SEQ], f32r, A_AT + KD * SEQ * 4)
    ada = place("ada", [P, 2, D], f32, S_AT)
    hm = place("hm", [P, T, D], f32, S_AT)
    h_hi = place("h_hi", [P, FK, SEQ], f32r, U_AT)
    h_lo = place("h_lo", [P, FK, SEQ], f32r, U_AT + FK * SEQ * 4)
    h = place("h", [P, T, HALF], f32, F_AT)
    qkv = place("qkv", [P, T, QKV], f32, U_AT)
    bias = place("bias", [P, HEADS, 2 * P], f32, U_AT + 12288)
    bias_rev = place("bias_rev", [P, HEADS, 2 * P], f32, A_AT)
    reversal = place("reversal", [P, P], f32, U_AT + 28672)
    q_t = place("q_t", [P, KD, SEQ], f32, U_AT + 28672)
    k_t = place("k_t", [P, KV, SEQ], f32, U_AT + 36864)
    sc = place("sc", [P, 2, GQ * 2 * P], f32, U_AT + 40960)
    qk_square = place("qk_square", [P, (HEADS + KV) * HD], f32, U_AT + 40960)
    p_t = place("p_t", [P, 2, GQ * P], f32, U_AT + 49152)
    k2 = place("k2", [P, T, KV, 2, HD], f32, U_AT + 53248)
    sinks = place("sinks", [P, HEADS], f32, F_AT)
    qk_gain = place("qk_gain", [P, 2, HD], f32, F_AT + 64)
    relb = place("relb", [BUCKETS + 1, HEADS], f32, F_AT + 576)
    table = place("table", [BUCKETS + 1, 3 * P], f32, F_AT + 640)
    reltab = place("reltab", [HEADS, 3 * P], f32, F_AT + 2176)
    NQK = HEADS + KV
    qk_ss = place("qk_ss", [P, NQK], f32, F_AT + 3712)
    stat = place("stat", [P, 4, GQ], f32, F_AT + 3808)
    z_s = place("z_s", [P, T, DI], f32, U_AT)
    xbc = place("xbc", [P, T, XBC], f32, U_AT + 16384)
    b_t = place("b_t", [P, SG, SEQ], f32, U_AT + 40960)
    c_t = place("c_t", [P, SG, SEQ], f32, U_AT + 45056)
    u_pad = place("u_pad", [P, 2, 2, SEQ + TAPS], f32, S_AT)
    cv = place("cv", [P, 2, 2, SEQ], f32, U_AT + 49152)
    dec = place("dec", [P, 2, HG * P], f32, U_AT + 49152)
    xd = place("xd", [P, 2, HG * SHD], f32, A_AT)
    xde = place("xde", [P, 2, HG * SHD], f32, A_AT + 4096)
    y_tmp = place("y_tmp", [P, HG * SHD], f32, S_AT)
    y_sq = place("y_sq", [P, HG * SHD], f32, S_AT + 2048)
    state = place("state", [P, SG, HG * SHD], f32, A_AT + 8192)
    w_dt = place("w_dt", [P, KD, SH], f32, F_AT)
    srow = place("srow", [P, 3, SH], f32, F_AT + 1024)
    dt = place("dt", [P, T, SH], f32, F_AT + 1408)
    dt_a = place("dt_a", [P, T, SH], f32, F_AT + 1664)
    dt_e = place("dt_e", [P, T, SH], f32, F_AT + 1920)
    acs = place("acs", [P, 2 * T, SH], f32, F_AT + 2176)
    acs_e = place("acs_e", [P, T, SH], f32, F_AT + 2688)
    end_e = place("end_e", [P, T, SH], f32, F_AT + 2944)
    cbm = place("cbm", [P, P], f32, F_AT + 3200)
    yss = place("yss", [P, T, SG], f32, F_AT + 3712)
    y_hi = place("y_hi", [P, DI // P, SEQ], f32r, A_AT)
    y_lo = place("y_lo", [P, DI // P, SEQ], f32r, U_AT)
    EH = FK * P * 4
    e_hi = place("e_hi", [P, FK, P], f32r, U_AT)
    e_lo = place("e_lo", [P, FK, P], f32r, U_AT + EH)
    t_hi = place("t_hi", [P, T, D], f32r, U_AT + 2 * EH)
    t_lo = place("t_lo", [P, T, D], f32r, U_AT + 2 * EH + 8192)
    y_sum = place("y_sum", [P, T, D], f32, U_AT + 2 * EH + 16384)
    pick = place("pick", [P, T, P], f32r, U_AT + 2 * EH + 24576)
    put = place("put", [P, T, P], f32r, U_AT + 2 * EH + 25600)
    g_hi = place("g_hi", [P, KD, P], f32r, A_AT)
    g_lo = place("g_lo", [P, KD, P], f32r, A_AT + 4096)
    yd_hi = place("yd_hi", [P, D], f32r, A_AT + 8192)
    yd_lo = place("yd_lo", [P, D], f32r, A_AT + 12288)
    lg = place("lg", [P, T, EXPERTS], f32, F_AT + 2304)
    mx = place("mx", [P, T, 8], f32, F_AT + 2368)
    mi = place("mi", [P, T, 8], u32, F_AT + 2432)
    mif = place("mif", [P, T, 8], f32, F_AT + 2496)
    oh = place("oh", [P, T, 2, EXPERTS], f32, F_AT + 2560)
    tw = place("tw", [P, T, 3], f32, F_AT + 2688)
    msk = place("msk", [P, T, EXPERTS], f32, F_AT + 2720)
    cmax = place("cmax", [P, 1], f32, F_AT + 2784)

    acc = [nc.alloc_psum_tensor(f"acc{n}", [P, 2 * HALF], f32) for n in range(3)]
    xb = [nc.alloc_psum_tensor(f"xb{n}", [P, HALF], f32) for n in range(2)]
    rel_dram = nc.dram_tensor("rel_scratch", (HEADS, 3 * P), f32, kind="Internal").ap()

    def r32(ap):
        return ap.bitcast(f32)

    sem = nc.alloc_semaphore
    raw_ready = [sem(f"raw_ready{n}") for n in range(RAW)]
    raw_used = sem("raw_used")
    hi_ready = sem("hi_ready")
    w_used = sem("w_used")
    acc_full = sem("acc_full")
    acc_done = [sem(f"acc_done{n}") for n in range(3)]
    xb_full = sem("xb_full")
    xb_done = [sem(f"xb_done{n}") for n in range(2)]
    xb_hi = sem("xb_hi")
    dve_step = sem("dve_step")
    act_step = sem("act_step")
    ld_square, ld_rows, ld_vecs, ld_x, ld_tab, ld_att, ld_bias, ld_mix, ld_norm, ld_router, st_rel, st_out = (
        sem(n) for n in ("ld_square", "ld_rows", "ld_vecs", "ld_x", "ld_tab", "ld_att", "ld_bias", "ld_mix",
                         "ld_norm", "ld_router", "st_rel", "st_out"))
    relb_set, cond_ready, ada_ready = (
        sem(n) for n in ("relb_set", "cond_ready", "ada_ready"))
    ss_ready, ms_ready, root_ready, hm_ready, x_ready = (
        sem(n) for n in ("ss_ready", "ms_ready", "root_ready", "hm_ready", "x_ready"))
    qkv_ready, qk_sq, qk_ms, qk_root, qk_ready, max_ready, exp_ready, p_ready = (
        sem(n) for n in ("qkv_ready", "qk_sq", "qk_ms", "qk_root", "qk_ready", "max_ready",
                         "exp_ready", "p_ready"))
    gate_ready = sem("gate_ready")
    z_ready, xbc_ready, u_ready, cv_ready, cs_ready, norm_free = (
        sem(n) for n in ("z_ready", "xbc_ready", "u_ready", "cv_ready", "cs_ready", "norm_free"))
    dtv_ready, dte_ready, dta_ready, acs_ready, acse_ready = (
        sem(n) for n in ("dtv_ready", "dte_ready", "dta_ready", "acs_ready", "acse_ready"))
    d_ready, e_ready, mt_ready, y_ready, yss_ready, yms_ready, yroot, yn_ready = (
        sem(n) for n in ("d_ready", "e_ready", "mt_ready", "y_ready", "yss_ready", "yms_ready",
                         "yroot", "yn_ready"))
    t_hi_ready, t_lo_ready, tw_in, tw_exp, mask_ready, route_ready = (
        sem(n) for n in ("t_hi_ready", "t_lo_ready", "tw_in", "tw_exp", "mask_ready", "route_ready"))
    pick_ready, put_ready, yd_hi_ready, yd_lo_ready, final_step = (
        sem(n) for n in ("pick_ready", "put_ready", "yd_hi_ready", "yd_lo_ready", "final_step"))

    def ada_after(s):
        return (s + 1) * 6 * KD // BODY != s * 6 * KD // BODY

    n_ada = 6 * KD
    raw0, spl0, pc0, pr0 = {}, {}, {}, {}
    at = [0, 0, 0, 0]
    for stage, raws, splits, pieces, pairs in (
        ("start", 0, 0, 2, 0), ("ada", n_ada, 0, 16 + 8, 0), ("norm0", 0, 0, 4, 0),
        ("qkv", 12, 12, 0, 4), ("heads", 0, 0, 6, 0), ("attend", 0, 0, 12, 16),
        ("wo", KD, KD, 0, 2), ("norm1", 0, 0, 4, 0),
        ("ffn", BODY + n_ada, BODY, 2 * FJ + 16, 2 * FJ + 2), ("norm2", 0, 0, 4, 0),
        ("proj", 5 * KD, 5 * KD, 1, 10), ("conv", 0, 0, 22, 0), ("sums", 0, 0, 1, 0),
        ("ssd", 0, 0, 8, 16), ("ynorm", 0, 0, 8, 0), ("wout", 2 * KD, 2 * KD, 0, 2),
        ("norm3", 0, 0, 4, 0), ("route", 0, 0, 2, 0), ("moe", 0, 0, 0, 0),
    ):
        raw0[stage], spl0[stage], pc0[stage], pr0[stage] = at
        at = [a + b for a, b in zip(at, (raws, splits, pieces, pairs))]

    def body_pieces(mixture):
        after = {}
        for j in range(FJ):
            after.setdefault(KD * (j + 1) + 3, []).extend(("h", j, t) for t in range(1 if mixture else T))
        if mixture:
            for n in range(2 * T):
                after.setdefault(2 * KD + 4 + 2 * n, []).append(("scatter", n // 2, n % 2))
            after.setdefault(3 * KD + 4, []).append(("put",))
            for n in range(4):
                after.setdefault(FJ * KD + 8 + 4 * n, []).append(("gather", n // 2, n % 2))
        else:
            done = 0
            for s in range(BODY):
                if ada_after(s):
                    done += 1
                    if done % KD == 0:
                        c = done // KD - 1
                        after.setdefault(min(s + 1, BODY - 1), []).extend(("ada", c, n) for n in range(4 if IS_SCALE[c] else 2))
        order, n = {}, 0
        for s in sorted(after):
            order[s] = [(n + m, *what) for m, what in enumerate(after[s])]
            n += len(after[s])
        return order

    PIECES = {False: body_pieces(False), True: body_pieces(True)}
    assert sum(len(v) for v in PIECES[True].values()) == 16
    assert sum(len(v) for v in PIECES[False].values()) == 2 * FJ + 16

    def pieces_read_after(mixture, s):
        last = s == BODY - 1
        found = list(PIECES[mixture].get(s - LEAD, []))
        if last:
            for later in range(s - LEAD + 1, BODY):
                found += PIECES[mixture].get(later, [])
        return found

    UNITS = [(g, b) for g in range(KV) for b in range(T)]
    att_pair, n = {}, pr0["attend"]
    for what in [("s", 0), ("s", 1)] + [w for u in range(8) for w in ([("o", u)] + ([("s", u + 2)] if u < 6 else []))]:
        att_pair[what] = n
        n += 1
    att_piece, n = {}, pc0["attend"]
    for u, (g, b) in enumerate(UNITS):
        att_piece[u] = n
        n += b + 1
    SUNITS = [(c, g) for c in range(T) for g in range(SG)]
    ssd_pair, n = {}, pr0["ssd"]
    for what in [("a", 0), ("a", 1)] + [w for u in range(8) for w in ([("y", u)] + ([("a", u + 2)] if u < 6 else []))]:
        ssd_pair[what] = n
        n += 1
    def full_no(n):
        return n - pr0["attend"] + 1 if n < pr0["wo"] else 16 + n - pr0["ssd"] + 1

    NCV = CH // 2
    CBACK = 10
    cv_piece, n = {}, pc0["conv"]
    for what in [("f", 0), ("f", 1)] + [w for q in range(NCV) for w in (([("b", q)] if q < CBACK else []) + ([("f", q + 2)] if q < NCV - 2 else []))]:
        cv_piece[what] = n
        n += 1
    assert n == pc0["conv"] + 22

    moe_uses = [(FJ + 1) // 2, FJ // 2, 1]
    pair_uses0 = [len([m for m in range(pr0["moe"]) if m % 3 == q]) for q in range(3)]
    ROUND_PIECES = 4 + 16 * EXPERTS + 4

    class Body:

        def __init__(self, mixture, e=0, rnd=0):
            self.mixture, self.e = mixture, e
            self.tiles = 1 if mixture else T
            if mixture:
                self.raw = raw0["moe"] + rnd * EXPERTS * BODY
                self.spl = spl0["moe"] + rnd * EXPERTS * BODY
                self.pc = pc0["moe"] + rnd * ROUND_PIECES + 4
                self.pr = pr0["moe"] + rnd * EXPERTS * (FJ + 1)
                self.rnd = rnd
            else:
                self.raw, self.spl, self.pc, self.pr, self.rnd = raw0["ffn"], spl0["ffn"], pc0["ffn"], pr0["ffn"], 0

        def raw_no(self, s):
            extra = 0 if self.mixture else s * n_ada // BODY
            return self.raw + s + extra

        def pair(self, j, t):
            if not self.mixture:
                n = self.pr + T * j + t
                return n % 3, n // 3
            q = 2 if j == FJ else j % 2
            used = pair_uses0[q] + self.rnd * EXPERTS * moe_uses[q] + (0 if j == FJ else j // 2)
            return q, used + self.e * moe_uses[q]

        def full(self, j):
            return self.spl + KD * (j + 1) + self.e * BODY

    def rep(e, per):
        return e * per

    def swiglu_source(w_gu, w_down, s):
        if s < FJ * KD:
            j, k = divmod(s, KD)
            return w_gu[k * P:(k + 1) * P, :].rearrange("p (h n) -> p h n", h=2)[:, :, j * HALF:(j + 1) * HALF]
        k = s - FJ * KD
        return w_down[k * P:(k + 1) * P, :]

    block = nc.Block()
    with block:

        @block.sync
        def _(sp):
            def load(no, src, e=0):
                if no >= RAW:
                    sp.wait_ge(raw_used, no - RAW + 1 + rep(e, BODY))
                dst = raw[:, no % RAW, :]
                if len(src.shape) == 3:
                    dst = dst.rearrange("p (h n) -> p h n", h=src.shape[1])
                sp.dma_start(dst, src).then_inc(raw_ready[no % RAW], 16)

            def row(src, n):
                return bass.AP(src.tensor, src.offset, [[0, P], [1, n]])

            sp.dma_start(square[:, :, :], square_in[:, 0:5 * P].rearrange("p (n m) -> p n m", n=5)).then_inc(ld_square, 16)
            sp.dma_start(reversal[:, :], square_in[:, 5 * P:6 * P]).then_inc(ld_square, 16)
            sp.dma_start(vec_rows[0:KD, :], A["c"].rearrange("b (k p) -> (b k) p", p=P)).then_inc(ld_vecs, 16)
            sp.dma_start(vec_rows[KD:KD + TAPS * CH, :], A["ssm_conv_w"][0].rearrange("t (k p) -> (t k) p", p=P)).then_inc(ld_vecs, 16)
            sp.dma_start(vec_rows[KD + TAPS * CH:P, :], A["ssm_conv_b"].rearrange("b (k p) -> (b k) p", p=P)).then_inc(ld_vecs, 16)
            sp.dma_start(table[:, :], table_in).then_inc(ld_tab, 16)
            sp.dma_start(rel_rows[:, :], A["rel_bias"]).then_inc(ld_tab, 16)
            sp.dma_start(rows16[0:12, :], A["ada_b"].rearrange("l (g n) -> (l g) n", n=D)).then_inc(ld_rows, 16)
            sp.dma_start(rows16[12:16, :], A["norm_gain"].rearrange("l g n -> (l g) n")).then_inc(ld_rows, 16)
            sp.dma_start(x[:, :, :], A["x"][0].rearrange("(t p) n -> p t n", p=P)).then_inc(ld_x, 16)
            sp.dma_start(w_r[:, :, :], A["moe_w_router"][0].rearrange("(k p) n -> p k n", p=P)).then_inc(ld_router, 16)
            sp.dma_start(sinks[:, :], row(A["attn_sinks"], HEADS)).then_inc(ld_att, 16)
            sp.dma_start(qk_gain[:, 0, :], row(A["attn_q_gain"], HD)).then_inc(ld_att, 16)
            sp.dma_start(qk_gain[:, 1, :], row(A["attn_k_gain"], HD)).then_inc(ld_att, 16)

            no = 0
            for c in range(6):
                if c == 1:
                    sp.wait_ge(xb_done[1], 1)
                    sp.dma_start(rel_dram, reltab[:, :]).then_inc(st_rel, 16)
                    sp.wait_ge(st_rel, 16)
                    sp.dma_start(bias_rev[:, :, :], bass.AP(rel_dram.tensor, 0, [[1, P], [3 * P, HEADS], [1, 2 * P]])).then_inc(ld_bias, 16)
                for k in range(KD):
                    load(no, A["ada_w"][0, k * P:(k + 1) * P, c * D:(c + 1) * D])
                    no += 1
            w = A["attn_w_qkv"][0]
            for k in range(KD):
                load(no, w[k * P:(k + 1) * P, 0:D])
                no += 1
            for k in range(0, KD, 2):
                load(no, w[k * P:(k + 2) * P, D:QKV].rearrange("(h p) n -> p h n", h=2))
                no += 1
            for k in range(KD):
                load(no, A["attn_w_o"][0, k * P:(k + 1) * P, :])
                no += 1
            n = 0
            for s in range(BODY):
                load(no, swiglu_source(A["ffn_w_gu"][0], A["ffn_w_down"][0], s))
                no += 1
                if ada_after(s):
                    c, k = divmod(n, KD)
                    load(no, A["ada_w"][1, k * P:(k + 1) * P, c * D:(c + 1) * D])
                    n += 1
                    no += 1
            w = A["ssm_w_in"][0]
            for g in range(5):
                for k in range(KD):
                    load(no, w[k * P:(k + 1) * P, g * TW:(g + 1) * TW])
                    no += 1
                if g == 0:
                    sp.wait_ge(x_ready, 2)
                    sp.dma_start(w_dt[:, :, :], w[:, 5 * TW:NPROJ].rearrange("(k p) n -> p k n", p=P)).then_inc(ld_mix, 16)
                    for r, name in enumerate(("ssm_dt_bias", "ssm_a_log", "ssm_d")):
                        sp.dma_start(srow[:, r, :], row(A[name], SH)).then_inc(ld_mix, 16)
            sp.wait_ge(norm_free, 1)
            sp.dma_start(mod[:, 0:2, :], bass.AP(A["ssm_norm_w"].tensor, 0, [[0, P], [1, DI]])).then_inc(ld_norm, 16)
            for k in range(2 * KD):
                load(no, A["ssm_w_out"][0, k * P:(k + 1) * P, :])
                no += 1
            assert no == raw0["moe"]

            def experts(rnd):
                with sp.Fori(0, EXPERTS) as e:
                    for s in range(BODY):
                        load(raw0["moe"] + rnd * EXPERTS * BODY + s,
                             swiglu_source(A["moe_w_gu"][0, e], A["moe_w_down"][0, e], s), e)

            experts(0)
            sp.wait_ge(route_ready, 1)
            most = sp.value_load(flag[0:1, 0:1], min_val=0, max_val=SEQ)
            with sp.If(most > overflow_at):
                experts(1)
            sp.wait_ge(x_ready, 4)
            sp.dma_start(out[0].rearrange("(t p) n -> p t n", p=P), x[:, :, :]).then_inc(st_out, 16)
            sp.wait_ge(st_out, 16)

        @block.scalar
        def _(act):
            steps = [0]

            def own(ins):
                steps[0] += 1
                ins.then_inc(act_step, 1)
                act.wait_ge(act_step, steps[0])

            def split_hi(no, w, e=0, per=0, per_raw=0):
                act.wait_ge(raw_ready[no % RAW], 16 * (no // RAW + 1) + rep(e, 16 * per_raw // RAW))
                if w >= SPLIT:
                    act.wait_ge(w_used, w - SPLIT + 1 + rep(e, per))
                act.activation(w_hi[:, w % SPLIT, :], raw[:, no % RAW, :], ACT.Copy).then_inc(hi_ready, 1)

            def piece(c):
                act.wait_ge(xb_full, c + 1)
                return xb[c % 2]

            def gemm(stage, evacuate, groups):
                i = 0
                pr = pr0[stage]

                def out_of(gi):
                    act.wait_ge(w_used, spl0[stage] + sum(groups[:gi + 1]))
                    evacuate(gi, pr + T * gi)

                for gi, n_tiles in enumerate(groups):
                    for k in range(n_tiles):
                        split_hi(raw0[stage] + i, spl0[stage] + i)
                        i += 1
                        if evacuate and gi and k == 1:
                            out_of(gi - 1)
                if evacuate:
                    out_of(len(groups) - 1)

            def norm(n, stage):
                if n == 0:
                    act.wait_ge(ld_x, 16)
                    act.wait_ge(ada_ready, 6)
                else:
                    act.wait_ge(x_ready, n)
                for t in range(T):
                    act.activation(hm[:, t, :], x[:, t, :], ACT.Square, accum_out=ss[:, t:t + 1]).then_inc(ss_ready, 1)
                act.wait_ge(ms_ready, n + 1)
                act.activation(rs[:, :], ms[:, :], ACT.Sqrt).then_inc(root_ready, 1)
                if n == 3:
                    for t in range(T):
                        act.wait_ge(hm_ready, T * n + t + 1)
                        act.activation(t_hi[:, t, :], hm[:, t, :], ACT.Copy).then_inc(t_hi_ready, 1)
                for t in range(T):
                    for hf in range(2):
                        b = piece(pc0[stage] + 2 * t + hf)
                        act.activation(a_hi[:, 4 * hf:4 * hf + 4, t * P:(t + 1) * P],
                                       b[:, :].rearrange("p (k m) -> p k m", k=4), ACT.Copy).then_inc(xb_hi, 1)

            b = piece(0)
            act.activation(vecs[:, :], b[:, 0:P], ACT.Copy).then_inc(xb_done[0], 1)
            act.wait_ge(xb_done[0], 1)
            act.activation(cond[:, :], vecs[:, 0:KD], ACT.Silu).then_inc(cond_ready, 1)
            b = piece(1)
            act.activation(reltab[:, :], b[0:HEADS, 0:3 * P], ACT.Copy).then_inc(xb_done[1], 1)

            for n in range(8):
                c = pc0["ada"] + 6 + n
                b = piece(c)
                act.activation(bias[:, 2 * n:2 * n + 2, :], b[:, :].rearrange("p (k m) -> p k m", k=2), ACT.Copy).then_inc(xb_done[c % 2], 1)

            norm(0, "norm0")

            def qkv_out(g, pr):
                lo, n = (0, D) if g == 0 else (D, QKV - D)
                for t in range(T):
                    act.activation(qkv[:, t, lo:lo + n], acc[(pr + t) % 3][:, 0:n], ACT.Copy).then_inc(acc_done[(pr + t) % 3], 1)

            gemm("qkv", qkv_out, (KD, KD // 2))
            pr = pr0["qkv"]
            for q in range(3):
                act.wait_ge(acc_done[q], len([m for m in range(pr + 4) if m % 3 == q]))
            act.sem_inc(qkv_ready, 1)
            for t in range(T):
                if t:
                    act.wait_ge(qk_ms, t)
                act.activation(qk_square[:, :], qkv[:, t, 0:NQK * HD], ACT.Square).then_inc(qk_sq, 1)
                act.wait_ge(qk_ms, t + 1)
                act.activation(qk_ss[:, :], qk_ss[:, :], ACT.Sqrt).then_inc(qk_root, 1)
            for n in range(6):
                c = pc0["heads"] + n
                b = piece(c)
                t, part = divmod(n, 3)
                dst = k_t[:, :, t * P:(t + 1) * P] if part == 2 else q_t[:, 4 * part:4 * part + 4, t * P:(t + 1) * P]
                act.activation(dst, b[:, :].rearrange("p (k m) -> p k m", k=4), ACT.Copy).then_inc(xb_done[c % 2], 1)

            def exps(u):
                g, blk = UNITS[u]
                w = P * (blk + 1)
                act.wait_ge(max_ready, u + 1)
                for i in range(GQ):
                    act.activation(sc[:, u % 2, i * w:(i + 1) * w], sc[:, u % 2, i * w:(i + 1) * w], ACT.Exp,
                                   bias=stat[:, 1, i:i + 1], accum_out=stat[:, 2, i:i + 1])
                act.activation(stat[:, 3, :], stat[:, 3, :], ACT.Exp).then_inc(exp_ready, 1)

            def heads_out(u):
                g, blk = UNITS[u]
                for kc in range(blk + 1):
                    c = att_piece[u] + kc
                    b = piece(c)
                    act.activation(p_t[:, kc, :], b[:, :], ACT.Copy).then_inc(xb_done[c % 2], 1)
                n = att_pair["o", u]
                act.wait_ge(acc_full, full_no(n))
                act.activation(a_hi[:, 2 * g:2 * g + 2, blk * P:(blk + 1) * P],
                               acc[n % 3][:, 0:2 * P].rearrange("p (k m) -> p k m", k=2), ACT.Copy).then_inc(xb_hi, 1)

            exps(0)
            for u in range(8):
                heads_out(u)
                if u < 7:
                    exps(u + 1)

            gemm("wo", None, (KD,))
            norm(1, "norm1")

            def body(B):
                e = B.e
                for s in range(BODY):
                    split_hi(B.raw_no(s), B.spl + s, e, BODY, BODY)
                    if B.mixture and s == 2:
                        act.wait_ge(w_used, B.full(-1))
                        act.activation(yd_hi[:, :], acc[2][:, :], ACT.Copy).then_inc(yd_hi_ready, 1)
                    j, k = divmod(s, KD)
                    if 1 <= j <= FJ and k == 2:
                        act.wait_ge(w_used, B.full(j - 1))
                        for t in range(B.tiles):
                            act.activation(h[:, t, :], acc[B.pair(j - 1, t)[0]][:, 0:HALF], ACT.Silu).then_inc(gate_ready, 1)
                    for c, kind, *which in pieces_read_after(B.mixture, s):
                        c += B.pc
                        if kind == "h":
                            act.wait_ge(xb_full, c + 1 + rep(e, 16))
                            j, t = which
                            dst = (e_hi if B.mixture else h_hi)[:, 4 * j:4 * j + 4, t * P:(t + 1) * P]
                            act.activation(dst, xb[c % 2][:, :].rearrange("p (k m) -> p k m", k=4), ACT.Copy).then_inc(xb_hi, 1)
                        elif kind == "put":
                            act.wait_ge(xb_full, c + 1 + rep(e, 16))
                            act.activation(put[:, :, :], xb[c % 2][:, 0:T * P].rearrange("p (t m) -> p t m", t=T),
                                           ACT.Copy).then_inc(xb_done[c % 2], 1)
                        elif kind == "gather" and which[0] == 0:
                            act.wait_ge(xb_full, c + 1 + rep(e, 16))
                            q = which[1]
                            act.activation(g_hi[:, 4 * q:4 * q + 4, :], xb[c % 2][:, :].rearrange("p (k m) -> p k m", k=4),
                                           ACT.Copy).then_inc(xb_done[c % 2], 1)

            body(Body(False))
            norm(2, "norm2")

            def proj_out(g, pr):
                for t in range(T):
                    n = pr + t
                    if g < 2:
                        act.activation(z_s[:, t, g * TW:(g + 1) * TW], acc[n % 3][:, :], ACT.Silu).then_inc(acc_done[n % 3], 1)
                    else:
                        act.activation(xbc[:, t, (g - 2) * TW:(g - 1) * TW], acc[n % 3][:, :], ACT.Copy).then_inc(acc_done[n % 3], 1)

            gemm("proj", proj_out, (KD,) * 5)
            for q in range(3):
                act.wait_ge(acc_done[q], len([m for m in range(pr0["ssd"]) if m % 3 == q]))
            act.sem_inc(xbc_ready, 1)

            def conv_in(q):
                b = piece(cv_piece["f", q])
                if q < 2:
                    act.wait_ge(u_ready, 1)
                act.activation(u_pad[:, q % 2, :, TAPS - 1:TAPS - 1 + SEQ], b[:, :].rearrange("p (k m) -> p k m", k=2),
                               ACT.Copy).then_inc(xb_done[cv_piece["f", q] % 2], 1)

            conv_in(0)
            conv_in(1)
            for q in range(NCV):
                act.wait_ge(cv_ready, q + 1)
                dst = cv[:, q % 2] if q < 8 else (b_t if q < CBACK else c_t)[:, 2 * (q % 2):2 * (q % 2) + 2, :]
                act.activation(dst, cv[:, q % 2], ACT.Silu).then_inc(cs_ready, 1)
                if q < NCV - 2:
                    conv_in(q + 2)
                if q < CBACK:
                    c = cv_piece["b", q]
                    b = piece(c)
                    act.activation(xbc[:, :, 2 * P * q:2 * P * (q + 1)], b[:, :].rearrange("p (t m) -> p t m", t=T),
                                   ACT.Copy).then_inc(xb_done[c % 2], 1)

            act.wait_ge(dtv_ready, 1)
            own(act.activation(dt_e[:, :, :], dt[:, :, :], ACT.Abs))
            own(act.activation(dt_e[:, :, :], dt_e[:, :, :], ACT.Exp, scale=-1.0))
            own(act.activation(dt_e[:, :, :], dt_e[:, :, :], ACT.Ln, bias=ones[:, 0:1]))
            act.activation(srow[:, 1, :], srow[:, 1, :], ACT.Exp).then_inc(dte_ready, 1)
            act.wait_ge(acs_ready, 1)
            act.activation(acs_e[:, :, :], acs[:, 0:T, :], ACT.Exp).then_inc(acse_ready, 1)
            act.activation(end_e[:, :, :], end_e[:, :, :], ACT.Exp).then_inc(acse_ready, 1)

            def y_square(u):
                c, g = SUNITS[u]
                act.wait_ge(y_ready, u + 1)
                act.wait_ge(yss_ready, u)
                act.activation(y_sq[:, :], xbc[:, c, 512 * g:512 * (g + 1)], ACT.Square, accum_out=yss[:, c, g:g + 1]).then_inc(yss_ready, 1)

            for u in range(8):
                act.wait_ge(d_ready, u + 1)
                own(act.activation(dec[:, u % 2, :], dec[:, u % 2, :], ACT.Relu))
                act.activation(dec[:, u % 2, :], dec[:, u % 2, :], ACT.Exp, scale=-1.0).then_inc(e_ready, 1)
                if u >= 2:
                    y_square(u - 2)
            y_square(6)
            y_square(7)
            act.wait_ge(yms_ready, 1)
            act.activation(rs[:, :], ms[:, :], ACT.Sqrt).then_inc(yroot, 1)
            for n in range(8):
                c = pc0["ynorm"] + n
                b = piece(c)
                t, q = divmod(n, 4)
                act.activation(y_hi[:, 4 * q:4 * q + 4, t * P:(t + 1) * P], b[:, :].rearrange("p (k m) -> p k m", k=4),
                               ACT.Copy).then_inc(xb_hi, 1)
            gemm("wout", None, (2 * KD,))
            norm(3, "norm3")

            act.wait_ge(tw_in, 1)
            act.activation(tw[:, :, 0], tw[:, :, 0], ACT.Exp).then_inc(tw_exp, 1)

            def first_gather(rnd):
                for q in range(2):
                    c = pc0["moe"] + rnd * ROUND_PIECES + q
                    b = piece(c)
                    act.activation(g_hi[:, 4 * q:4 * q + 4, :], b[:, :].rearrange("p (k m) -> p k m", k=4),
                                   ACT.Copy).then_inc(xb_done[c % 2], 1)

            def experts(rnd):
                first_gather(rnd)
                with act.Fori(0, EXPERTS) as e:
                    body(Body(True, e, rnd))
                act.wait_ge(w_used, spl0["moe"] + (rnd + 1) * EXPERTS * BODY)
                act.activation(yd_hi[:, :], acc[2][:, :], ACT.Copy).then_inc(yd_hi_ready, 1)

            experts(0)
            most = act.value_load(flag[0:1, 0:1], min_val=0, max_val=SEQ)
            with act.If(most > overflow_at):
                experts(1)

        @block.vector
        def _(dve):
            steps = [0]

            def own(ins):
                steps[0] += 1
                ins.then_inc(dve_step, 1)
                dve.wait_ge(dve_step, steps[0])

            def split_lo(no, w, e=0):
                dve.wait_ge(hi_ready, w + 1 + rep(e, BODY))
                dve.tensor_tensor(w_lo[:, w % SPLIT, :], raw[:, no % RAW, :], r32(w_hi[:, w % SPLIT, :]), ALU.subtract).then_inc(raw_used, 1)

            def ada_tile(no, k, buf):
                dve.wait_ge(raw_ready[no % RAW], 16 * (no // RAW + 1))
                if k == 0:
                    dve.tensor_scalar(ada[:, buf, :], raw[:, no % RAW, :], cond[:, 0:1], None, ALU.mult).then_inc(raw_used, 1)
                else:
                    dve.wait_ge(raw_used, no)
                    dve.scalar_tensor_tensor(ada[:, buf, :], raw[:, no % RAW, :], cond[:, k:k + 1], ada[:, buf, :],
                                             ALU.mult, ALU.add).then_inc(raw_used, 1)

            def ada_piece(layer, c, n, pc):
                dve.wait_ge(xb_full, pc + 1)
                dst = mod[:, MOD_SLOT[layer][c], (n % 2) * HALF:(n % 2 + 1) * HALF]
                if IS_SCALE[c] and n >= 2:
                    dve.wait_ge(xb_done[pc % 2], pc // 2)
                    dve.scalar_tensor_tensor(dst, xb[pc % 2][:, :], 1.0, dst, ALU.add, ALU.mult).then_inc(xb_done[pc % 2], 1)
                else:
                    dve.tensor_copy(dst, xb[pc % 2][:, :]).then_inc(xb_done[pc % 2], 1)

            lows = [0]

            def piece_lo(c, dst, m=4):
                lows[0] += 1
                dve.wait_ge(xb_hi, lows[0])
                d_hi, d_lo = dst
                dve.tensor_tensor(d_lo, xb[c % 2][:, :].rearrange("p (k m) -> p k m", k=m), r32(d_hi), ALU.subtract).then_inc(xb_done[c % 2], 1)

            def norm(n, stage):
                layer, half = divmod(n, 2)
                sh, g = (mod[:, MOD_SLOT[layer][3 * half + q], :] for q in range(2))
                dve.wait_ge(ss_ready, T * (n + 1))
                dve.tensor_scalar(ms[:, :], ss[:, :], 1.0 / D, EPS, ALU.mult, ALU.add).then_inc(ms_ready, 1)
                dve.wait_ge(root_ready, n + 1)
                own(dve.reciprocal(rs[:, :], rs[:, :]))
                for t in range(T):
                    own(dve.scalar_tensor_tensor(hm[:, t, :], x[:, t, :], rs[:, t:t + 1], g, ALU.mult, ALU.mult))
                    dve.tensor_tensor(hm[:, t, :], hm[:, t, :], sh, ALU.add).then_inc(hm_ready, 1)
                if n == 3:
                    dve.wait_ge(hm_ready, T * n + T)
                    for t in range(T):
                        dve.wait_ge(t_hi_ready, t + 1)
                        dve.tensor_tensor(t_lo[:, t, :], hm[:, t, :], r32(t_hi[:, t, :]), ALU.subtract).then_inc(t_lo_ready, 1)
                for t in range(T):
                    for hf in range(2):
                        part = (slice(None), slice(4 * hf, 4 * hf + 4), slice(t * P, (t + 1) * P))
                        piece_lo(pc0[stage] + 2 * t + hf, (a_hi[part], a_lo[part]))

            def residual(stage, groups_before, gate):
                first = pr0[stage] + T * groups_before
                after = {"wo": "norm1", "ffn": "norm2", "wout": "norm3"}[stage]
                dve.wait_ge(w_used, spl0[after])
                for t in range(T):
                    n = first + t
                    dve.tensor_tensor(hm[:, t, :], acc[n % 3][:, :], gate, ALU.mult).then_inc(acc_done[n % 3], 1)
                    dve.wait_ge(acc_done[n % 3], n // 3 + 1)
                    own(dve.tensor_tensor(x[:, t, :], x[:, t, :], hm[:, t, :], ALU.add))
                dve.sem_inc(x_ready, 1)

            def gemm(stage, groups):
                for i in range(sum(groups)):
                    split_lo(raw0[stage] + i, spl0[stage] + i)

            dve.memset(relb[BUCKETS:BUCKETS + 1, :], MASKED).then_inc(relb_set, 1)
            dve.wait_ge(ld_tab, 32)
            for o in range(2):
                dve.tensor_copy(relb[0:BUCKETS, :].rearrange("b (g o i) -> b g o i", o=2, i=2)[:, :, o, :],
                                rel_rows[:, :].rearrange("b (g i o) -> b g i o", o=2, i=2)[:, :, :, o]).then_inc(relb_set, 1)
            dve.wait_ge(cond_ready, 1)
            pc = pc0["ada"]
            for c in range(6):
                for k in range(KD):
                    if k == 0 and c >= 2:
                        dve.wait_ge(xb_full, pc)
                    ada_tile(c * KD + k, k, c % 2)
                    if c and k == 1:
                        for n in range(4 if IS_SCALE[c - 1] else 2):
                            ada_piece(0, c - 1, n, pc)
                            pc += 1
                        if c == 2:
                            pc += 8
            for n in range(2):
                ada_piece(0, 5, n, pc)
                pc += 1
            norm(0, "norm0")
            gemm("qkv", (KD, KD // 2))

            dve.wait_ge(qkv_ready, 1)
            dve.wait_ge(ld_att, 48)
            for t in range(T):
                dve.wait_ge(qk_sq, t + 1)
                own(dve.reduce_sum(qk_ss[:, :], qk_square[:, :].rearrange("p (h d) -> p h d", d=HD), axis=AX.X))
                dve.tensor_scalar(qk_ss[:, :], qk_ss[:, :], 1.0 / HD, EPS, ALU.mult, ALU.add).then_inc(qk_ms, 1)
                dve.wait_ge(qk_root, t + 1)
                own(dve.reciprocal(qk_ss[:, :], qk_ss[:, :]))
                v = qkv[:, t, 0:NQK * HD].rearrange("p (h d) -> p h d", d=HD)
                own(dve.tensor_tensor(v, v, qk_ss[:, :].unsqueeze(2).to_broadcast([P, NQK, HD]), ALU.mult))
                dve.tensor_tensor(v[:, 0:HEADS, :], v[:, 0:HEADS, :],
                                  qk_gain[:, 0:1, :].to_broadcast([P, HEADS, HD]), ALU.mult).then_inc(qk_ready, 1)
                for twice in range(2):
                    dve.tensor_tensor(k2[:, t, :, twice, :], v[:, HEADS:NQK, :],
                                      qk_gain[:, 1:2, :].to_broadcast([P, KV, HD]), ALU.mult).then_inc(qk_ready, 1)

            def unit_scores(u):
                g, blk = UNITS[u]
                w = P * (blk + 1)
                n = att_pair["s", u]
                dve.wait_ge(acc_full, full_no(n))
                s3 = sc[:, u % 2, 0:GQ * w].rearrange("p (i m) -> p i m", i=GQ)
                sink = sinks[:, GQ * g:GQ * (g + 1)].rearrange("p (i o) -> p o i", o=2)
                top_, exit_ = (stat[:, q, :].rearrange("p (o i) -> p o i", o=2) for q in (0, 3))
                for o in range(2):
                    own(dve.scalar_tensor_tensor(s3[:, 2 * o:2 * o + 2, :],
                                                 acc[n % 3][:, o * HALF:o * HALF + 2 * w].rearrange("p (i m) -> p i m", i=2), HD ** -0.5,
                                                 bias[:, GQ * g + 2 * o:GQ * g + 2 * o + 2, (1 - blk) * P:2 * P], ALU.mult, ALU.add))
                dve.sem_inc(acc_done[n % 3], 1)
                own(dve.reduce_max(stat[:, 0, :], s3, axis=AX.X))
                own(dve.tensor_tensor(top_, top_, sink, ALU.max))
                own(dve.tensor_scalar(stat[:, 1, :], stat[:, 0, :], -1.0, None, ALU.mult))
                dve.tensor_tensor(exit_, sink, top_, ALU.subtract).then_inc(max_ready, 1)

            def unit_probs(u):
                g, blk = UNITS[u]
                w = P * (blk + 1)
                dve.wait_ge(exp_ready, u + 1)
                s3 = sc[:, u % 2, 0:GQ * w].rearrange("p (i m) -> p i m", i=GQ)
                own(dve.tensor_tensor(stat[:, 0, :], stat[:, 2, :], stat[:, 3, :], ALU.add))
                own(dve.reciprocal(stat[:, 0, :], stat[:, 0, :]))
                dve.tensor_tensor(s3, s3, stat[:, 0, :].unsqueeze(2).to_broadcast([P, GQ, w]), ALU.mult).then_inc(p_ready, 1)

            for q in range(2):
                dve.wait_ge(xb_done[q], (pc0["qkv"] + 1 - q) // 2)
            unit_scores(0)
            for u in range(8):
                unit_probs(u)
                if u < 7:
                    unit_scores(u + 1)
                g, blk = UNITS[u]
                n = att_pair["o", u]
                lows[0] += 1
                dve.wait_ge(xb_hi, lows[0])
                part = (slice(None), slice(2 * g, 2 * g + 2), slice(blk * P, (blk + 1) * P))
                dve.tensor_tensor(a_lo[part], acc[n % 3][:, 0:2 * P].rearrange("p (k m) -> p k m", k=2), r32(a_hi[part]),
                                  ALU.subtract).then_inc(acc_done[n % 3], 1)

            gemm("wo", (KD,))
            residual("wo", 0, mod[:, MOD_SLOT[0][2], :])
            norm(1, "norm1")

            def body(B):
                e = B.e
                ada_n = 0
                for s in range(BODY):
                    split_lo(B.raw_no(s), B.spl + s, e)
                    if not B.mixture and ada_after(s):
                        c, k = divmod(ada_n, KD)
                        if k == 0 and c >= 2:
                            dve.wait_ge(ada_ready, 6 + c - 1)
                        ada_tile(B.raw_no(s) + 1, k, c % 2)
                        ada_n += 1
                    if B.mixture and s == 2:
                        dve.wait_ge(yd_hi_ready, B.rnd * (EXPERTS + 1) + 1 + rep(e, 1))
                        dve.tensor_tensor(yd_lo[:, :], acc[2][:, :], r32(yd_hi[:, :]), ALU.subtract).then_inc(acc_done[2], 1)
                    j, k = divmod(s, KD)
                    if 1 <= j <= FJ and k == 2:
                        for t in range(B.tiles):
                            q, _ = B.pair(j - 1, t)
                            dve.wait_ge(gate_ready, gates(B, j - 1, t))
                            dve.tensor_tensor(h[:, t, :], h[:, t, :], acc[q][:, HALF:2 * HALF], ALU.mult).then_inc(acc_done[q], 1)
                    if B.mixture and s == FJ * KD + 4:
                        build_pick(e + 1, B.rnd)
                    for c, kind, *which in pieces_read_after(B.mixture, s):
                        c += B.pc
                        if kind == "h":
                            j, t = which
                            part = (slice(None), slice(4 * j, 4 * j + 4), slice(t * P, (t + 1) * P))
                            d_hi, d_lo = (e_hi, e_lo) if B.mixture else (h_hi, h_lo)
                            dve.wait_ge(xb_hi, h_highs(B, j, t))
                            dve.tensor_tensor(d_lo[part], xb[c % 2][:, :].rearrange("p (k m) -> p k m", k=4), r32(d_hi[part]),
                                              ALU.subtract).then_inc(xb_done[c % 2], 1)
                        elif kind == "ada":
                            ada_piece(1, which[0], which[1], c)
                        elif kind == "scatter":
                            scatter_sum(c, which[0], which[1], e, e)
                        elif kind == "gather" and which[0] == 1:
                            dve.wait_ge(xb_full, c + 1 + rep(e, 16))
                            q = which[1]
                            dve.tensor_copy(g_lo[:, 4 * q:4 * q + 4, :], xb[c % 2][:, :].rearrange("p (k m) -> p k m", k=4)).then_inc(xb_done[c % 2], 1)

            def gates(B, j, t):
                if not B.mixture:
                    return T * j + t + 1
                return T * FJ + B.rnd * EXPERTS * FJ + j + 1 + rep(B.e, FJ)

            def h_highs(B, j, t):
                if not B.mixture:
                    return highs_ffn + T * j + t + 1
                return highs_moe + B.rnd * EXPERTS * FJ + j + 1 + rep(B.e, FJ)

            def build_pick(col, rnd):
                for t in range(T):
                    dve.tensor_scalar(pick[:, t, :], column, slot_of[:, t, bass.ds(col, 1)],
                                      None, ALU.is_equal).then_inc(pick_ready, 1)

            def scatter_sum(c, t, hf, col, e=0):
                dve.wait_ge(xb_full, c + 1 + rep(e, 16))
                dve.wait_ge(xb_done[c % 2], c // 2 + rep(e, 8))
                dst = y_sum[:, t, hf * HALF:(hf + 1) * HALF]
                dve.scalar_tensor_tensor(dst, xb[c % 2][:, :], comb[:, t, bass.ds(col, 1)], dst, ALU.mult, ALU.add).then_inc(xb_done[c % 2], 1)

            highs_ffn = lows[0]
            body(Body(False))
            lows[0] += T * FJ
            residual("ffn", FJ, mod[:, MOD_SLOT[0][5], :])
            norm(2, "norm2")
            dve.wait_ge(hm_ready, 6)
            dve.sem_inc(norm_free, 1)
            gemm("proj", (KD,) * 5)

            dve.wait_ge(ld_mix, 64)
            c = pc0["proj"]
            dve.wait_ge(xb_full, c + 1)
            own(dve.tensor_tensor(dt[:, :, :], xb[c % 2][:, 0:T * SH].rearrange("p (t m) -> p t m", t=T),
                                  srow[:, 0:1, :].to_broadcast([P, T, SH]), ALU.add))
            dve.sem_inc(xb_done[c % 2], 1)
            dve.sem_inc(dtv_ready, 1)
            own(dve.memset(u_pad[:, :, :, 0:TAPS - 1], 0.0))
            dve.sem_inc(u_ready, 1)
            for q in range(NCV):
                c = cv_piece["f", q]
                dve.wait_ge(xb_done[c % 2], c // 2 + 1)
                if q >= 2:
                    dve.wait_ge(cs_ready, q - 1)
                    if q - 2 < 8:
                        dve.wait_ge(xb_full, cv_piece["b", q - 2] + 1)
                for tap in range(TAPS):
                    for m in range(2):
                        k = 2 * q + m
                        src = u_pad[:, q % 2, m, tap:tap + SEQ]
                        wt = vecs[:, KD + tap * CH + k:KD + tap * CH + k + 1]
                        if tap == 0:
                            ins = dve.tensor_scalar(cv[:, q % 2, m, :], src, wt, vecs[:, KD + TAPS * CH + k:KD + TAPS * CH + k + 1],
                                                    ALU.mult, ALU.add)
                        else:
                            ins = dve.scalar_tensor_tensor(cv[:, q % 2, m, :], src, wt, cv[:, q % 2, m, :], ALU.mult, ALU.add)
                        steps[0] += 1
                        ins.then_inc(dve_step, 1)
                        if tap or m:
                            dve.wait_ge(dve_step, steps[0] - 1)
                dve.wait_ge(dve_step, steps[0])
                dve.sem_inc(cv_ready, 1)

            dve.wait_ge(dte_ready, 1)
            own(dve.scalar_tensor_tensor(dt[:, :, :], dt[:, :, :], 0.0, dt_e[:, :, :], ALU.max, ALU.add))
            dve.scalar_tensor_tensor(dt_a[:, :, :], dt[:, :, :], -1.0, srow[:, 1:2, :].to_broadcast([P, T, SH]),
                                     ALU.mult, ALU.mult).then_inc(dta_ready, 1)
            c = pc0["sums"]
            dve.wait_ge(xb_full, c + 1)
            own(dve.tensor_copy(acs[:, :, :], xb[c % 2][:, 0:2 * T * SH].rearrange("p (t m) -> p t m", t=2 * T)))
            dve.sem_inc(xb_done[c % 2], 1)
            own(dve.tensor_tensor(end_e[:, :, :], acs[:, T:2 * T, :], acs[:, 0:T, :], ALU.subtract))
            dve.sem_inc(acs_ready, 1)
            dve.wait_ge(acse_ready, 2)
            for q in range(2):
                dve.wait_ge(xb_done[q], (pc0["sums"] + 1 - q) // 2)

            def heads_of(row_, g):
                return row_[:, HG * g:HG * (g + 1)].unsqueeze(2)

            def unit_in(u):
                c, g = SUNITS[u]
                n = ssd_pair["a", u]
                dve.wait_ge(acc_full, full_no(n))
                d3 = dec[:, u % 2, :].rearrange("p (h m) -> p h m", h=HG)
                own(dve.tensor_tensor(d3, heads_of(acs[:, c, :], g).to_broadcast([P, HG, P]),
                                      acc[n % 3][:, :].rearrange("p (h m) -> p h m", h=HG), ALU.subtract))
                dve.sem_inc(acc_done[n % 3], 1)
                dve.sem_inc(d_ready, 1)
                xs3 = xbc[:, c, 512 * g:512 * (g + 1)].rearrange("p (h m) -> p h m", h=HG)
                xd3 = xd[:, u % 2, :].rearrange("p (h m) -> p h m", h=HG)
                own(dve.tensor_tensor(xd3, xs3, heads_of(dt[:, c, :], g).to_broadcast([P, HG, SHD]), ALU.mult))

            def unit_mid(u):
                c, g = SUNITS[u]
                pc = pc0["ssd"] + u
                dve.wait_ge(xb_full, pc + 1)
                if c == 0:
                    own(dve.tensor_tensor(xde[:, u % 2, :].rearrange("p (h m) -> p h m", h=HG), xd[:, u % 2, :].rearrange("p (h m) -> p h m", h=HG),
                                          heads_of(end_e[:, 0, :], g).to_broadcast([P, HG, SHD]), ALU.mult))
                own(dve.tensor_tensor(cbm[:, :], xb[pc % 2][:, 0:P], tri, ALU.mult))
                dve.sem_inc(xb_done[pc % 2], 1)
                dve.wait_ge(e_ready, u + 1)
                d3 = dec[:, u % 2, :].rearrange("p (h m) -> p h m", h=HG)
                dve.tensor_tensor(d3, d3, cbm[:, :].unsqueeze(1).to_broadcast([P, HG, P]), ALU.mult).then_inc(mt_ready, 1)

            def unit_out(u):
                c, g = SUNITS[u]
                n = ssd_pair["y", u]
                y = xbc[:, c, 512 * g:512 * (g + 1)]
                y3 = y.rearrange("p (h m) -> p h m", h=HG)
                own(dve.tensor_tensor(y3, y3, heads_of(srow[:, 2, :], g).to_broadcast([P, HG, SHD]), ALU.mult))
                dve.wait_ge(acc_full, full_no(n))
                if c == 0:
                    dve.tensor_copy(state[:, g, :], acc[n % 3][:, HALF:2 * HALF])
                else:
                    own(dve.tensor_tensor(y_tmp[:, :].rearrange("p (h m) -> p h m", h=HG),
                                          acc[n % 3][:, HALF:2 * HALF].rearrange("p (h m) -> p h m", h=HG),
                                          heads_of(acs_e[:, c, :], g).to_broadcast([P, HG, SHD]), ALU.mult))
                    own(dve.tensor_tensor(y, y, y_tmp[:, :], ALU.add))
                own(dve.tensor_tensor(y, y, acc[n % 3][:, 0:HALF], ALU.add))
                dve.sem_inc(acc_done[n % 3], 1)
                dve.tensor_tensor(y, y, z_s[:, c, 512 * g:512 * (g + 1)], ALU.mult).then_inc(y_ready, 1)

            unit_in(0)
            unit_in(1)
            unit_mid(0)
            for u in range(8):
                if u < 7:
                    unit_mid(u + 1)
                unit_out(u)
                if u < 6:
                    unit_in(u + 2)
            dve.wait_ge(yss_ready, 8)
            own(dve.reduce_sum(ss[:, :], yss[:, :, :], axis=AX.X))
            dve.tensor_scalar(ms[:, :], ss[:, :], 1.0 / DI, EPS, ALU.mult, ALU.add).then_inc(yms_ready, 1)
            dve.wait_ge(yroot, 1)
            own(dve.reciprocal(rs[:, :], rs[:, :]))
            dve.wait_ge(ld_norm, 16)
            for t in range(T):
                dve.scalar_tensor_tensor(xbc[:, t, 0:DI], xbc[:, t, 0:DI], rs[:, t:t + 1],
                                         mod[:, 0:2, :].rearrange("p a n -> p (a n)"), ALU.mult, ALU.mult).then_inc(yn_ready, 1)
            for n in range(8):
                t, q = divmod(n, 4)
                part = (slice(None), slice(4 * q, 4 * q + 4), slice(t * P, (t + 1) * P))
                piece_lo(pc0["ynorm"] + n, (y_hi[part], y_lo[part]))
            gemm("wout", (2 * KD,))
            residual("wout", 0, mod[:, MOD_SLOT[1][2], :])
            norm(3, "norm3")

            dve.wait_ge(xb_full, pc0["route"] + 1)
            b = xb[pc0["route"] % 2]
            own(dve.tensor_copy(lg[:, :, :], b[:, 0:T * EXPERTS].rearrange("p (t m) -> p t m", t=T)))
            dve.sem_inc(xb_done[pc0["route"] % 2], 1)
            for t in range(T):
                own(dve.max(mx[:, t, :], lg[:, t, :]))
                own(dve.max_index(mi[:, t, :], mx[:, t, :], lg[:, t, :]))
            own(dve.tensor_copy(mif[:, :, :], mi[:, :, :]))
            own(dve.tensor_tensor(tw[:, :, 0], mx[:, :, 1], mx[:, :, 0], ALU.subtract))
            dve.sem_inc(tw_in, 1)
            own(dve.memset(comb[:, :, :], 0.0))
            own(dve.memset(slot_of[:, :, :], -1.0))
            for t in range(T):
                for q in range(2):
                    own(dve.tensor_scalar(oh[:, t, q, :], column[:, 0:EXPERTS], mif[:, t, q:q + 1], None, ALU.is_equal))
                own(dve.tensor_tensor(msk[:, t, :], oh[:, t, 0, :], oh[:, t, 1, :], ALU.add))
            dve.sem_inc(mask_ready, 1)
            dve.wait_ge(tw_exp, 1)
            own(dve.tensor_scalar(tw[:, :, 1], tw[:, :, 0], 1.0, None, ALU.add))
            own(dve.reciprocal(tw[:, :, 1], tw[:, :, 1]))
            own(dve.tensor_tensor(tw[:, :, 2], tw[:, :, 0], tw[:, :, 1], ALU.mult))
            for t in range(T):
                own(dve.tensor_scalar(comb[:, t, 1:1 + EXPERTS], oh[:, t, 0, :], tw[:, t, 1:2], None, ALU.mult))
                own(dve.scalar_tensor_tensor(comb[:, t, 1:1 + EXPERTS], oh[:, t, 1, :], tw[:, t, 2:3], comb[:, t, 1:1 + EXPERTS],
                                             ALU.mult, ALU.add))
            c = pc0["route"] + 1
            dve.wait_ge(xb_full, c + 1)
            b = xb[c % 2]
            for t in range(T):
                own(dve.scalar_tensor_tensor(slot_of[:, t, 0:EXPERTS], b[:, t * EXPERTS:(t + 1) * EXPERTS], 1.0, msk[:, t, :],
                                             ALU.add, ALU.mult))
                own(dve.tensor_scalar(slot_of[:, t, 0:EXPERTS], slot_of[:, t, 0:EXPERTS], -1.0, None, ALU.add))
            own(dve.reduce_max(cmax[:, :], b[:, 2 * EXPERTS:3 * EXPERTS], axis=AX.X))
            dve.sem_inc(xb_done[c % 2], 1)
            own(dve.tensor_copy(flag[:, :], cmax[0:1, :]))
            own(dve.memset(y_sum[:, :, :], 0.0))
            own(dve.memset(r32(put[:, :, :]), 0.0))
            own(dve.memset(acc[2][:, :], 0.0))
            dve.sem_inc(route_ready, 1)

            highs_moe = lows[0]

            def experts(rnd):
                if rnd:
                    for q in range(2):
                        dve.wait_ge(xb_done[q], (pc0["moe"] + ROUND_PIECES + 1 - q) // 2)
                    own(dve.tensor_scalar(slot_of[:, :, :], slot_of[:, :, :], -float(P), None, ALU.add))
                    own(dve.memset(r32(put[:, :, :]), 0.0))
                    dve.sem_inc(route_ready, 1)
                build_pick(0, rnd)
                for q in range(2):
                    c = pc0["moe"] + rnd * ROUND_PIECES + 2 + q
                    dve.wait_ge(xb_full, c + 1)
                    dve.tensor_copy(g_lo[:, 4 * q:4 * q + 4, :], xb[c % 2][:, :].rearrange("p (k m) -> p k m", k=4)).then_inc(xb_done[c % 2], 1)
                with dve.Fori(0, EXPERTS) as e:
                    body(Body(True, e, rnd))
                dve.wait_ge(yd_hi_ready, (rnd + 1) * (EXPERTS + 1))
                dve.tensor_tensor(yd_lo[:, :], acc[2][:, :], r32(yd_hi[:, :]), ALU.subtract).then_inc(yd_lo_ready, 1)
                for n in range(4):
                    scatter_sum(pc0["moe"] + rnd * ROUND_PIECES + 4 + 16 * EXPERTS + n, n // 2, n % 2, EXPERTS)

            experts(0)
            most = dve.value_load(flag[0:1, 0:1], min_val=0, max_val=SEQ)
            with dve.If(most > overflow_at):
                experts(1)
            for q in range(2):
                dve.wait_ge(xb_done[q], (pc0["moe"] + ROUND_PIECES + 1 - q) // 2)
            for t in range(T):
                dve.tensor_tensor(y_sum[:, t, :], y_sum[:, t, :], mod[:, MOD_SLOT[1][5], :], ALU.mult).then_inc(final_step, 1)
                dve.wait_ge(final_step, 2 * t + 1)
                dve.tensor_tensor(x[:, t, :], x[:, t, :], y_sum[:, t, :], ALU.add).then_inc(final_step, 1)
            dve.wait_ge(final_step, 2 * T)
            dve.sem_inc(x_ready, 1)

        @block.tensor
        def _(pe):
            def open_piece(c, e=0, per=0):
                if c >= 2:
                    pe.wait_ge(xb_done[c % 2], c // 2 + rep(e, per // 2))
                return xb[c % 2]

            def open_pair(q, used):
                if not isinstance(used, int) or used:
                    pe.wait_ge(acc_done[q], used)
                return acc[q]

            def weight_tile(w, parts, pairs, lhs, tiles, first, last, e=0, no=0):
                l_hi, l_lo = lhs
                hi, lo = w_hi[:, w % SPLIT, :], w_lo[:, w % SPLIT, :]
                pe.wait_ge(hi_ready, w + 1 + rep(e, BODY))
                for t in range(tiles):
                    if first:
                        open_pair(*pairs[t])
                    for m, (k, to, col) in enumerate(parts):
                        o = acc[pairs[t][0]][:, to:to + HALF]
                        new = first and (m == 0 or parts[m][1] != parts[m - 1][1])
                        pe.matmul(o, l_hi[:, k, t * P:(t + 1) * P], hi[:, col:col + HALF], start=new, stop=False)
                        pe.matmul(o, l_lo[:, k, t * P:(t + 1) * P], hi[:, col:col + HALF], start=False, stop=False)
                pe.wait_ge(raw_used, no + 1 + rep(e, BODY))
                for t in range(tiles):
                    for m, (k, to, col) in enumerate(parts):
                        o = acc[pairs[t][0]][:, to:to + HALF]
                        end = last and (m == len(parts) - 1 or parts[m][1] != parts[m + 1][1])
                        mm = pe.matmul(o, l_hi[:, k, t * P:(t + 1) * P], lo[:, col:col + HALF], start=False, stop=end)
                mm.then_inc(w_used, 1)

            def gemm(stage, groups, lhs):
                i = 0
                for gi, tiles in enumerate(groups):
                    pr = pr0[stage] + T * gi
                    pairs = [((pr + t) % 3, (pr + t) // 3) for t in range(T)]
                    for n, parts in enumerate(tiles):
                        weight_tile(spl0[stage] + i, parts, pairs, lhs, T, n == 0, n == len(tiles) - 1, no=raw0[stage] + i)
                        i += 1

            def wide(k):
                return [(k, 0, 0), (k, HALF, HALF)]

            def turn(c, src, n):
                b = open_piece(c)
                for m in range(n):
                    mm = pe.transpose(b[:, m * P:(m + 1) * P], src(m), ident)
                mm.then_inc(xb_full, 1)

            def norm(n, stage):
                for t in range(T):
                    pe.wait_ge(hm_ready, T * n + t + 1)
                    for hf in range(2):
                        turn(pc0[stage] + 2 * t + hf, lambda m: hm[:, t, (4 * hf + m) * P:(4 * hf + m + 1) * P], 4)
                for q in range(2):
                    pe.wait_ge(xb_done[q], pieces_on(q, pc0[stage] + 4))

            def pieces_on(q, c):
                return (c + 1 - q) // 2

            pe.wait_ge(ld_square, 32)
            pe.wait_ge(ld_vecs, 48)
            pe.transpose(xb[0][:, 0:P], vec_rows[:, :], ident).then_inc(xb_full, 1)
            pe.wait_ge(relb_set, 3)
            pe.wait_ge(ld_tab, 32)
            pe.matmul(xb[1][0:HEADS, 0:3 * P], relb[:, :], table[:, :], start=True, stop=True).then_inc(xb_full, 1)
            pe.wait_ge(ld_rows, 32)

            def ada_group(layer, c, pc, raws):
                pe.wait_ge(raw_used, raws)
                for n in range(4 if IS_SCALE[c] else 2):
                    one_ada(layer, c, n, pc + n)

            def one_ada(layer, c, n, pc):
                b = open_piece(pc)
                cols = slice((n % 2) * HALF, (n % 2 + 1) * HALF)
                if IS_SCALE[c] and n < 2:
                    r = 12 + 2 * layer + (c > 2)
                    mm = pe.matmul(b[:, :], ident[0:16, r:r + 1].to_broadcast([16, P]), rows16[:, cols], start=True, stop=True)
                else:
                    r = 6 * layer + c
                    pe.matmul(b[:, :], ones, ada[:, c % 2, cols], start=True, stop=False)
                    mm = pe.matmul(b[:, :], ident[0:16, r:r + 1].to_broadcast([16, P]), rows16[:, cols], start=False, stop=True)
                mm.then_inc(xb_full, 1)
                if n == (3 if IS_SCALE[c] else 1):
                    pe.wait_ge(xb_full, pc + 1)
                    pe.sem_inc(ada_ready, 1)

            pc = pc0["ada"]
            for c in range(6):
                ada_group(0, c, pc, (c + 1) * KD)
                pc += 4 if IS_SCALE[c] else 2
                if c == 1:
                    pe.wait_ge(ld_bias, 16)
                    for n in range(8):
                        pe.matmul(open_piece(pc)[:, :], reversal[:, :], bias_rev[:, 2 * n:2 * n + 2, :].rearrange("p k m -> p (k m)"),
                                  start=True, stop=True).then_inc(xb_full, 1)
                        pc += 1
            norm(0, "norm0")
            gemm("qkv", [[wide(k) for k in range(KD)], [[(k, 0, 0), (k + 1, 0, HALF)] for k in range(0, KD, 2)]], (a_hi, a_lo))
            for t in range(T):
                pe.wait_ge(qk_ready, 3 * t + 3)
                for part in range(2):
                    turn(pc0["heads"] + 3 * t + part, lambda m: qkv[:, t, (4 * part + m) * P:(4 * part + m + 1) * P], 4)
                turn(pc0["heads"] + 3 * t + 2, lambda m: k2[:, t, m].rearrange("p a d -> p (a d)"), 4)
            for q in range(2):
                pe.wait_ge(xb_done[q], pieces_on(q, pc0["attend"]))

            def scores(u):
                g, blk = UNITS[u]
                w = P * (blk + 1)
                n = att_pair["s", u]
                o = open_pair(n % 3, n // 3)
                for i in range(GQ):
                    hh = HD * (i % 2)
                    at_ = HALF * (i % 2) + w * (i // 2)
                    mm = pe.matmul(o[:, at_:at_ + w], q_t[hh:hh + HD, (GQ * g + i) // 2, blk * P:(blk + 1) * P],
                                   k_t[hh:hh + HD, g, 0:w], start=True, stop=True)
                mm.then_inc(acc_full, 1)

            def attend(u):
                g, blk = UNITS[u]
                w = P * (blk + 1)
                pe.wait_ge(p_ready, u + 1)
                for kc in range(blk + 1):
                    turn(att_piece[u] + kc, lambda m: sc[:, u % 2, m * w + kc * P:m * w + (kc + 1) * P], GQ)
                for kc in range(blk + 1):
                    c = att_piece[u] + kc
                    pe.wait_ge(xb_done[c % 2], c // 2 + 1)
                n = att_pair["o", u]
                o = open_pair(n % 3, n // 3)
                for odd in range(2):
                    for kc in range(blk + 1):
                        probs = p_t[:, kc, 2 * P * odd:2 * P * (odd + 1)].rearrange("p (i m) -> p i m", i=2)
                        mm = pe.matmul(o[HD * odd:HD * (odd + 1), 0:2 * P].rearrange("p (i m) -> p i m", i=2),
                                       qkv[:, kc, D + KV * HD + g * HD:D + KV * HD + (g + 1) * HD], probs,
                                       start=kc == 0, stop=kc == blk)
                mm.then_inc(acc_full, 1)

            scores(0)
            scores(1)
            for u in range(8):
                attend(u)
                if u < 6:
                    scores(u + 2)
            for q in range(3):
                pe.wait_ge(acc_done[q], len([m for m in range(pr0["wo"]) if m % 3 == q]))
            gemm("wo", [[wide(k) for k in range(KD)]], (a_hi, a_lo))
            norm(1, "norm1")

            def body(B):
                e = B.e
                per = 16 if B.mixture else 0
                gu = (g_hi, g_lo) if B.mixture else (a_hi, a_lo)
                hid = (e_hi, e_lo) if B.mixture else (h_hi, h_lo)
                for s in range(BODY):
                    if s < FJ * KD:
                        j, k = divmod(s, KD)
                        first, last, lhs = k == 0, k == KD - 1, gu
                    else:
                        j, k = FJ, s - FJ * KD
                        first, last, lhs = k == 0, k == FK - 1, hid
                        if k % 4 == 0:
                            for c, *what in [w for v in PIECES[B.mixture].values() for w in v]:
                                if what[0] == "h" and what[1] == k // 4:
                                    c += B.pc
                                    pe.wait_ge(xb_done[c % 2], c // 2 + 1 + rep(e, per // 2))
                    if B.mixture and s == 0:
                        for c in (B.pc - 2, B.pc - 1):
                            pe.wait_ge(xb_done[c % 2], c // 2 + 1 + rep(e, per // 2))
                    if B.mixture and first and j == FJ:
                        pairs = [(2, B.pair(FJ, 0)[1] + 1)]
                    else:
                        pairs = [B.pair(j, t) for t in range(B.tiles)]
                    weight_tile(B.spl + s, wide(k), pairs, lhs, B.tiles, first, last, e, B.raw_no(s))
                    for c, kind, *which in PIECES[B.mixture].get(s, []):
                        c += B.pc
                        if kind == "h":
                            j, t = which
                            q, used = B.pair(j, t)
                            pe.wait_ge(acc_done[q], used + 1)
                            b = open_piece(c, e, per)
                            for m in range(4):
                                mm = pe.transpose(b[:, m * P:(m + 1) * P], h[:, t, m * P:(m + 1) * P], ident)
                            mm.then_inc(xb_full, 1)
                        elif kind == "ada":
                            cc, n = which
                            if n == 0:
                                pe.wait_ge(raw_used, ada_group_end[cc])
                            one_ada(1, cc, n, c)
                        elif kind == "scatter":
                            t, hf = which
                            pe.wait_ge(acc_done[2], B.pair(FJ, 0)[1] + 1)
                            scatter(c, t, hf, e, per)
                        elif kind == "put":
                            b = open_piece(c, e, per)
                            for t in range(T):
                                mm = pe.transpose(b[:, t * P:(t + 1) * P], r32(pick[:, t, :]), ident)
                            mm.then_inc(xb_full, 1)
                        elif kind == "gather":
                            gather(c, which[0], which[1], e, per, B.rnd)

            def scatter(c, t, hf, e, per):
                b = open_piece(c, e, per)
                cols = slice(hf * HALF, (hf + 1) * HALF)
                pe.matmul(b[:, :], put[:, t, :], yd_hi[:, cols], start=True, stop=False)
                pe.matmul(b[:, :], put[:, t, :], yd_lo[:, cols], start=False, stop=True).then_inc(xb_full, 1)

            def gather(c, low, hf, e, per, rnd):
                if low == 0 and hf == 0:
                    pe.wait_ge(pick_ready, rnd * T * (EXPERTS + 1) + T + rep(e, T) + (T if per else 0))
                b = open_piece(c, e, per)
                src = t_lo if low else t_hi
                for m in range(4):
                    for t in range(T):
                        mm = pe.matmul(b[:, m * P:(m + 1) * P], src[:, t, (4 * hf + m) * P:(4 * hf + m + 1) * P], pick[:, t, :],
                                       start=t == 0, stop=t == T - 1)
                mm.then_inc(xb_full, 1)

            ada_group_end, n = {}, 0
            for s in range(BODY):
                if ada_after(s):
                    n += 1
                    if n % KD == 0:
                        ada_group_end[n // KD - 1] = Body(False).raw_no(s) + 2
            body(Body(False))
            norm(2, "norm2")
            gemm("proj", [[wide(k) for k in range(KD)]] * 5, (a_hi, a_lo))
            pe.wait_ge(ld_mix, 64)
            c = pc0["proj"]
            b = open_piece(c)
            for t in range(T):
                for k in range(KD):
                    for src in (a_hi, a_lo):
                        mm = pe.matmul(b[:, t * SH:(t + 1) * SH], r32(src[:, k, t * P:(t + 1) * P]), w_dt[:, k, :],
                                       start=k == 0 and src is a_hi, stop=k == KD - 1 and src is a_lo)
            mm.then_inc(xb_full, 1)

            def conv_in(q):
                turn(cv_piece["f", q], lambda m: xbc[:, m % 2, (2 * q + m // 2) * P:(2 * q + m // 2 + 1) * P], 4)

            pe.wait_ge(xbc_ready, 1)
            conv_in(0)
            conv_in(1)
            for q in range(NCV):
                if q < CBACK:
                    pe.wait_ge(cs_ready, q + 1)
                    if q < 8:
                        turn(cv_piece["b", q], lambda m: cv[:, q % 2, m % 2, (m // 2) * P:(m // 2 + 1) * P], 4)
                    else:
                        turn(cv_piece["b", q], lambda m: b_t[:, 2 * (q % 2) + m % 2, (m // 2) * P:(m // 2 + 1) * P], 4)
                if q < NCV - 2:
                    conv_in(q + 2)
            pe.wait_ge(cs_ready, NCV)
            pe.wait_ge(dta_ready, 1)
            b = open_piece(pc0["sums"])
            for n in range(2 * T):
                mm = pe.matmul(b[:, n * SH:(n + 1) * SH], tri if n < T else ones, dt_a[:, n % T, :], start=True, stop=True)
            mm.then_inc(xb_full, 1)

            def unit_in(u):
                c, g = SUNITS[u]
                n = ssd_pair["a", u]
                o = open_pair(n % 3, n // 3)
                for i in range(HG):
                    mm = pe.matmul(o[:, i * P:(i + 1) * P], dt_a[:, c, HG * g + i:HG * g + i + 1].to_broadcast([P, P]), tri,
                                   start=True, stop=True)
                mm.then_inc(acc_full, 1)
                pc = pc0["ssd"] + u
                b = open_piece(pc)
                pe.matmul(b[:, 0:P], b_t[:, g, c * P:(c + 1) * P], c_t[:, g, c * P:(c + 1) * P], start=True, stop=True).then_inc(xb_full, 1)

            def unit_out(u):
                c, g = SUNITS[u]
                n = ssd_pair["y", u]
                pe.wait_ge(mt_ready, u + 1)
                o = open_pair(n % 3, n // 3)
                if c == 0:
                    pe.matmul(o[:, HALF:2 * HALF], xbc[:, c, DI + g * NS:DI + (g + 1) * NS], xde[:, u % 2, :], start=True, stop=True)
                else:
                    pe.matmul(o[:, HALF:2 * HALF], c_t[:, g, c * P:(c + 1) * P], state[:, g, :], start=True, stop=True)
                for i in range(HG):
                    mm = pe.matmul(o[:, i * SHD:(i + 1) * SHD], dec[:, u % 2, i * P:(i + 1) * P],
                                   xd[:, u % 2, i * SHD:(i + 1) * SHD], start=True, stop=True)
                mm.then_inc(acc_full, 1)

            unit_in(0)
            unit_in(1)
            for u in range(8):
                unit_out(u)
                if u < 6:
                    unit_in(u + 2)
            for n in range(8):
                t, q = divmod(n, 4)
                pe.wait_ge(yn_ready, t + 1)
                turn(pc0["ynorm"] + n, lambda m: xbc[:, t, (4 * q + m) * P:(4 * q + m + 1) * P], 4)
            for q in range(2):
                pe.wait_ge(xb_done[q], pieces_on(q, pc0["wout"]))
            gemm("wout", [[wide(k) for k in range(2 * KD)]], (y_hi, y_lo))
            norm(3, "norm3")

            pe.wait_ge(ld_router, 16)
            b = open_piece(pc0["route"])
            for t in range(T):
                for k in range(KD):
                    for src in (a_hi, a_lo):
                        mm = pe.matmul(b[:, t * EXPERTS:(t + 1) * EXPERTS], r32(src[:, k, t * P:(t + 1) * P]), w_r[:, k, :],
                                       start=k == 0 and src is a_hi, stop=k == KD - 1 and src is a_lo)
            mm.then_inc(xb_full, 1)
            pe.wait_ge(mask_ready, 1)
            b = open_piece(pc0["route"] + 1)
            pe.matmul(b[:, 0:EXPERTS], tri_strict, msk[:, 0, :], start=True, stop=True)
            pe.matmul(b[:, EXPERTS:2 * EXPERTS], tri_strict, msk[:, 1, :], start=True, stop=False)
            pe.matmul(b[:, EXPERTS:2 * EXPERTS], ones, msk[:, 0, :], start=False, stop=True)
            pe.matmul(b[:, 2 * EXPERTS:3 * EXPERTS], ones, msk[:, 0, :], start=True, stop=False)
            pe.matmul(b[:, 2 * EXPERTS:3 * EXPERTS], ones, msk[:, 1, :], start=False, stop=True).then_inc(xb_full, 1)

            def experts(rnd):
                pe.wait_ge(route_ready, rnd + 1)
                pe.wait_ge(t_lo_ready, T)
                for n in range(4):
                    gather(pc0["moe"] + rnd * ROUND_PIECES + n, n // 2, n % 2, 0, 0, rnd)
                with pe.Fori(0, EXPERTS) as e:
                    body(Body(True, e, rnd))
                pe.wait_ge(yd_lo_ready, rnd + 1)
                for n in range(4):
                    scatter(pc0["moe"] + rnd * ROUND_PIECES + 4 + 16 * EXPERTS + n, n // 2, n % 2, 0, 0)

            experts(0)
            most = pe.value_load(flag[0:1, 0:1], min_val=0, max_val=SEQ)
            with pe.If(most > overflow_at):
                experts(1)


_INS = ["x", "c", "ada_w", "ada_b", "norm_gain", "rel_bias", "attn_w_qkv", "attn_q_gain", "attn_k_gain",
        "attn_sinks", "attn_w_o", "ssm_w_in", "ssm_conv_w", "ssm_conv_b", "ssm_dt_bias", "ssm_a_log",
        "ssm_d", "ssm_norm_w", "ssm_w_out", "ffn_w_gu", "ffn_w_down", "moe_w_router", "moe_w_gu", "moe_w_down"]


def kernel(**inputs):
    import concourse.bacc as bacc
    from concourse.bass_utils import run_bass_kernel_spmd

    nc = bacc.Bacc("TRN2", target_bir_lowering=False, num_devices=1)
    f32 = mybir.dt.float32
    arrays = {name: np.ascontiguousarray(inputs[name]) for name in _INS}
    arrays["square"], arrays["table"] = shape_constants()
    A = {name: nc.dram_tensor(f"in_{name}", a.shape, f32, kind="ExternalInput").ap() for name, a in arrays.items()}
    out = nc.dram_tensor("out", (1, SEQ, D), f32, kind="ExternalOutput").ap()
    build(nc, A, out, A["square"], A["table"])
    r = run_bass_kernel_spmd(nc, [{f"in_{name}": a for name, a in arrays.items()}], core_ids=[0])
    return r.results[0]["out"]
```

```python
import math

import numpy as np
import concourse.bass as bass
from concourse import mybir

P = 128
D = 1024
SEQ = 256
T = SEQ // P
KD = D // P
HEADS, KV, HD = 16, 4, 64
GQ = HEADS // KV
QKV = (HEADS + 2 * KV) * HD
WINDOW, BUCKETS, MAXDIST = 128, 32, 128
DI = 2 * D
SH, SHD, SG, NS = 32, 64, 4, 128
HG = SH // SG
XBC = DI + 2 * SG * NS
NPROJ = DI + XBC + SH
TAPS = 4
CH = XBC // P
FF = 7 * D // 2
EXPERTS = 8
EPS = 1e-6
MASKED = -1e30

HALF = 512
TW = 1024
RAW = 12
SPLIT = 4
FJ = FF // HALF
FK = FF // P
BODY = FJ * KD + FK
LEAD = 3
EARLY = {"qkv": 3, "wo": 4, "ffn": 2, "proj": 3, "wout": 4}
assert BODY % RAW == 0 and BODY % SPLIT == 0

IS_SCALE = (0, 1, 0, 0, 1, 0)
MOD_SLOT = ((0, 1, 2, 3, 4, 5), (0, 1, 2, 3, 4, 6))


def bucket_of(dist):
    exact = BUCKETS // 2
    if dist < exact:
        return dist
    return min(BUCKETS - 1, exact + int(math.log(dist / exact) / math.log(MAXDIST / exact) * (BUCKETS - exact)))


def shape_constants():
    i = np.arange(P)
    square = np.zeros((P, 6, P), np.float32)
    square[:, 5] = np.eye(P)[::-1]
    square[:, 0] = np.eye(P)
    square[:, 1] = 1
    square[:, 2] = i[:, None] <= i[None]
    square[:, 3] = i[:, None] < i[None]
    square[:, 4] = i[None]
    table = np.zeros((BUCKETS + 1, 3 * P), np.float32)
    for j in range(3 * P):
        dist = 2 * P - 1 - j
        table[bucket_of(dist) if 0 <= dist < WINDOW else BUCKETS, j] = 1
    return square.reshape(P, 6 * P), table


def build(nc, A, out, square_in, table_in, overflow_at=P):
    f32, f32r, i32, u32 = mybir.dt.float32, mybir.dt.float32r, mybir.dt.int32, mybir.dt.uint32
    ACT = mybir.ActivationFunctionType
    ALU = mybir.AluOpType
    AX = mybir.AxisListType

    top = [(nc.sbuf_base + 31) // 32 * 32]

    def place(name, shape, dtype=f32, at=None):
        size = int(np.prod(shape[1:])) * 4
        if at is None:
            at = top[0]
            top[0] += (size + 31) // 32 * 32
        return nc.alloc_sbuf_tensor_at(name, shape, dtype, offset=at)

    def area(size):
        top[0] += size
        return top[0] - size

    raw = place("raw", [P, RAW, TW])
    w_hi = place("w_hi", [P, SPLIT, TW], f32r)
    w_lo = place("w_lo", [P, SPLIT, TW], f32r)
    x = place("x", [P, T, D])
    A_AT = area(2 * KD * SEQ * 4)
    U_AT = area(2 * FK * SEQ * 4)
    mod = place("mod", [P, 7, D])
    S_AT = area(2 * D * 4)
    square = place("square", [P, 5, P])
    F_AT = area(4096)
    bias_rows = place("bias_rows", [12, D])
    vecs = place("vecs", [P, P])
    cond = place("cond", [P, KD])
    cond_hi, cond_lo = (place(n, [P, KD], f32r) for n in ("cond_hi", "cond_lo"))
    ss, ms, rs = (place(n, [P, 2]) for n in ("ss", "ms", "rs"))
    flag = place("flag", [1, 1], i32)
    spare = place("spare", [P, 9])
    w_r = place("w_r", [P, KD, EXPERTS])
    comb = place("comb", [P, T, EXPERTS + 1])
    slot_of = place("slot_of", [P, T, EXPERTS + 1])
    assert top[0] <= nc.sbuf_usable_end, top[0]
    ident, ones, tri, tri_strict, column = (square[:, n, :] for n in range(5))

    rel_rows = place("rel_rows", [BUCKETS, HEADS], f32, A_AT + 512)
    vec_rows = place("vec_rows", [P, P], f32, A_AT)
    a_hi = place("a_hi", [P, KD, SEQ], f32r, A_AT)
    a_lo = place("a_lo", [P, KD, SEQ], f32r, A_AT + KD * SEQ * 4)
    ada = place("ada", [P, 2, D], f32, S_AT)
    hm = place("hm", [P, T, D], f32, S_AT)
    h_hi = place("h_hi", [P, FK, SEQ], f32r, U_AT)
    h_lo = place("h_lo", [P, FK, SEQ], f32r, U_AT + FK * SEQ * 4)
    h = place("h", [P, T, HALF], f32, F_AT)
    qkv = place("qkv", [P, T, QKV], f32, U_AT)
    bias = place("bias", [P, HEADS, 2 * P], f32, U_AT + 12288)
    bias_rev = place("bias_rev", [P, KV, GQ, 2 * P], f32, A_AT)
    BIAS_PLACE = (0, 2, 1, 3)
    reversal = mod[:, 6, 0:P]
    q_t = place("q_t", [P, KD, SEQ], f32, U_AT + 28672)
    k_t = place("k_t", [P, KV, SEQ], f32, U_AT + 36864)
    sc = place("sc", [P, 2, GQ * 2 * P], f32, U_AT + 40960)
    qk_square = place("qk_square", [P, (HEADS + KV) * HD], f32, U_AT + 40960)
    p_t = [place("p_t0", [P, 1, GQ * P], f32, U_AT + 53248), place("p_t1", [P, 2, GQ * P], f32, U_AT + 49152)]
    k2 = place("k2", [P, T, KV, 2, HD], f32, U_AT + 53248)
    sinks = place("sinks", [P, HEADS], f32, F_AT)
    qk_gain = place("qk_gain", [P, 2, HD], f32, F_AT + 64)
    relb = place("relb", [BUCKETS + 1, HEADS], f32, F_AT + 576)
    table = place("table", [BUCKETS + 1, 3 * P], f32, F_AT + 640)
    reltab = place("reltab", [HEADS, 3 * P], f32, F_AT + 2176)
    NQK = HEADS + KV
    qk_ss = place("qk_ss", [P, NQK], f32, F_AT + 3712)
    stat = place("stat", [P, 2, 4, GQ], f32, F_AT + 3808)
    z_s = place("z_s", [P, T, DI], f32, U_AT)
    xbc = place("xbc", [P, T, XBC], f32, U_AT + 16384)
    b_t = place("b_t", [P, SG, SEQ], f32, U_AT + 40960)
    c_t = place("c_t", [P, SG, SEQ], f32, U_AT + 45056)
    u_pad = place("u_pad", [P, 2, 2, SEQ + TAPS], f32, S_AT)
    cv = place("cv", [P, 2, 2, SEQ], f32, U_AT + 49152)
    dec = place("dec", [P, 2, HG * P], f32, U_AT + 49152)
    xd = place("xd", [P, 2, HG * SHD], f32, A_AT)
    xde = place("xde", [P, 2, HG * SHD], f32, A_AT + 4096)
    y_tmp = place("y_tmp", [P, HG * SHD], f32, S_AT)
    y_sq = place("y_sq", [P, HG * SHD], f32, S_AT + 2048)
    state = place("state", [P, SG, HG * SHD], f32, A_AT + 8192)
    w_dt = place("w_dt", [P, KD, SH], f32, F_AT)
    srow = place("srow", [P, 3, SH], f32, F_AT + 1024)
    dt = place("dt", [P, T, SH], f32, F_AT + 1408)
    dt_a = place("dt_a", [P, T, SH], f32, F_AT + 1664)
    dt_e = place("dt_e", [P, T, SH], f32, F_AT + 1920)
    acs = place("acs", [P, 2 * T, SH], f32, F_AT + 2176)
    acs_e = place("acs_e", [P, T, SH], f32, F_AT + 2688)
    end_e = place("end_e", [P, T, SH], f32, F_AT + 2944)
    cbm = place("cbm", [P, P], f32, F_AT + 3200)
    yss = place("yss", [P, T, SG], f32, F_AT + 3712)
    y_hi = place("y_hi", [P, DI // P, SEQ], f32r, A_AT)
    y_lo = place("y_lo", [P, DI // P, SEQ], f32r, U_AT)
    EH = FK * P * 4
    e_hi = place("e_hi", [P, FK, P], f32r, U_AT)
    e_lo = place("e_lo", [P, FK, P], f32r, U_AT + EH)
    t_hi = place("t_hi", [P, T, D], f32r, U_AT + 2 * EH)
    t_lo = place("t_lo", [P, T, D], f32r, U_AT + 2 * EH + 8192)
    y_sum = place("y_sum", [P, T, D], f32, U_AT + 2 * EH + 16384)
    pick = place("pick", [P, T, P], f32r, U_AT + 2 * EH + 24576)
    put = place("put", [P, T, P], f32r, U_AT + 2 * EH + 25600)
    g_hi = place("g_hi", [P, KD, P], f32r, A_AT)
    g_lo = place("g_lo", [P, KD, P], f32r, A_AT + 4096)
    yd_hi = place("yd_hi", [P, D], f32r, A_AT + 8192)
    yd_lo = place("yd_lo", [P, D], f32r, A_AT + 12288)
    lg = place("lg", [P, T, EXPERTS], f32, F_AT + 2304)
    mx = place("mx", [P, T, 8], f32, F_AT + 2368)
    mi = place("mi", [P, T, 8], u32, F_AT + 2432)
    mif = place("mif", [P, T, 8], f32, F_AT + 2496)
    oh = place("oh", [P, T, 2, EXPERTS], f32, F_AT + 2560)
    tw = place("tw", [P, T, 3], f32, F_AT + 2688)
    msk = place("msk", [P, T, EXPERTS], f32, F_AT + 2720)
    cmax = place("cmax", [P, 1], f32, F_AT + 2784)

    acc = [nc.alloc_psum_tensor(f"acc{n}", [P, 2 * HALF], f32) for n in range(3)]
    xb = [nc.alloc_psum_tensor(f"xb{n}", [P, HALF], f32) for n in range(2)]
    rel_dram = nc.dram_tensor("rel_scratch", (HEADS, 3 * P), f32, kind="Internal").ap()

    def r32(ap):
        return ap.bitcast(f32)

    sem = nc.alloc_semaphore
    raw_ready = [sem(f"raw_ready{n}") for n in range(RAW)]
    raw_used = sem("raw_used")
    hi_ready = sem("hi_ready")
    w_used = sem("w_used")
    acc_full = sem("acc_full")
    acc_done = [sem(f"acc_done{n}") for n in range(3)]
    xb_full = sem("xb_full")
    xb_done = [sem(f"xb_done{n}") for n in range(2)]
    xb_hi = sem("xb_hi")
    dve_step = sem("dve_step")
    act_step = sem("act_step")
    ld_square, ld_rows, ld_vecs, ld_x, ld_tab, ld_att, ld_bias, ld_mix, ld_norm, ld_router, st_rel, st_out = (
        sem(n) for n in ("ld_square", "ld_rows", "ld_vecs", "ld_x", "ld_tab", "ld_att", "ld_bias", "ld_mix",
                         "ld_norm", "ld_router", "st_rel", "st_out"))
    relb_set, cond_ready, ada_ready, ld_gain = (
        sem(n) for n in ("relb_set", "cond_ready", "ada_ready", "ld_gain"))
    ss_ready, ms_ready, root_ready, hm_ready, x_ready = (
        sem(n) for n in ("ss_ready", "ms_ready", "root_ready", "hm_ready", "x_ready"))
    qkv_ready, qk_sq, qk_ms, qk_root, qk_ready, max_ready, exp_ready, p_ready = (
        sem(n) for n in ("qkv_ready", "qk_sq", "qk_ms", "qk_root", "qk_ready", "max_ready",
                         "exp_ready", "p_ready"))
    gate_ready = sem("gate_ready")
    z_ready, u_ready, cv_ready, cs_ready, norm_free = (
        sem(n) for n in ("z_ready", "u_ready", "cv_ready", "cs_ready", "norm_free"))
    dtv_ready, dte_ready, dta_ready, acs_ready, acse_ready = (
        sem(n) for n in ("dtv_ready", "dte_ready", "dta_ready", "acs_ready", "acse_ready"))
    d_ready, e_ready, mt_ready, y_ready, yss_ready, yms_ready, yroot, yn_ready = (
        sem(n) for n in ("d_ready", "e_ready", "mt_ready", "y_ready", "yss_ready", "yms_ready",
                         "yroot", "yn_ready"))
    t_hi_ready, t_lo_ready, tw_in, tw_exp, mask_ready, route_ready = (
        sem(n) for n in ("t_hi_ready", "t_lo_ready", "tw_in", "tw_exp", "mask_ready", "route_ready"))
    pick_ready, put_ready, yd_hi_ready, yd_lo_ready, final_step = (
        sem(n) for n in ("pick_ready", "put_ready", "yd_hi_ready", "yd_lo_ready", "final_step"))

    def ada_after(s):
        return (s + 1) * 6 * KD // BODY != s * 6 * KD // BODY

    n_ada = 6 * KD
    raw0, spl0, pc0, pr0 = {}, {}, {}, {}
    at = [0, 0, 0, 0]
    for stage, raws, splits, pieces, pairs in (
        ("start", 0, 0, 2, 0), ("ada", 2 * KD, 2 * KD, 0, 2), ("norm0", 0, 0, 4, 0),
        ("qkv", 12, 12, 0, 4), ("heads", 0, 0, 6 + 2, 0), ("attend", 4 * KD, 0, 20 + 6, 12),
        ("wo", KD, KD, 0, 2), ("norm1", 0, 0, 4, 0),
        ("ffn", BODY + n_ada, BODY, 2 * FJ + 12, 2 * FJ + 2), ("norm2", 0, 0, 4, 0),
        ("proj", 5 * KD, 5 * KD, 1 + 22 + 1, 10),
        ("ssd", 0, 0, 8, 16), ("ynorm", 0, 0, 8, 0), ("wout", 2 * KD, 2 * KD, 0, 2),
        ("norm3", 0, 0, 4, 0), ("route", 0, 0, 2, 0), ("moe", 0, 0, 0, 0),
    ):
        raw0[stage], spl0[stage], pc0[stage], pr0[stage] = at
        at = [a + b for a, b in zip(at, (raws, splits, pieces, pairs))]

    def body_pieces(mixture):
        after = {}
        for j in range(FJ):
            after.setdefault(KD * (j + 1) + 3, []).extend(("h", j, t) for t in range(1 if mixture else T))
        if mixture:
            for n in range(2 * T):
                after.setdefault(2 * KD + 4 + 2 * n, []).append(("scatter", n // 2, n % 2))
            after.setdefault(3 * KD + 4, []).append(("put",))
            for n in range(4):
                after.setdefault(FJ * KD + 8 + 4 * n, []).append(("gather", n // 2, n % 2))
        else:
            done = 0
            for s in range(BODY):
                if ada_after(s):
                    done += 1
                    if done % KD == 0:
                        c = done // KD - 1
                        after.setdefault(min(s + 1, BODY - 1), []).extend(("ada", c, n) for n in range(2))
        order, n = {}, 0
        for s in sorted(after):
            order[s] = [(n + m, *what) for m, what in enumerate(after[s])]
            n += len(after[s])
        return order

    PIECES = {False: body_pieces(False), True: body_pieces(True)}
    assert sum(len(v) for v in PIECES[True].values()) == 16
    assert sum(len(v) for v in PIECES[False].values()) == 2 * FJ + 12

    def pieces_read_after(mixture, s):
        last = s == BODY - 1
        found = list(PIECES[mixture].get(s - LEAD, []))
        if last:
            for later in range(s - LEAD + 1, BODY):
                found += PIECES[mixture].get(later, [])
        return found

    UNITS = [(g, b) for g in range(KV) for b in range(T)]
    PER_UNIT = 4 * KD // len(UNITS)

    def score_pair(u):
        return pr0["attend"] + 3 * (u // 2) + u % 2

    def ada_pair(c):
        return pr0["ada"] + c if c < 2 else pr0["attend"] + 3 * (c - 2) + 2

    att_piece, out_piece, bias_piece, n = {}, {}, {0: pc0["heads"] + 3}, pc0["attend"]
    for u, (g, b) in enumerate(UNITS):
        if u:
            out_piece[u - 1] = n
            n += 1
        att_piece[u] = n
        n += b + 1
        if u < KV - 1:
            bias_piece[u + 1] = n
            n += 2
    out_piece[len(UNITS) - 1] = n
    assert n + 1 == pc0["wo"]

    def turn_piece(t, part):
        return pc0["heads"] + 5 * t + part

    SUNITS = [(c, g) for c in range(T) for g in range(SG)]
    ssd_pair, n = {}, pr0["ssd"]
    for what in [("a", 0), ("a", 1)] + [w for u in range(8) for w in ([("y", u)] + ([("a", u + 2)] if u < 6 else []))]:
        ssd_pair[what] = n
        n += 1
    def full_no(n):
        return len(UNITS) + n - pr0["ssd"] + 1

    PROJ_GROUPS = (2, 3, 4, 0, 1)
    NCV = CH // 2
    CBACK = 10

    def conv_in_at(q):
        return KD + 2 + 2 * q

    def conv_back_at(q):
        return conv_in_at(q) + 4

    DT_AT = 6
    SUMS_AT = KD + 3
    sums_piece = pc0["proj"] + 2
    cv_piece, n = {("f", 0): pc0["proj"] + 1}, pc0["proj"] + 3
    for what in [("f", 1)] + [w for q in range(NCV) for w in (([("b", q)] if q < CBACK else []) + ([("f", q + 2)] if q < NCV - 2 else []))]:
        cv_piece[what] = n
        n += 1
    assert n == pc0["ssd"]

    moe_uses = [(FJ + 1) // 2, FJ // 2, 1]
    pair_uses0 = [len([m for m in range(pr0["moe"]) if m % 3 == q]) for q in range(3)]
    ROUND_PIECES = 4 + 16 * EXPERTS + 4

    class Body:

        def __init__(self, mixture, e=0, rnd=0):
            self.mixture, self.e = mixture, e
            self.tiles = 1 if mixture else T
            if mixture:
                self.raw = raw0["moe"] + rnd * EXPERTS * BODY
                self.spl = spl0["moe"] + rnd * EXPERTS * BODY
                self.pc = pc0["moe"] + rnd * ROUND_PIECES + 4
                self.pr = pr0["moe"] + rnd * EXPERTS * (FJ + 1)
                self.rnd = rnd
            else:
                self.raw, self.spl, self.pc, self.pr, self.rnd = raw0["ffn"], spl0["ffn"], pc0["ffn"], pr0["ffn"], 0

        def raw_no(self, s):
            extra = 0 if self.mixture else s * n_ada // BODY
            return self.raw + s + extra

        def pair(self, j, t):
            if not self.mixture:
                n = self.pr + T * j + t
                return n % 3, n // 3
            q = 2 if j == FJ else j % 2
            used = pair_uses0[q] + self.rnd * EXPERTS * moe_uses[q] + (0 if j == FJ else j // 2)
            return q, used + self.e * moe_uses[q]

        def full(self, j):
            return self.spl + KD * (j + 1) + self.e * BODY

    def rep(e, per):
        return e * per

    def swiglu_source(w_gu, w_down, s):
        if s < FJ * KD:
            j, k = divmod(s, KD)
            return w_gu[k * P:(k + 1) * P, :].rearrange("p (h n) -> p h n", h=2)[:, :, j * HALF:(j + 1) * HALF]
        k = s - FJ * KD
        return w_down[k * P:(k + 1) * P, :]

    block = nc.Block()
    with block:

        @block.sync
        def _(sp):
            def load(no, src, e=0):
                if no >= RAW:
                    sp.wait_ge(raw_used, no - RAW + 1 + rep(e, BODY))
                dst = raw[:, no % RAW, :]
                if len(src.shape) == 3:
                    dst = dst.rearrange("p (h n) -> p h n", h=src.shape[1])
                sp.dma_start(dst, src).then_inc(raw_ready[no % RAW], 16)

            def row(src, n):
                return bass.AP(src.tensor, src.offset, [[0, P], [1, n]])

            sp.dma_start(square[:, :, :], square_in[:, 0:5 * P].rearrange("p (n m) -> p n m", n=5)).then_inc(ld_square, 16)
            sp.dma_start(reversal, square_in[:, 5 * P:6 * P]).then_inc(ld_square, 16)
            sp.dma_start(vec_rows[0:KD, :], A["c"].rearrange("b (k p) -> (b k) p", p=P)).then_inc(ld_vecs, 16)
            sp.dma_start(vec_rows[KD:KD + TAPS * CH, :], A["ssm_conv_w"][0].rearrange("t (k p) -> (t k) p", p=P)).then_inc(ld_vecs, 16)
            sp.dma_start(vec_rows[KD + TAPS * CH:P, :], A["ssm_conv_b"].rearrange("b (k p) -> (b k) p", p=P)).then_inc(ld_vecs, 16)
            sp.dma_start(table[:, :], table_in).then_inc(ld_tab, 16)
            sp.dma_start(rel_rows[:, :], A["rel_bias"]).then_inc(ld_tab, 16)
            sp.dma_start(bias_rows[:, :], A["ada_b"].rearrange("l (g n) -> (l g) n", n=D)).then_inc(ld_rows, 16)
            sp.dma_start(x[:, :, :], A["x"][0].rearrange("(t p) n -> p t n", p=P)).then_inc(ld_x, 16)
            sp.dma_start(w_r[:, :, :], A["moe_w_router"][0].rearrange("(k p) n -> p k n", p=P)).then_inc(ld_router, 16)
            sp.dma_start(sinks[:, :], row(A["attn_sinks"], HEADS)).then_inc(ld_att, 16)
            sp.dma_start(qk_gain[:, 0, :], row(A["attn_q_gain"], HD)).then_inc(ld_att, 16)
            sp.dma_start(qk_gain[:, 1, :], row(A["attn_k_gain"], HD)).then_inc(ld_att, 16)

            def ada_load(layer, no, i):
                c, k = divmod(i, KD)
                load(no, A["ada_w"][layer, k * P:(k + 1) * P, c * D:(c + 1) * D])

            no = 0
            for i in range(2 * KD):
                ada_load(0, no, i)
                no += 1
                if i == KD:
                    for half in range(2):
                        sp.dma_start(mod[:, 1 + 3 * half, :], row(A["norm_gain"][0, half:half + 1, :], D)).then_inc(ld_gain, 16)
                    sp.wait_ge(xb_done[1], 1)
                    sp.dma_start(rel_dram, reltab[:, :]).then_inc(st_rel, 16)
            w = A["attn_w_qkv"][0]
            for k in range(KD):
                load(no, w[k * P:(k + 1) * P, 0:D])
                no += 1
            for k in range(0, KD, 2):
                load(no, w[k * P:(k + 2) * P, D:QKV].rearrange("(h p) n -> p h n", h=2))
                no += 1
            for i in range(2 * KD, 6 * KD):
                if i == 2 * KD + RAW:
                    sp.wait_ge(st_rel, 16)
                    sp.wait_ge(w_used, spl0["heads"])
                    for g in range(KV):
                        sp.dma_start(bias_rev[:, BIAS_PLACE[g], :, :],
                                     bass.AP(rel_dram.tensor, g * GQ * 3 * P, [[1, P], [3 * P, GQ], [1, 2 * P]])).then_inc(ld_bias, 16)
                ada_load(0, no, i)
                no += 1
            for k in range(KD):
                load(no, A["attn_w_o"][0, k * P:(k + 1) * P, :])
                no += 1
            n = 0
            for s in range(BODY):
                load(no, swiglu_source(A["ffn_w_gu"][0], A["ffn_w_down"][0], s))
                no += 1
                if s == RAW:
                    sp.wait_ge(hm_ready, 4 * T)
                    for c in range(6):
                        src = A["norm_gain"][1, c // 3:c // 3 + 1, :] if IS_SCALE[c] else A["ada_b"][1:2, c * D:(c + 1) * D]
                        sp.dma_start(mod[:, MOD_SLOT[1][c], :], row(src, D)).then_inc(ld_gain, 16)
                if ada_after(s):
                    ada_load(1, no, n)
                    n += 1
                    no += 1
            w = A["ssm_w_in"][0]
            for i in range(5 * KD):
                g, k = PROJ_GROUPS[i // KD], i % KD
                load(no, w[k * P:(k + 1) * P, g * TW:(g + 1) * TW])
                no += 1
                if i == KD - 1:
                    sp.wait_ge(x_ready, 2 * T)
                    sp.dma_start(w_dt[:, :, :], w[:, 5 * TW:NPROJ].rearrange("(k p) n -> p k n", p=P)).then_inc(ld_mix, 16)
                    for r, name in enumerate(("ssm_dt_bias", "ssm_a_log", "ssm_d")):
                        sp.dma_start(srow[:, r, :], row(A[name], SH)).then_inc(ld_mix, 16)
            sp.wait_ge(norm_free, 1)
            sp.dma_start(mod[:, 0:2, :], bass.AP(A["ssm_norm_w"].tensor, 0, [[0, P], [1, DI]])).then_inc(ld_norm, 16)
            for k in range(2 * KD):
                load(no, A["ssm_w_out"][0, k * P:(k + 1) * P, :])
                no += 1
            assert no == raw0["moe"]

            def experts(rnd):
                with sp.Fori(0, EXPERTS) as e:
                    for s in range(BODY):
                        load(raw0["moe"] + rnd * EXPERTS * BODY + s,
                             swiglu_source(A["moe_w_gu"][0, e], A["moe_w_down"][0, e], s), e)

            experts(0)
            sp.wait_ge(route_ready, 1)
            most = sp.value_load(flag[0:1, 0:1], min_val=0, max_val=SEQ)
            with sp.If(most > overflow_at):
                experts(1)
            sp.wait_ge(x_ready, 3 * T + 1)
            sp.dma_start(out[0].rearrange("(t p) n -> p t n", p=P), x[:, :, :]).then_inc(st_out, 16)
            sp.wait_ge(st_out, 16)

        @block.scalar
        def _(act):
            steps = [0]

            def own(ins):
                steps[0] += 1
                ins.then_inc(act_step, 1)
                act.wait_ge(act_step, steps[0])

            def split_hi(no, w, e=0, per=0, per_raw=0):
                act.wait_ge(raw_ready[no % RAW], 16 * (no // RAW + 1) + rep(e, 16 * per_raw // RAW))
                if w >= SPLIT:
                    act.wait_ge(w_used, w - SPLIT + 1 + rep(e, per))
                act.activation(w_hi[:, w % SPLIT, :], raw[:, no % RAW, :], ACT.Copy).then_inc(hi_ready, 1)

            def early_hi(stage):
                for i in range(EARLY[stage]):
                    split_hi(raw0[stage] + i, spl0[stage] + i)

            def warm(function):
                warmed[0] += 1
                act.activation(spare[:, warmed[0]:warmed[0] + 1], ones[:, 0:1], function)

            warmed = [-1]

            def piece(c):
                act.wait_ge(xb_full, c + 1)
                return xb[c % 2]

            def gemm(stage, evacuate, groups, after=None):
                i = 0
                pr = pr0[stage]
                early = EARLY.get(stage, 0)

                def out_of(gi):
                    act.wait_ge(w_used, spl0[stage] + sum(groups[:gi + 1]))
                    evacuate(gi, pr + T * gi)

                for gi, n_tiles in enumerate(groups):
                    for k in range(n_tiles):
                        if i >= early:
                            split_hi(raw0[stage] + i, spl0[stage] + i)
                        i += 1
                        if evacuate and gi and k == 1:
                            out_of(gi - 1)
                        if after:
                            after(i - 1)
                if evacuate:
                    out_of(len(groups) - 1)

            def norm_root(n):
                warm(ACT.Sqrt)
                if n == 0:
                    act.wait_ge(ld_x, 16)
                for t in range(T):
                    if n:
                        act.wait_ge(x_ready, T * (n - 1) + t + 1)
                    act.activation(hm[:, t, :], x[:, t, :], ACT.Square, accum_out=ss[:, t:t + 1]).then_inc(ss_ready, 1)
                act.wait_ge(ms_ready, n + 1)
                act.activation(rs[:, :], ms[:, :], ACT.Sqrt).then_inc(root_ready, 1)

            def norm(n, stage):
                if n:
                    norm_root(n)
                for hf in range(2):
                    for t in range(T):
                        b = piece(pc0[stage] + T * hf + t)
                        act.activation(a_hi[:, 4 * hf:4 * hf + 4, t * P:(t + 1) * P],
                                       b[:, :].rearrange("p (k m) -> p k m", k=4), ACT.Copy).then_inc(xb_hi, 1)
                if n == 3:
                    for t in range(T):
                        act.activation(t_hi[:, t, :], hm[:, t, :], ACT.Copy).then_inc(t_hi_ready, 1)

            b = piece(0)
            act.activation(vecs[:, :], b[:, 0:P], ACT.Copy).then_inc(xb_done[0], 1)
            act.wait_ge(xb_done[0], 1)
            act.activation(cond[:, :], vecs[:, 0:KD], ACT.Silu).then_inc(cond_ready, 1)
            act.wait_ge(cond_ready, 1)
            act.activation(cond_hi[:, :], cond[:, :], ACT.Copy).then_inc(cond_ready, 1)
            b = piece(1)
            act.activation(reltab[:, :], b[0:HEADS, 0:3 * P], ACT.Copy).then_inc(xb_done[1], 1)
            norm_root(0)

            def ada_hi(first, n):
                for i in range(first, first + n):
                    split_hi(raw0["ada"] + i, spl0["ada"] + i)

            ada_hi(0, 2 * KD)
            early_hi("qkv")
            norm(0, "norm0")

            def qkv_out(g, pr):
                lo, n = (0, D) if g == 0 else (D, QKV - D)
                for t in range(T):
                    act.activation(qkv[:, t, lo:lo + n], acc[(pr + t) % 3][:, 0:n], ACT.Copy).then_inc(acc_done[(pr + t) % 3], 1)

            gemm("qkv", qkv_out, (KD, KD // 2))
            pr = pr0["qkv"]
            for q in range(3):
                act.wait_ge(acc_done[q], len([m for m in range(pr + 4) if m % 3 == q]))
            act.sem_inc(qkv_ready, 1)
            for t in range(T):
                if t:
                    act.wait_ge(qk_ms, t)
                act.activation(qk_square[:, :], qkv[:, t, 0:NQK * HD], ACT.Square).then_inc(qk_sq, 1)
                act.wait_ge(qk_ms, t + 1)
                act.activation(qk_ss[:, :], qk_ss[:, :], ACT.Sqrt).then_inc(qk_root, 1)
            def bias_in(g):
                for m in range(2):
                    n, c = 2 * g + m, bias_piece[g] + m
                    b = piece(c)
                    act.activation(bias[:, 2 * n:2 * n + 2, :], b[:, :].rearrange("p (k m) -> p k m", k=2), ACT.Copy).then_inc(xb_done[c % 2], 1)

            for t in range(T):
                for part in range(3):
                    c = turn_piece(t, part)
                    b = piece(c)
                    dst = k_t[:, :, t * P:(t + 1) * P] if part == 2 else q_t[:, 4 * part:4 * part + 4, t * P:(t + 1) * P]
                    act.activation(dst, b[:, :].rearrange("p (k m) -> p k m", k=4), ACT.Copy).then_inc(xb_done[c % 2], 1)
                if t == 0:
                    bias_in(0)

            def exps(u):
                g, blk = UNITS[u]
                w = P * (blk + 1)
                act.wait_ge(max_ready, u + 1)
                for i in range(GQ):
                    act.activation(sc[:, u % 2, i * w:(i + 1) * w], sc[:, u % 2, i * w:(i + 1) * w], ACT.Exp,
                                   bias=stat[:, u % 2, 1, i:i + 1], accum_out=stat[:, u % 2, 2, i:i + 1])
                act.activation(stat[:, u % 2, 3, :], stat[:, u % 2, 3, :], ACT.Exp).then_inc(exp_ready, 1)

            def probs_out(u):
                g, blk = UNITS[u]
                for kc in range(blk + 1):
                    c = att_piece[u] + kc
                    b = piece(c)
                    act.activation(p_t[blk][:, kc, :], b[:, :], ACT.Copy).then_inc(xb_done[c % 2], 1)

            def heads_hi(u):
                g, blk = UNITS[u]
                b = piece(out_piece[u])
                act.activation(a_hi[:, 2 * g:2 * g + 2, blk * P:(blk + 1) * P],
                               b[:, 0:2 * P].rearrange("p (k m) -> p k m", k=2), ACT.Copy).then_inc(xb_hi, 1)

            warm(ACT.Exp)
            exps(0)
            for u in range(8):
                if u:
                    heads_hi(u - 1)
                if u < 7:
                    exps(u + 1)
                probs_out(u)
                if u < KV - 1:
                    bias_in(u + 1)
            early_hi("wo")
            heads_hi(7)

            gemm("wo", None, (KD,))
            early_hi("ffn")
            norm(1, "norm1")

            def body(B):
                e = B.e
                for s in range(BODY):
                    if B.mixture or s >= EARLY["ffn"]:
                        split_hi(B.raw_no(s), B.spl + s, e, BODY, BODY)
                    if B.mixture and s == 2:
                        act.wait_ge(w_used, B.full(-1))
                        act.activation(yd_hi[:, :], acc[2][:, :], ACT.Copy).then_inc(yd_hi_ready, 1)
                    j, k = divmod(s, KD)
                    if 1 <= j <= FJ and k == 2:
                        act.wait_ge(w_used, B.full(j - 1))
                        for t in range(B.tiles):
                            act.activation(h[:, t, :], acc[B.pair(j - 1, t)[0]][:, 0:HALF], ACT.Silu).then_inc(gate_ready, 1)
                    for c, kind, *which in pieces_read_after(B.mixture, s):
                        c += B.pc
                        if kind == "h":
                            act.wait_ge(xb_full, c + 1 + rep(e, 16))
                            j, t = which
                            dst = (e_hi if B.mixture else h_hi)[:, 4 * j:4 * j + 4, t * P:(t + 1) * P]
                            act.activation(dst, xb[c % 2][:, :].rearrange("p (k m) -> p k m", k=4), ACT.Copy).then_inc(xb_hi, 1)
                        elif kind == "put":
                            act.wait_ge(xb_full, c + 1 + rep(e, 16))
                            act.activation(put[:, :, :], xb[c % 2][:, 0:T * P].rearrange("p (t m) -> p t m", t=T),
                                           ACT.Copy).then_inc(xb_done[c % 2], 1)
                        elif kind == "gather" and which[0] == 0:
                            act.wait_ge(xb_full, c + 1 + rep(e, 16))
                            q = which[1]
                            act.activation(g_hi[:, 4 * q:4 * q + 4, :], xb[c % 2][:, :].rearrange("p (k m) -> p k m", k=4),
                                           ACT.Copy).then_inc(xb_done[c % 2], 1)

            body(Body(False))
            early_hi("proj")
            norm(2, "norm2")

            def proj_out(gi, pr):
                g = PROJ_GROUPS[gi]
                for t in range(T):
                    n = pr + t
                    if g < 2:
                        act.activation(z_s[:, t, g * TW:(g + 1) * TW], acc[n % 3][:, :], ACT.Silu).then_inc(acc_done[n % 3], 1)
                    else:
                        act.activation(xbc[:, t, (g - 2) * TW:(g - 1) * TW], acc[n % 3][:, :], ACT.Copy).then_inc(acc_done[n % 3], 1)

            def mixer_steps(i):
                if i == DT_AT + LEAD:
                    act.wait_ge(dtv_ready, 1)
                    own(act.activation(dt_e[:, :, :], dt[:, :, :], ACT.Abs))
                    own(act.activation(dt_e[:, :, :], dt_e[:, :, :], ACT.Exp, scale=-1.0))
                    own(act.activation(dt_e[:, :, :], dt_e[:, :, :], ACT.Ln, bias=ones[:, 0:1]))
                    act.activation(srow[:, 1, :], srow[:, 1, :], ACT.Exp).then_inc(dte_ready, 1)
                for q in range(NCV):
                    if q < CBACK and i == conv_back_at(q) + LEAD:
                        c = cv_piece["b", q]
                        b = piece(c)
                        act.activation(xbc[:, :, 2 * P * q:2 * P * (q + 1)], b[:, :].rearrange("p (t m) -> p t m", t=T),
                                       ACT.Copy).then_inc(xb_done[c % 2], 1)
                for q in range(NCV):
                    if i == conv_in_at(q) + LEAD:
                        b = piece(cv_piece["f", q])
                        if q < 2:
                            act.wait_ge(u_ready, 1)
                        act.activation(u_pad[:, q % 2, :, TAPS - 1:TAPS - 1 + SEQ], b[:, :].rearrange("p (k m) -> p k m", k=2),
                                       ACT.Copy).then_inc(xb_done[cv_piece["f", q] % 2], 1)
                    if i == conv_in_at(q) + LEAD + 1:
                        act.wait_ge(cv_ready, q + 1)
                        dst = cv[:, q % 2] if q < 8 else (b_t if q < CBACK else c_t)[:, 2 * (q % 2):2 * (q % 2) + 2, :]
                        act.activation(dst, cv[:, q % 2], ACT.Silu).then_inc(cs_ready, 1)

            gemm("proj", proj_out, (KD,) * 5, mixer_steps)
            early_hi("wout")
            act.wait_ge(acs_ready, 1)
            act.activation(acs_e[:, :, :], acs[:, 0:T, :], ACT.Exp).then_inc(acse_ready, 1)
            act.activation(end_e[:, :, :], end_e[:, :, :], ACT.Exp).then_inc(acse_ready, 1)

            def y_square(u):
                c, g = SUNITS[u]
                act.wait_ge(y_ready, u + 1)
                act.wait_ge(yss_ready, u)
                act.activation(y_sq[:, :], xbc[:, c, 512 * g:512 * (g + 1)], ACT.Square, accum_out=yss[:, c, g:g + 1]).then_inc(yss_ready, 1)

            for u in range(8):
                act.wait_ge(d_ready, u + 1)
                own(act.activation(dec[:, u % 2, :], dec[:, u % 2, :], ACT.Relu))
                act.activation(dec[:, u % 2, :], dec[:, u % 2, :], ACT.Exp, scale=-1.0).then_inc(e_ready, 1)
                if u >= 2:
                    y_square(u - 2)
            warm(ACT.Sqrt)
            y_square(6)
            y_square(7)
            act.wait_ge(yms_ready, 1)
            act.activation(rs[:, :], ms[:, :], ACT.Sqrt).then_inc(yroot, 1)
            for n in range(8):
                c = pc0["ynorm"] + n
                b = piece(c)
                t, q = divmod(n, 4)
                act.activation(y_hi[:, 4 * q:4 * q + 4, t * P:(t + 1) * P], b[:, :].rearrange("p (k m) -> p k m", k=4),
                               ACT.Copy).then_inc(xb_hi, 1)
            gemm("wout", None, (2 * KD,))
            norm(3, "norm3")

            warm(ACT.Exp)
            act.wait_ge(tw_in, 1)
            act.activation(tw[:, :, 0], tw[:, :, 0], ACT.Exp).then_inc(tw_exp, 1)
            warm(ACT.Silu)

            def first_gather(rnd):
                for q in range(2):
                    c = pc0["moe"] + rnd * ROUND_PIECES + q
                    b = piece(c)
                    act.activation(g_hi[:, 4 * q:4 * q + 4, :], b[:, :].rearrange("p (k m) -> p k m", k=4),
                                   ACT.Copy).then_inc(xb_done[c % 2], 1)

            def experts(rnd):
                first_gather(rnd)
                with act.Fori(0, EXPERTS) as e:
                    body(Body(True, e, rnd))
                act.wait_ge(w_used, spl0["moe"] + (rnd + 1) * EXPERTS * BODY)
                act.activation(yd_hi[:, :], acc[2][:, :], ACT.Copy).then_inc(yd_hi_ready, 1)

            experts(0)
            most = act.value_load(flag[0:1, 0:1], min_val=0, max_val=SEQ)
            with act.If(most > overflow_at):
                experts(1)

        @block.vector
        def _(dve):
            steps = [0]

            def own(ins):
                steps[0] += 1
                ins.then_inc(dve_step, 1)
                dve.wait_ge(dve_step, steps[0])

            def split_lo(no, w, e=0):
                dve.wait_ge(hi_ready, w + 1 + rep(e, BODY))
                dve.tensor_tensor(w_lo[:, w % SPLIT, :], raw[:, no % RAW, :], r32(w_hi[:, w % SPLIT, :]), ALU.subtract).then_inc(raw_used, 1)

            def early_lo(stage):
                for i in range(EARLY[stage]):
                    split_lo(raw0[stage] + i, spl0[stage] + i)

            def ada_tile(no, k, buf):
                dve.wait_ge(raw_ready[no % RAW], 16 * (no // RAW + 1))
                if k == 0:
                    dve.tensor_scalar(ada[:, buf, :], raw[:, no % RAW, :], cond[:, 0:1], None, ALU.mult).then_inc(raw_used, 1)
                else:
                    dve.wait_ge(raw_used, no)
                    dve.scalar_tensor_tensor(ada[:, buf, :], raw[:, no % RAW, :], cond[:, k:k + 1], ada[:, buf, :],
                                             ALU.mult, ALU.add).then_inc(raw_used, 1)

            def ada_piece(c, n, pc):
                dve.wait_ge(xb_full, pc + 1)
                dve.wait_ge(ld_gain, 16 * 8)
                dst = mod[:, MOD_SLOT[1][c], n * HALF:(n + 1) * HALF]
                if IS_SCALE[c]:
                    dve.scalar_tensor_tensor(dst, xb[pc % 2][:, :], 1.0, dst, ALU.add, ALU.mult).then_inc(xb_done[pc % 2], 1)
                else:
                    dve.tensor_tensor(dst, xb[pc % 2][:, :], dst, ALU.add).then_inc(xb_done[pc % 2], 1)

            lows = [0]

            def piece_lo(c, dst, m=4):
                lows[0] += 1
                dve.wait_ge(xb_hi, lows[0])
                d_hi, d_lo = dst
                dve.tensor_tensor(d_lo, xb[c % 2][:, :].rearrange("p (k m) -> p k m", k=m), r32(d_hi), ALU.subtract).then_inc(xb_done[c % 2], 1)

            def norm_root(n):
                dve.wait_ge(ss_ready, T * (n + 1))
                dve.tensor_scalar(ms[:, :], ss[:, :], 1.0 / D, EPS, ALU.mult, ALU.add).then_inc(ms_ready, 1)
                dve.wait_ge(root_ready, n + 1)
                own(dve.reciprocal(rs[:, :], rs[:, :]))

            def norm(n, stage):
                if n:
                    dve.wait_ge(x_ready, T * n)
                layer, half = divmod(n, 2)
                sh, g = (mod[:, MOD_SLOT[layer][3 * half + q], :] for q in range(2))
                if n:
                    norm_root(n)

                def rows(t, hf):
                    cols = slice(hf * HALF, (hf + 1) * HALF)
                    own(dve.scalar_tensor_tensor(hm[:, t, cols], x[:, t, cols], rs[:, t:t + 1], g[:, cols], ALU.mult, ALU.mult))
                    dve.tensor_tensor(hm[:, t, cols], hm[:, t, cols], sh[:, cols], ALU.add).then_inc(hm_ready, 1)

                def turned_lo(m):
                    hf, t = divmod(m, T)
                    part = (slice(None), slice(4 * hf, 4 * hf + 4), slice(t * P, (t + 1) * P))
                    piece_lo(pc0[stage] + m, (a_hi[part], a_lo[part]))

                rows(0, 0)
                rows(1, 0)
                rows(0, 1)
                turned_lo(0)
                rows(1, 1)
                for m in range(1, 4):
                    turned_lo(m)
                if n == 3:
                    dve.wait_ge(hm_ready, 2 * T * (n + 1))
                    for t in range(T):
                        dve.wait_ge(t_hi_ready, t + 1)
                        dve.tensor_tensor(t_lo[:, t, :], hm[:, t, :], r32(t_hi[:, t, :]), ALU.subtract).then_inc(t_lo_ready, 1)

            def residual(stage, groups_before, gate):
                first = pr0[stage] + T * groups_before
                after = {"wo": "norm1", "ffn": "norm2", "wout": "norm3"}[stage]
                dve.wait_ge(w_used, spl0[after])
                for t in range(T):
                    n = first + t
                    dve.tensor_tensor(hm[:, t, :], acc[n % 3][:, :], gate, ALU.mult).then_inc(acc_done[n % 3], 1)
                    dve.wait_ge(acc_done[n % 3], n // 3 + 1)
                    dve.tensor_tensor(x[:, t, :], x[:, t, :], hm[:, t, :], ALU.add).then_inc(x_ready, 1)

            def gemm(stage, groups, after=None):
                for i in range(sum(groups)):
                    if i >= EARLY.get(stage, 0):
                        split_lo(raw0[stage] + i, spl0[stage] + i)
                    if after:
                        after(i)

            dve.memset(relb[BUCKETS:BUCKETS + 1, :], MASKED).then_inc(relb_set, 1)
            dve.wait_ge(ld_tab, 32)
            for o in range(2):
                dve.tensor_copy(relb[0:BUCKETS, :].rearrange("b (g o i) -> b g o i", o=2, i=2)[:, :, o, :],
                                rel_rows[:, :].rearrange("b (g i o) -> b g i o", o=2, i=2)[:, :, :, o]).then_inc(relb_set, 1)
            dve.wait_ge(cond_ready, 1)
            dve.wait_ge(cond_ready, 2)
            dve.tensor_tensor(cond_lo[:, :], cond[:, :], r32(cond_hi[:, :]), ALU.subtract).then_inc(cond_ready, 1)

            def ada_row(c):
                n = ada_pair(c)
                if c < 2:
                    dve.wait_ge(w_used, spl0["ada"] + (c + 1) * KD)
                else:
                    dve.wait_ge(ada_ready, c - 1)
                dst = mod[:, MOD_SLOT[0][c], :]
                if IS_SCALE[c]:
                    dve.wait_ge(ld_gain, 32)
                    dve.scalar_tensor_tensor(dst, acc[n % 3][:, :], 1.0, dst, ALU.add, ALU.mult).then_inc(acc_done[n % 3], 1)
                else:
                    dve.tensor_copy(dst, acc[n % 3][:, :]).then_inc(acc_done[n % 3], 1)

            def ada_rows_stand(*groups):
                for c in groups:
                    n = ada_pair(c)
                    dve.wait_ge(acc_done[n % 3], n // 3 + 1)

            norm_root(0)
            for i in range(2 * KD):
                split_lo(raw0["ada"] + i, spl0["ada"] + i)
                if i == KD + 1:
                    ada_row(0)
            early_lo("qkv")
            ada_row(1)
            ada_rows_stand(0, 1)
            norm(0, "norm0")
            gemm("qkv", (KD, KD // 2))

            dve.wait_ge(qkv_ready, 1)
            dve.wait_ge(ld_att, 48)
            for t in range(T):
                dve.wait_ge(qk_sq, t + 1)
                own(dve.reduce_sum(qk_ss[:, :], qk_square[:, :].rearrange("p (h d) -> p h d", d=HD), axis=AX.X))
                dve.tensor_scalar(qk_ss[:, :], qk_ss[:, :], 1.0 / HD, EPS, ALU.mult, ALU.add).then_inc(qk_ms, 1)
                dve.wait_ge(qk_root, t + 1)
                own(dve.reciprocal(qk_ss[:, :], qk_ss[:, :]))
                v = qkv[:, t, 0:NQK * HD].rearrange("p (h d) -> p h d", d=HD)
                own(dve.tensor_tensor(v, v, qk_ss[:, :].unsqueeze(2).to_broadcast([P, NQK, HD]), ALU.mult))
                dve.tensor_tensor(v[:, 0:HEADS, :], v[:, 0:HEADS, :],
                                  qk_gain[:, 0:1, :].to_broadcast([P, HEADS, HD]), ALU.mult).then_inc(qk_ready, 1)
                for twice in range(2):
                    dve.tensor_tensor(k2[:, t, :, twice, :], v[:, HEADS:NQK, :],
                                      qk_gain[:, 1:2, :].to_broadcast([P, KV, HD]), ALU.mult).then_inc(qk_ready, 1)

            def unit_scores(u):
                g, blk = UNITS[u]
                w = P * (blk + 1)
                n = score_pair(u)
                if blk == 0:
                    for c in (bias_piece[g], bias_piece[g] + 1):
                        dve.wait_ge(xb_done[c % 2], c // 2 + 1)
                dve.wait_ge(acc_full, u + 1)
                s3 = sc[:, u % 2, 0:GQ * w].rearrange("p (i m) -> p i m", i=GQ)
                sink = sinks[:, GQ * g:GQ * (g + 1)].rearrange("p (i o) -> p o i", o=2)
                top_, exit_ = (stat[:, u % 2, q, :].rearrange("p (o i) -> p o i", o=2) for q in (0, 3))
                for o in range(2):
                    own(dve.scalar_tensor_tensor(s3[:, 2 * o:2 * o + 2, :],
                                                 acc[n % 3][:, o * HALF:o * HALF + 2 * w].rearrange("p (i m) -> p i m", i=2), HD ** -0.5,
                                                 bias[:, GQ * g + 2 * o:GQ * g + 2 * o + 2, (1 - blk) * P:2 * P], ALU.mult, ALU.add))
                dve.sem_inc(acc_done[n % 3], 1)
                own(dve.reduce_max(stat[:, u % 2, 0, :], s3, axis=AX.X))
                own(dve.tensor_tensor(top_, top_, sink, ALU.max))
                own(dve.tensor_scalar(stat[:, u % 2, 1, :], stat[:, u % 2, 0, :], -1.0, None, ALU.mult))
                dve.tensor_tensor(exit_, sink, top_, ALU.subtract).then_inc(max_ready, 1)

            def unit_probs(u):
                g, blk = UNITS[u]
                w = P * (blk + 1)
                dve.wait_ge(exp_ready, u + 1)
                s3 = sc[:, u % 2, 0:GQ * w].rearrange("p (i m) -> p i m", i=GQ)
                total = stat[:, u % 2, 0, :]
                own(dve.tensor_tensor(total, stat[:, u % 2, 2, :], stat[:, u % 2, 3, :], ALU.add))
                own(dve.reciprocal(total, total))
                dve.tensor_tensor(s3, s3, total.unsqueeze(2).to_broadcast([P, GQ, w]), ALU.mult).then_inc(p_ready, 1)

            def heads_lo(u):
                g, blk = UNITS[u]
                c = out_piece[u]
                lows[0] += 1
                dve.wait_ge(xb_hi, lows[0])
                part = (slice(None), slice(2 * g, 2 * g + 2), slice(blk * P, (blk + 1) * P))
                dve.tensor_tensor(a_lo[part], xb[c % 2][:, 0:2 * P].rearrange("p (k m) -> p k m", k=2), r32(a_hi[part]),
                                  ALU.subtract).then_inc(xb_done[c % 2], 1)

            unit_scores(0)
            for u in range(8):
                if u < 7:
                    if u:
                        dve.wait_ge(xb_full, att_piece[u - 1] + UNITS[u - 1][1] + 1)
                    unit_scores(u + 1)
                unit_probs(u)
                if u:
                    heads_lo(u - 1)
                for i in range(PER_UNIT * u, PER_UNIT * (u + 1)):
                    c, k = divmod(i, KD)
                    ada_tile(raw0["attend"] + i, k, c % 2)
                if u >= 3 and u % 2:
                    ada_row((u + 1) // 2)
            early_lo("wo")
            heads_lo(7)

            gemm("wo", (KD,))
            ada_row(5)
            ada_rows_stand(2, 3, 4, 5)
            early_lo("ffn")
            residual("wo", 0, mod[:, MOD_SLOT[0][2], :])
            norm(1, "norm1")

            def body(B):
                e = B.e
                ada_n = 0
                for s in range(BODY):
                    if B.mixture or s >= EARLY["ffn"]:
                        split_lo(B.raw_no(s), B.spl + s, e)
                    if not B.mixture and ada_after(s):
                        c, k = divmod(ada_n, KD)
                        if k == 0 and c >= 2:
                            dve.wait_ge(ada_ready, 4 + c - 1)
                        ada_tile(B.raw_no(s) + 1, k, c % 2)
                        ada_n += 1
                    if B.mixture and s == 2:
                        dve.wait_ge(yd_hi_ready, B.rnd * (EXPERTS + 1) + 1 + rep(e, 1))
                        dve.tensor_tensor(yd_lo[:, :], acc[2][:, :], r32(yd_hi[:, :]), ALU.subtract).then_inc(acc_done[2], 1)
                    j, k = divmod(s, KD)
                    if 1 <= j <= FJ and k == 2:
                        for t in range(B.tiles):
                            q, _ = B.pair(j - 1, t)
                            dve.wait_ge(gate_ready, gates(B, j - 1, t))
                            dve.tensor_tensor(h[:, t, :], h[:, t, :], acc[q][:, HALF:2 * HALF], ALU.mult).then_inc(acc_done[q], 1)
                    if B.mixture and s == FJ * KD + 4:
                        build_pick(e + 1, B.rnd)
                    for c, kind, *which in pieces_read_after(B.mixture, s):
                        c += B.pc
                        if kind == "h":
                            j, t = which
                            part = (slice(None), slice(4 * j, 4 * j + 4), slice(t * P, (t + 1) * P))
                            d_hi, d_lo = (e_hi, e_lo) if B.mixture else (h_hi, h_lo)
                            dve.wait_ge(xb_hi, h_highs(B, j, t))
                            dve.tensor_tensor(d_lo[part], xb[c % 2][:, :].rearrange("p (k m) -> p k m", k=4), r32(d_hi[part]),
                                              ALU.subtract).then_inc(xb_done[c % 2], 1)
                        elif kind == "ada":
                            ada_piece(which[0], which[1], c)
                        elif kind == "scatter":
                            scatter_sum(c, which[0], which[1], e, e)
                        elif kind == "gather" and which[0] == 1:
                            dve.wait_ge(xb_full, c + 1 + rep(e, 16))
                            q = which[1]
                            dve.tensor_copy(g_lo[:, 4 * q:4 * q + 4, :], xb[c % 2][:, :].rearrange("p (k m) -> p k m", k=4)).then_inc(xb_done[c % 2], 1)

            def gates(B, j, t):
                if not B.mixture:
                    return T * j + t + 1
                return T * FJ + B.rnd * EXPERTS * FJ + j + 1 + rep(B.e, FJ)

            def h_highs(B, j, t):
                if not B.mixture:
                    return highs_ffn + T * j + t + 1
                return highs_moe + B.rnd * EXPERTS * FJ + j + 1 + rep(B.e, FJ)

            def build_pick(col, rnd):
                for t in range(T):
                    dve.tensor_scalar(pick[:, t, :], column, slot_of[:, t, bass.ds(col, 1)],
                                      None, ALU.is_equal).then_inc(pick_ready, 1)

            def scatter_sum(c, t, hf, col, e=0):
                dve.wait_ge(xb_full, c + 1 + rep(e, 16))
                dve.wait_ge(xb_done[c % 2], c // 2 + rep(e, 8))
                dst = y_sum[:, t, hf * HALF:(hf + 1) * HALF]
                dve.scalar_tensor_tensor(dst, xb[c % 2][:, :], comb[:, t, bass.ds(col, 1)], dst, ALU.mult, ALU.add).then_inc(xb_done[c % 2], 1)

            highs_ffn = lows[0]
            body(Body(False))
            lows[0] += T * FJ
            early_lo("proj")
            residual("ffn", FJ, mod[:, MOD_SLOT[0][5], :])
            norm(2, "norm2")
            dve.wait_ge(hm_ready, 6 * T)
            dve.sem_inc(norm_free, 1)

            def dt_sum():
                dve.wait_ge(ld_mix, 64)
                c = pc0["proj"]
                dve.wait_ge(xb_full, c + 1)
                own(dve.tensor_tensor(dt[:, :, :], xb[c % 2][:, 0:T * SH].rearrange("p (t m) -> p t m", t=T),
                                      srow[:, 0:1, :].to_broadcast([P, T, SH]), ALU.add))
                dve.sem_inc(xb_done[c % 2], 1)
                dve.sem_inc(dtv_ready, 1)

            def dt_parts():
                dve.wait_ge(dte_ready, 1)
                own(dve.scalar_tensor_tensor(dt[:, :, :], dt[:, :, :], 0.0, dt_e[:, :, :], ALU.max, ALU.add))
                dve.scalar_tensor_tensor(dt_a[:, :, :], dt[:, :, :], -1.0, srow[:, 1:2, :].to_broadcast([P, T, SH]),
                                         ALU.mult, ALU.mult).then_inc(dta_ready, 1)

            def run_sums():
                c = sums_piece
                dve.wait_ge(xb_full, c + 1)
                own(dve.tensor_copy(acs[:, :, :], xb[c % 2][:, 0:2 * T * SH].rearrange("p (t m) -> p t m", t=2 * T)))
                dve.sem_inc(xb_done[c % 2], 1)
                own(dve.tensor_tensor(end_e[:, :, :], acs[:, T:2 * T, :], acs[:, 0:T, :], ALU.subtract))
                dve.sem_inc(acs_ready, 1)

            def convolve(q):
                c = cv_piece["f", q]
                dve.wait_ge(xb_done[c % 2], c // 2 + 1)
                if q >= 2:
                    dve.wait_ge(cs_ready, q - 1)
                    if q - 2 < 8:
                        dve.wait_ge(xb_full, cv_piece["b", q - 2] + 1)
                for tap in range(TAPS):
                    for m in range(2):
                        k = 2 * q + m
                        src = u_pad[:, q % 2, m, tap:tap + SEQ]
                        wt = vecs[:, KD + tap * CH + k:KD + tap * CH + k + 1]
                        if tap == 0:
                            ins = dve.tensor_scalar(cv[:, q % 2, m, :], src, wt, vecs[:, KD + TAPS * CH + k:KD + TAPS * CH + k + 1],
                                                    ALU.mult, ALU.add)
                        else:
                            ins = dve.scalar_tensor_tensor(cv[:, q % 2, m, :], src, wt, cv[:, q % 2, m, :], ALU.mult, ALU.add)
                        steps[0] += 1
                        ins.then_inc(dve_step, 1)
                        if tap or m:
                            dve.wait_ge(dve_step, steps[0] - 1)
                dve.wait_ge(dve_step, steps[0])
                dve.sem_inc(cv_ready, 1)

            def mixer_steps(i):
                if i == DT_AT + LEAD:
                    dt_sum()
                if i == DT_AT + LEAD + 2:
                    dt_parts()
                if i == SUMS_AT + LEAD:
                    run_sums()
                for q in range(NCV):
                    if i == conv_in_at(q) + LEAD:
                        convolve(q)

            own(dve.memset(u_pad[:, :, :, 0:TAPS - 1], 0.0))
            dve.sem_inc(u_ready, 1)
            gemm("proj", (KD,) * 5, mixer_steps)
            early_lo("wout")
            dve.wait_ge(acse_ready, 2)
            for q in range(3):
                dve.wait_ge(acc_done[q], len([m for m in range(pr0["ssd"]) if m % 3 == q]))
            for q in range(2):
                dve.wait_ge(xb_done[q], (pc0["ssd"] + 1 - q) // 2)

            def heads_of(row_, g):
                return row_[:, HG * g:HG * (g + 1)].unsqueeze(2)

            def unit_in(u):
                c, g = SUNITS[u]
                n = ssd_pair["a", u]
                dve.wait_ge(acc_full, full_no(n))
                d3 = dec[:, u % 2, :].rearrange("p (h m) -> p h m", h=HG)
                own(dve.tensor_tensor(d3, heads_of(acs[:, c, :], g).to_broadcast([P, HG, P]),
                                      acc[n % 3][:, :].rearrange("p (h m) -> p h m", h=HG), ALU.subtract))
                dve.sem_inc(acc_done[n % 3], 1)
                dve.sem_inc(d_ready, 1)
                xs3 = xbc[:, c, 512 * g:512 * (g + 1)].rearrange("p (h m) -> p h m", h=HG)
                xd3 = xd[:, u % 2, :].rearrange("p (h m) -> p h m", h=HG)
                own(dve.tensor_tensor(xd3, xs3, heads_of(dt[:, c, :], g).to_broadcast([P, HG, SHD]), ALU.mult))

            def unit_mid(u):
                c, g = SUNITS[u]
                pc = pc0["ssd"] + u
                dve.wait_ge(xb_full, pc + 1)
                if c == 0:
                    own(dve.tensor_tensor(xde[:, u % 2, :].rearrange("p (h m) -> p h m", h=HG), xd[:, u % 2, :].rearrange("p (h m) -> p h m", h=HG),
                                          heads_of(end_e[:, 0, :], g).to_broadcast([P, HG, SHD]), ALU.mult))
                own(dve.tensor_tensor(cbm[:, :], xb[pc % 2][:, 0:P], tri, ALU.mult))
                dve.sem_inc(xb_done[pc % 2], 1)
                dve.wait_ge(e_ready, u + 1)
                d3 = dec[:, u % 2, :].rearrange("p (h m) -> p h m", h=HG)
                dve.tensor_tensor(d3, d3, cbm[:, :].unsqueeze(1).to_broadcast([P, HG, P]), ALU.mult).then_inc(mt_ready, 1)

            def unit_out(u):
                c, g = SUNITS[u]
                n = ssd_pair["y", u]
                y = xbc[:, c, 512 * g:512 * (g + 1)]
                y3 = y.rearrange("p (h m) -> p h m", h=HG)
                own(dve.tensor_tensor(y3, y3, heads_of(srow[:, 2, :], g).to_broadcast([P, HG, SHD]), ALU.mult))
                dve.wait_ge(acc_full, full_no(n))
                if c == 0:
                    dve.tensor_copy(state[:, g, :], acc[n % 3][:, HALF:2 * HALF])
                else:
                    own(dve.tensor_tensor(y_tmp[:, :].rearrange("p (h m) -> p h m", h=HG),
                                          acc[n % 3][:, HALF:2 * HALF].rearrange("p (h m) -> p h m", h=HG),
                                          heads_of(acs_e[:, c, :], g).to_broadcast([P, HG, SHD]), ALU.mult))
                    own(dve.tensor_tensor(y, y, y_tmp[:, :], ALU.add))
                own(dve.tensor_tensor(y, y, acc[n % 3][:, 0:HALF], ALU.add))
                dve.sem_inc(acc_done[n % 3], 1)
                dve.tensor_tensor(y, y, z_s[:, c, 512 * g:512 * (g + 1)], ALU.mult).then_inc(y_ready, 1)

            unit_in(0)
            unit_in(1)
            unit_mid(0)
            for u in range(8):
                if u < 7:
                    unit_mid(u + 1)
                unit_out(u)
                if u < 6:
                    unit_in(u + 2)
            dve.wait_ge(yss_ready, 8)
            own(dve.reduce_sum(ss[:, :], yss[:, :, :], axis=AX.X))
            dve.tensor_scalar(ms[:, :], ss[:, :], 1.0 / DI, EPS, ALU.mult, ALU.add).then_inc(yms_ready, 1)
            dve.wait_ge(yroot, 1)
            own(dve.reciprocal(rs[:, :], rs[:, :]))
            dve.wait_ge(ld_norm, 16)
            for t in range(T):
                dve.scalar_tensor_tensor(xbc[:, t, 0:DI], xbc[:, t, 0:DI], rs[:, t:t + 1],
                                         mod[:, 0:2, :].rearrange("p a n -> p (a n)"), ALU.mult, ALU.mult).then_inc(yn_ready, 1)
            for n in range(8):
                t, q = divmod(n, 4)
                part = (slice(None), slice(4 * q, 4 * q + 4), slice(t * P, (t + 1) * P))
                piece_lo(pc0["ynorm"] + n, (y_hi[part], y_lo[part]))
            gemm("wout", (2 * KD,))
            residual("wout", 0, mod[:, MOD_SLOT[1][2], :])
            norm(3, "norm3")

            dve.wait_ge(xb_full, pc0["route"] + 1)
            b = xb[pc0["route"] % 2]
            own(dve.tensor_copy(lg[:, :, :], b[:, 0:T * EXPERTS].rearrange("p (t m) -> p t m", t=T)))
            dve.sem_inc(xb_done[pc0["route"] % 2], 1)
            for t in range(T):
                own(dve.max(mx[:, t, :], lg[:, t, :]))
                own(dve.max_index(mi[:, t, :], mx[:, t, :], lg[:, t, :]))
            own(dve.tensor_copy(mif[:, :, :], mi[:, :, :]))
            own(dve.tensor_tensor(tw[:, :, 0], mx[:, :, 1], mx[:, :, 0], ALU.subtract))
            dve.sem_inc(tw_in, 1)
            own(dve.memset(comb[:, :, :], 0.0))
            own(dve.memset(slot_of[:, :, :], -1.0))
            for t in range(T):
                for q in range(2):
                    own(dve.tensor_scalar(oh[:, t, q, :], column[:, 0:EXPERTS], mif[:, t, q:q + 1], None, ALU.is_equal))
                own(dve.tensor_tensor(msk[:, t, :], oh[:, t, 0, :], oh[:, t, 1, :], ALU.add))
            dve.sem_inc(mask_ready, 1)
            dve.wait_ge(tw_exp, 1)
            own(dve.tensor_scalar(tw[:, :, 1], tw[:, :, 0], 1.0, None, ALU.add))
            own(dve.reciprocal(tw[:, :, 1], tw[:, :, 1]))
            own(dve.tensor_tensor(tw[:, :, 2], tw[:, :, 0], tw[:, :, 1], ALU.mult))
            for t in range(T):
                own(dve.tensor_scalar(comb[:, t, 1:1 + EXPERTS], oh[:, t, 0, :], tw[:, t, 1:2], None, ALU.mult))
                own(dve.scalar_tensor_tensor(comb[:, t, 1:1 + EXPERTS], oh[:, t, 1, :], tw[:, t, 2:3], comb[:, t, 1:1 + EXPERTS],
                                             ALU.mult, ALU.add))
            c = pc0["route"] + 1
            dve.wait_ge(xb_full, c + 1)
            b = xb[c % 2]
            for t in range(T):
                own(dve.scalar_tensor_tensor(slot_of[:, t, 0:EXPERTS], b[:, t * EXPERTS:(t + 1) * EXPERTS], 1.0, msk[:, t, :],
                                             ALU.add, ALU.mult))
                own(dve.tensor_scalar(slot_of[:, t, 0:EXPERTS], slot_of[:, t, 0:EXPERTS], -1.0, None, ALU.add))
            own(dve.reduce_max(cmax[:, :], b[:, 2 * EXPERTS:3 * EXPERTS], axis=AX.X))
            dve.sem_inc(xb_done[c % 2], 1)
            own(dve.tensor_copy(flag[:, :], cmax[0:1, :]))
            own(dve.memset(y_sum[:, :, :], 0.0))
            own(dve.memset(r32(put[:, :, :]), 0.0))
            own(dve.memset(acc[2][:, :], 0.0))
            dve.sem_inc(route_ready, 1)

            highs_moe = lows[0]

            def experts(rnd):
                if rnd:
                    for q in range(2):
                        dve.wait_ge(xb_done[q], (pc0["moe"] + ROUND_PIECES + 1 - q) // 2)
                    own(dve.tensor_scalar(slot_of[:, :, :], slot_of[:, :, :], -float(P), None, ALU.add))
                    own(dve.memset(r32(put[:, :, :]), 0.0))
                    dve.sem_inc(route_ready, 1)
                build_pick(0, rnd)
                for q in range(2):
                    c = pc0["moe"] + rnd * ROUND_PIECES + 2 + q
                    dve.wait_ge(xb_full, c + 1)
                    dve.tensor_copy(g_lo[:, 4 * q:4 * q + 4, :], xb[c % 2][:, :].rearrange("p (k m) -> p k m", k=4)).then_inc(xb_done[c % 2], 1)
                with dve.Fori(0, EXPERTS) as e:
                    body(Body(True, e, rnd))
                dve.wait_ge(yd_hi_ready, (rnd + 1) * (EXPERTS + 1))
                dve.tensor_tensor(yd_lo[:, :], acc[2][:, :], r32(yd_hi[:, :]), ALU.subtract).then_inc(yd_lo_ready, 1)
                for n in range(4):
                    scatter_sum(pc0["moe"] + rnd * ROUND_PIECES + 4 + 16 * EXPERTS + n, n // 2, n % 2, EXPERTS)

            experts(0)
            most = dve.value_load(flag[0:1, 0:1], min_val=0, max_val=SEQ)
            with dve.If(most > overflow_at):
                experts(1)
            for q in range(2):
                dve.wait_ge(xb_done[q], (pc0["moe"] + ROUND_PIECES + 1 - q) // 2)
            for t in range(T):
                dve.tensor_tensor(y_sum[:, t, :], y_sum[:, t, :], mod[:, MOD_SLOT[1][5], :], ALU.mult).then_inc(final_step, 1)
                dve.wait_ge(final_step, 2 * t + 1)
                dve.tensor_tensor(x[:, t, :], x[:, t, :], y_sum[:, t, :], ALU.add).then_inc(final_step, 1)
            dve.wait_ge(final_step, 2 * T)
            dve.sem_inc(x_ready, 1)

        @block.tensor
        def _(pe):
            def open_piece(c, e=0, per=0):
                if c >= 2:
                    pe.wait_ge(xb_done[c % 2], c // 2 + rep(e, per // 2))
                return xb[c % 2]

            def open_pair(q, used):
                if not isinstance(used, int) or used:
                    pe.wait_ge(acc_done[q], used)
                return acc[q]

            def weight_tile(w, parts, pairs, lhs, tiles, first, last, e=0, no=0):
                l_hi, l_lo = lhs
                hi, lo = w_hi[:, w % SPLIT, :], w_lo[:, w % SPLIT, :]
                pe.wait_ge(hi_ready, w + 1 + rep(e, BODY))
                for t in range(tiles):
                    if first:
                        open_pair(*pairs[t])
                    for m, (k, to, col) in enumerate(parts):
                        o = acc[pairs[t][0]][:, to:to + HALF]
                        new = first and (m == 0 or parts[m][1] != parts[m - 1][1])
                        pe.matmul(o, l_hi[:, k, t * P:(t + 1) * P], hi[:, col:col + HALF], start=new, stop=False)
                        pe.matmul(o, l_lo[:, k, t * P:(t + 1) * P], hi[:, col:col + HALF], start=False, stop=False)
                pe.wait_ge(raw_used, no + 1 + rep(e, BODY))
                for t in range(tiles):
                    for m, (k, to, col) in enumerate(parts):
                        o = acc[pairs[t][0]][:, to:to + HALF]
                        end = last and (m == len(parts) - 1 or parts[m][1] != parts[m + 1][1])
                        mm = pe.matmul(o, l_hi[:, k, t * P:(t + 1) * P], lo[:, col:col + HALF], start=False, stop=end)
                mm.then_inc(w_used, 1)

            def gemm(stage, groups, lhs, after=None, rows_of=None):
                i = 0
                for gi, tiles in enumerate(groups):
                    pr = pr0[stage] + T * gi
                    pairs = [((pr + t) % 3, (pr + t) // 3) for t in range(T)]
                    for n, parts in enumerate(tiles):
                        if rows_of and i == KD // 2:
                            turned(rows_of, 1)
                        weight_tile(spl0[stage] + i, parts, pairs, lhs, T, n == 0, n == len(tiles) - 1, no=raw0[stage] + i)
                        if after:
                            after(i)
                        i += 1

            def wide(k):
                return [(k, 0, 0), (k, HALF, HALF)]

            def turn(c, src, n):
                b = open_piece(c)
                for m in range(n):
                    mm = pe.transpose(b[:, m * P:(m + 1) * P], src(m), ident)
                mm.then_inc(xb_full, 1)

            def norm(n, stage):
                for hf in range(2):
                    for t in range(T):
                        m = T * hf + t
                        pe.wait_ge(hm_ready, 2 * T * n + m + 1)
                        turn(pc0[stage] + m, lambda m: hm[:, t, (4 * hf + m) * P:(4 * hf + m + 1) * P], 4)
                turned(stage, 0)

            def turned(stage, hf):
                for c in range(pc0[stage] + T * hf, pc0[stage] + T * (hf + 1)):
                    pe.wait_ge(xb_done[c % 2], c // 2 + 1)

            def pieces_on(q, c):
                return (c + 1 - q) // 2

            pe.wait_ge(ld_square, 32)
            pe.wait_ge(ld_vecs, 48)
            pe.transpose(xb[0][:, 0:P], vec_rows[:, :], ident).then_inc(xb_full, 1)
            pe.wait_ge(relb_set, 3)
            pe.wait_ge(ld_tab, 32)
            pe.matmul(xb[1][0:HEADS, 0:3 * P], relb[:, :], table[:, :], start=True, stop=True).then_inc(xb_full, 1)
            pe.wait_ge(ld_rows, 16)

            def one_ada(c, n, pc):
                b = open_piece(pc)
                cols = slice(n * HALF, (n + 1) * HALF)
                if IS_SCALE[c]:
                    pe.matmul(b[:, :], ident[0:12, 6 + c:7 + c].to_broadcast([12, P]), bias_rows[:, cols], start=True, stop=False)
                pe.matmul(b[:, :], ones, ada[:, c % 2, cols], start=not IS_SCALE[c], stop=True).then_inc(xb_full, 1)
                if n == 1:
                    pe.wait_ge(xb_full, pc + 1)
                    pe.sem_inc(ada_ready, 1)

            HALVES = (slice(0, HALF), slice(HALF, 2 * HALF))

            def ada_bias(c):
                pair = ada_pair(c)
                open_pair(pair % 3, pair // 3)
                for cols in HALVES:
                    pe.matmul(acc[pair % 3][:, cols], ident[0:12, c:c + 1].to_broadcast([12, P]), bias_rows[:, cols],
                              start=True, stop=False)

            def ada_sum(c):
                ada_bias(c)
                pe.wait_ge(raw_used, raw0["attend"] + (c - 1) * KD)
                for cols in HALVES:
                    mm = pe.matmul(acc[ada_pair(c) % 3][:, cols], ones, ada[:, c % 2, cols], start=False, stop=True)
                mm.then_inc(ada_ready, 1)

            def ada_tiles():
                for i in range(2 * KD):
                    c, k = divmod(i, KD)
                    no, w, pair = raw0["ada"] + i, spl0["ada"] + i, ada_pair(c)
                    if k == 0:
                        ada_bias(c)
                    pe.wait_ge(hi_ready, w + 1)
                    halves = [(acc[pair % 3][:, cols], w_hi[:, w % SPLIT, cols], w_lo[:, w % SPLIT, cols])
                              for cols in HALVES]
                    for part in (cond_hi, cond_lo):
                        for o, hi, lo in halves:
                            pe.matmul(o, part[:, k:k + 1].to_broadcast([P, P]), hi, start=False, stop=False)
                    pe.wait_ge(raw_used, no + 1)
                    for o, hi, lo in halves:
                        mm = pe.matmul(o, cond_hi[:, k:k + 1].to_broadcast([P, P]), lo, start=False, stop=k == KD - 1)
                    mm.then_inc(w_used, 1)

            pe.wait_ge(cond_ready, 3)
            ada_tiles()
            norm(0, "norm0")
            gemm("qkv", [[wide(k) for k in range(KD)], [[(k, 0, 0), (k + 1, 0, HALF)] for k in range(0, KD, 2)]], (a_hi, a_lo), rows_of="norm0")
            def bias_turn(g):
                for m in range(2):
                    pe.matmul(open_piece(bias_piece[g] + m)[:, :], reversal,
                              bias_rev[:, BIAS_PLACE[g], 2 * m:2 * m + 2, :].rearrange("p k m -> p (k m)"),
                              start=True, stop=True).then_inc(xb_full, 1)

            for t in range(T):
                pe.wait_ge(qk_ready, 3 * t + 3)
                for part in range(2):
                    turn(turn_piece(t, part), lambda m: qkv[:, t, (4 * part + m) * P:(4 * part + m + 1) * P], 4)
                turn(turn_piece(t, 2), lambda m: k2[:, t, m].rearrange("p a d -> p (a d)"), 4)
                if t == 0:
                    pe.wait_ge(ld_bias, 16 * KV)
                    bias_turn(0)
            for q in range(2):
                pe.wait_ge(xb_done[q], pieces_on(q, pc0["attend"]))

            def scores(u):
                g, blk = UNITS[u]
                w = P * (blk + 1)
                n = score_pair(u)
                o = open_pair(n % 3, n // 3)
                for i in range(GQ):
                    hh = HD * (i % 2)
                    at_ = HALF * (i % 2) + w * (i // 2)
                    mm = pe.matmul(o[:, at_:at_ + w], q_t[hh:hh + HD, (GQ * g + i) // 2, blk * P:(blk + 1) * P],
                                   k_t[hh:hh + HD, g, 0:w], start=True, stop=True)
                mm.then_inc(acc_full, 1)

            def turn_probs(u):
                g, blk = UNITS[u]
                w = P * (blk + 1)
                pe.wait_ge(p_ready, u + 1)
                for kc in range(blk + 1):
                    turn(att_piece[u] + kc, lambda m: sc[:, u % 2, m * w + kc * P:m * w + (kc + 1) * P], GQ)

            def attend(u):
                g, blk = UNITS[u]
                for kc in range(blk + 1):
                    c = att_piece[u] + kc
                    pe.wait_ge(xb_done[c % 2], c // 2 + 1)
                o = open_piece(out_piece[u])
                for odd in range(2):
                    for kc in range(blk + 1):
                        probs = p_t[blk][:, kc, 2 * P * odd:2 * P * (odd + 1)].rearrange("p (i m) -> p i m", i=2)
                        mm = pe.matmul(o[HD * odd:HD * (odd + 1), 0:2 * P].rearrange("p (i m) -> p i m", i=2),
                                       qkv[:, kc, D + KV * HD + g * HD:D + KV * HD + (g + 1) * HD], probs,
                                       start=kc == 0, stop=kc == blk)
                mm.then_inc(xb_full, 1)

            scores(0)
            scores(1)
            for u in range(8):
                if u:
                    attend(u - 1)
                    if u < 7:
                        scores(u + 1)
                turn_probs(u)
                if u < KV - 1:
                    bias_turn(u + 1)
                if u and u % 2 == 0:
                    ada_sum(1 + u // 2)
            attend(7)
            ada_sum(5)
            for q in range(2):
                pe.wait_ge(xb_done[q], pieces_on(q, pc0["wo"]))
            gemm("wo", [[wide(k) for k in range(KD)]], (a_hi, a_lo))
            norm(1, "norm1")

            def body(B):
                e = B.e
                per = 16 if B.mixture else 0
                gu = (g_hi, g_lo) if B.mixture else (a_hi, a_lo)
                hid = (e_hi, e_lo) if B.mixture else (h_hi, h_lo)
                for s in range(BODY):
                    if s < FJ * KD:
                        j, k = divmod(s, KD)
                        first, last, lhs = k == 0, k == KD - 1, gu
                    else:
                        j, k = FJ, s - FJ * KD
                        first, last, lhs = k == 0, k == FK - 1, hid
                        if k % 4 == 0:
                            for c, *what in [w for v in PIECES[B.mixture].values() for w in v]:
                                if what[0] == "h" and what[1] == k // 4:
                                    c += B.pc
                                    pe.wait_ge(xb_done[c % 2], c // 2 + 1 + rep(e, per // 2))
                    if B.mixture and s == 0:
                        for c in (B.pc - 2, B.pc - 1):
                            pe.wait_ge(xb_done[c % 2], c // 2 + 1 + rep(e, per // 2))
                    if not B.mixture and s == KD // 2:
                        turned("norm1", 1)
                    if B.mixture and first and j == FJ:
                        pairs = [(2, B.pair(FJ, 0)[1] + 1)]
                    else:
                        pairs = [B.pair(j, t) for t in range(B.tiles)]
                    weight_tile(B.spl + s, wide(k), pairs, lhs, B.tiles, first, last, e, B.raw_no(s))
                    for c, kind, *which in PIECES[B.mixture].get(s, []):
                        c += B.pc
                        if kind == "h":
                            j, t = which
                            q, used = B.pair(j, t)
                            pe.wait_ge(acc_done[q], used + 1)
                            b = open_piece(c, e, per)
                            for m in range(4):
                                mm = pe.transpose(b[:, m * P:(m + 1) * P], h[:, t, m * P:(m + 1) * P], ident)
                            mm.then_inc(xb_full, 1)
                        elif kind == "ada":
                            cc, n = which
                            if n == 0:
                                pe.wait_ge(raw_used, ada_group_end[cc])
                            one_ada(cc, n, c)
                        elif kind == "scatter":
                            t, hf = which
                            pe.wait_ge(acc_done[2], B.pair(FJ, 0)[1] + 1)
                            scatter(c, t, hf, e, per)
                        elif kind == "put":
                            b = open_piece(c, e, per)
                            for t in range(T):
                                mm = pe.transpose(b[:, t * P:(t + 1) * P], r32(pick[:, t, :]), ident)
                            mm.then_inc(xb_full, 1)
                        elif kind == "gather":
                            gather(c, which[0], which[1], e, per, B.rnd)

            def scatter(c, t, hf, e, per):
                b = open_piece(c, e, per)
                cols = slice(hf * HALF, (hf + 1) * HALF)
                pe.matmul(b[:, :], put[:, t, :], yd_hi[:, cols], start=True, stop=False)
                pe.matmul(b[:, :], put[:, t, :], yd_lo[:, cols], start=False, stop=True).then_inc(xb_full, 1)

            def gather(c, low, hf, e, per, rnd):
                if low == 0 and hf == 0:
                    pe.wait_ge(pick_ready, rnd * T * (EXPERTS + 1) + T + rep(e, T) + (T if per else 0))
                b = open_piece(c, e, per)
                src = t_lo if low else t_hi
                for m in range(4):
                    for t in range(T):
                        mm = pe.matmul(b[:, m * P:(m + 1) * P], src[:, t, (4 * hf + m) * P:(4 * hf + m + 1) * P], pick[:, t, :],
                                       start=t == 0, stop=t == T - 1)
                mm.then_inc(xb_full, 1)

            ada_group_end, n = {}, 0
            for s in range(BODY):
                if ada_after(s):
                    n += 1
                    if n % KD == 0:
                        ada_group_end[n // KD - 1] = Body(False).raw_no(s) + 2
            body(Body(False))
            norm(2, "norm2")

            def dt_product():
                pe.wait_ge(ld_mix, 64)
                b = open_piece(pc0["proj"])
                for t in range(T):
                    for k in range(KD):
                        for src in (a_hi, a_lo):
                            mm = pe.matmul(b[:, t * SH:(t + 1) * SH], r32(src[:, k, t * P:(t + 1) * P]), w_dt[:, k, :],
                                           start=k == 0 and src is a_hi, stop=k == KD - 1 and src is a_lo)
                mm.then_inc(xb_full, 1)

            def run_sums():
                pe.wait_ge(dta_ready, 1)
                b = open_piece(sums_piece)
                for n in range(2 * T):
                    mm = pe.matmul(b[:, n * SH:(n + 1) * SH], tri if n < T else ones, dt_a[:, n % T, :], start=True, stop=True)
                mm.then_inc(xb_full, 1)

            def mixer_steps(i):
                if i == DT_AT:
                    dt_product()
                if i == SUMS_AT:
                    run_sums()
                for q in range(CBACK):
                    if i == conv_back_at(q):
                        pe.wait_ge(cs_ready, q + 1)
                        if q < 8:
                            turn(cv_piece["b", q], lambda m: cv[:, q % 2, m % 2, (m // 2) * P:(m // 2 + 1) * P], 4)
                        else:
                            turn(cv_piece["b", q], lambda m: b_t[:, 2 * (q % 2) + m % 2, (m // 2) * P:(m // 2 + 1) * P], 4)
                for q in range(NCV):
                    if i == conv_in_at(q):
                        for n in range(pr0["proj"] + T * (q // 4), pr0["proj"] + T * (q // 4 + 1)):
                            pe.wait_ge(acc_done[n % 3], n // 3 + 1)
                        turn(cv_piece["f", q], lambda m: xbc[:, m % 2, (2 * q + m // 2) * P:(2 * q + m // 2 + 1) * P], 4)

            gemm("proj", [[wide(k) for k in range(KD)]] * 5, (a_hi, a_lo), mixer_steps, "norm2")
            pe.wait_ge(cs_ready, NCV)

            def unit_in(u):
                c, g = SUNITS[u]
                n = ssd_pair["a", u]
                o = open_pair(n % 3, n // 3)
                for i in range(HG):
                    mm = pe.matmul(o[:, i * P:(i + 1) * P], dt_a[:, c, HG * g + i:HG * g + i + 1].to_broadcast([P, P]), tri,
                                   start=True, stop=True)
                mm.then_inc(acc_full, 1)
                pc = pc0["ssd"] + u
                b = open_piece(pc)
                pe.matmul(b[:, 0:P], b_t[:, g, c * P:(c + 1) * P], c_t[:, g, c * P:(c + 1) * P], start=True, stop=True).then_inc(xb_full, 1)

            def unit_out(u):
                c, g = SUNITS[u]
                n = ssd_pair["y", u]
                pe.wait_ge(mt_ready, u + 1)
                o = open_pair(n % 3, n // 3)
                if c == 0:
                    pe.matmul(o[:, HALF:2 * HALF], xbc[:, c, DI + g * NS:DI + (g + 1) * NS], xde[:, u % 2, :], start=True, stop=True)
                else:
                    pe.matmul(o[:, HALF:2 * HALF], c_t[:, g, c * P:(c + 1) * P], state[:, g, :], start=True, stop=True)
                for i in range(HG):
                    mm = pe.matmul(o[:, i * SHD:(i + 1) * SHD], dec[:, u % 2, i * P:(i + 1) * P],
                                   xd[:, u % 2, i * SHD:(i + 1) * SHD], start=True, stop=True)
                mm.then_inc(acc_full, 1)

            unit_in(0)
            unit_in(1)
            for u in range(8):
                unit_out(u)
                if u < 6:
                    unit_in(u + 2)
            for n in range(8):
                t, q = divmod(n, 4)
                pe.wait_ge(yn_ready, t + 1)
                turn(pc0["ynorm"] + n, lambda m: xbc[:, t, (4 * q + m) * P:(4 * q + m + 1) * P], 4)
            for q in range(2):
                pe.wait_ge(xb_done[q], pieces_on(q, pc0["wout"]))
            gemm("wout", [[wide(k) for k in range(2 * KD)]], (y_hi, y_lo))
            norm(3, "norm3")

            pe.wait_ge(ld_router, 16)
            turned("norm3", 1)
            b = open_piece(pc0["route"])
            for t in range(T):
                for k in range(KD):
                    for src in (a_hi, a_lo):
                        mm = pe.matmul(b[:, t * EXPERTS:(t + 1) * EXPERTS], r32(src[:, k, t * P:(t + 1) * P]), w_r[:, k, :],
                                       start=k == 0 and src is a_hi, stop=k == KD - 1 and src is a_lo)
            mm.then_inc(xb_full, 1)
            pe.wait_ge(mask_ready, 1)
            b = open_piece(pc0["route"] + 1)
            pe.matmul(b[:, 0:EXPERTS], tri_strict, msk[:, 0, :], start=True, stop=True)
            pe.matmul(b[:, EXPERTS:2 * EXPERTS], tri_strict, msk[:, 1, :], start=True, stop=False)
            pe.matmul(b[:, EXPERTS:2 * EXPERTS], ones, msk[:, 0, :], start=False, stop=True)
            pe.matmul(b[:, 2 * EXPERTS:3 * EXPERTS], ones, msk[:, 0, :], start=True, stop=False)
            pe.matmul(b[:, 2 * EXPERTS:3 * EXPERTS], ones, msk[:, 1, :], start=False, stop=True).then_inc(xb_full, 1)

            def experts(rnd):
                pe.wait_ge(route_ready, rnd + 1)
                pe.wait_ge(t_lo_ready, T)
                for n in range(4):
                    gather(pc0["moe"] + rnd * ROUND_PIECES + n, n // 2, n % 2, 0, 0, rnd)
                with pe.Fori(0, EXPERTS) as e:
                    body(Body(True, e, rnd))
                pe.wait_ge(yd_lo_ready, rnd + 1)
                for n in range(4):
                    scatter(pc0["moe"] + rnd * ROUND_PIECES + 4 + 16 * EXPERTS + n, n // 2, n % 2, 0, 0)

            experts(0)
            most = pe.value_load(flag[0:1, 0:1], min_val=0, max_val=SEQ)
            with pe.If(most > overflow_at):
                experts(1)


_INS = ["x", "c", "ada_w", "ada_b", "norm_gain", "rel_bias", "attn_w_qkv", "attn_q_gain", "attn_k_gain",
        "attn_sinks", "attn_w_o", "ssm_w_in", "ssm_conv_w", "ssm_conv_b", "ssm_dt_bias", "ssm_a_log",
        "ssm_d", "ssm_norm_w", "ssm_w_out", "ffn_w_gu", "ffn_w_down", "moe_w_router", "moe_w_gu", "moe_w_down"]


def kernel(**inputs):
    import concourse.bacc as bacc
    from concourse.bass_utils import run_bass_kernel_spmd

    nc = bacc.Bacc("TRN2", target_bir_lowering=False, num_devices=1)
    f32 = mybir.dt.float32
    arrays = {name: np.ascontiguousarray(inputs[name]) for name in _INS}
    arrays["square"], arrays["table"] = shape_constants()
    A = {name: nc.dram_tensor(f"in_{name}", a.shape, f32, kind="ExternalInput").ap() for name, a in arrays.items()}
    out = nc.dram_tensor("out", (1, SEQ, D), f32, kind="ExternalOutput").ap()
    build(nc, A, out, A["square"], A["table"])
    r = run_bass_kernel_spmd(nc, [{f"in_{name}": a for name, a in arrays.items()}], core_ids=[0])
    return r.results[0]["out"]
```

```python
import math

import numpy as np
import concourse.bass as bass
from concourse import mybir

P = 128
D = 1024
SEQ = 256
T = SEQ // P
KD = D // P
HEADS, KV, HD = 16, 4, 64
GQ = HEADS // KV
QKV = (HEADS + 2 * KV) * HD
WINDOW, BUCKETS, MAXDIST = 128, 32, 128
DI = 2 * D
SH, SHD, SG, NS = 32, 64, 4, 128
HG = SH // SG
XBC = DI + 2 * SG * NS
NPROJ = DI + XBC + SH
TAPS = 4
CH = XBC // P
FF = 7 * D // 2
EXPERTS = 8
EPS = 1e-6
MASKED = -1e30

HALF = 512
TW = 1024
RAW = 12
SPLIT = 4
FJ = FF // HALF
FK = FF // P
BODY = FJ * KD + FK
WARM_NORM, WARM_SSD, WARM_Y, WARM_MASK, WARM_ROUTE = 9, 5, 4, 2, 3
LEAD = 3
EARLY = {"qkv": 3, "wo": 4, "ffn": 2, "proj": 3, "wout": 4}
assert BODY % RAW == 0 and BODY % SPLIT == 0

IS_SCALE = (0, 1, 0, 0, 1, 0)
MOD_SLOT = ((0, 1, 2, 3, 4, 5), (0, 1, 2, 3, 4, 6))


def bucket_of(dist):
    exact = BUCKETS // 2
    if dist < exact:
        return dist
    return min(BUCKETS - 1, exact + int(math.log(dist / exact) / math.log(MAXDIST / exact) * (BUCKETS - exact)))


def shape_constants():
    i = np.arange(P)
    square = np.zeros((P, 6, P), np.float32)
    square[:, 5] = np.eye(P)[::-1]
    square[:, 0] = np.eye(P)
    square[:, 1] = 1
    square[:, 2] = i[:, None] <= i[None]
    square[:, 3] = i[:, None] < i[None]
    square[:, 4] = i[None]
    table = np.zeros((BUCKETS + 1, 3 * P), np.float32)
    for j in range(3 * P):
        dist = 2 * P - 1 - j
        table[bucket_of(dist) if 0 <= dist < WINDOW else BUCKETS, j] = 1
    return square.reshape(P, 6 * P), table


def build(nc, A, out, square_in, table_in, overflow_at=P):
    f32, f32r, i32, u32 = mybir.dt.float32, mybir.dt.float32r, mybir.dt.int32, mybir.dt.uint32
    ACT = mybir.ActivationFunctionType
    ALU = mybir.AluOpType
    AX = mybir.AxisListType

    top = [(nc.sbuf_base + 31) // 32 * 32]

    def place(name, shape, dtype=f32, at=None):
        size = int(np.prod(shape[1:])) * 4
        if at is None:
            at = top[0]
            top[0] += (size + 31) // 32 * 32
        return nc.alloc_sbuf_tensor_at(name, shape, dtype, offset=at)

    def area(size):
        top[0] += size
        return top[0] - size

    raw = place("raw", [P, RAW, TW])
    w_hi = place("w_hi", [P, SPLIT, TW], f32r)
    w_lo = place("w_lo", [P, SPLIT, TW], f32r)
    x = place("x", [P, T, D])
    A_AT = area(2 * KD * SEQ * 4)
    U_AT = area(2 * FK * SEQ * 4)
    mod = place("mod", [P, 7, D])
    S_AT = area(2 * D * 4)
    square = place("square", [P, 5, P])
    F_AT = area(4096)
    bias_rows = place("bias_rows", [12, D])
    vecs = place("vecs", [P, P])
    cond = place("cond", [P, KD])
    cond_hi, cond_lo = (place(n, [P, KD], f32r) for n in ("cond_hi", "cond_lo"))
    ss, ms, rs = (place(n, [P, 2]) for n in ("ss", "ms", "rs"))
    flag = place("flag", [1, 1], i32)
    spare = place("spare", [P, 9])
    w_r = place("w_r", [P, KD, EXPERTS])
    comb = place("comb", [P, T, EXPERTS + 1])
    slot_of = place("slot_of", [P, T, EXPERTS + 1])
    assert top[0] <= nc.sbuf_usable_end, top[0]
    ident, ones, tri, tri_strict, column = (square[:, n, :] for n in range(5))

    rel_rows = place("rel_rows", [BUCKETS, HEADS], f32, A_AT + 512)
    vec_rows = place("vec_rows", [P, P], f32, A_AT)
    a_hi = place("a_hi", [P, KD, SEQ], f32r, A_AT)
    a_lo = place("a_lo", [P, KD, SEQ], f32r, A_AT + KD * SEQ * 4)
    ada = place("ada", [P, 2, D], f32, S_AT)
    hm = place("hm", [P, T, D], f32, S_AT)
    h_hi = place("h_hi", [P, FK, SEQ], f32r, U_AT)
    h_lo = place("h_lo", [P, FK, SEQ], f32r, U_AT + FK * SEQ * 4)
    h = place("h", [P, T, HALF], f32, F_AT)
    qkv = place("qkv", [P, T, QKV], f32, U_AT)
    bias = place("bias", [P, HEADS, 2 * P], f32, U_AT + 12288)
    bias_rev = [place(f"bias_rev{g}", [P, GQ, 2 * P], f32, at_)
                for g, at_ in enumerate((S_AT, S_AT + 4096, A_AT + 2048, A_AT + 10240))]
    reversal = mod[:, 6, 0:P]
    q_t = place("q_t", [P, KD, SEQ], f32, U_AT + 28672)
    k_t = place("k_t", [P, KV, SEQ], f32, U_AT + 36864)
    sc = place("sc", [P, 2, GQ * 2 * P], f32, U_AT + 40960)
    qk_square = place("qk_square", [P, T, HEADS * HD], f32, U_AT + 40960)
    p_t = [place("p_t0", [P, 1, GQ * P], f32, U_AT + 53248), place("p_t1", [P, 2, GQ * P], f32, U_AT + 49152)]
    k2 = place("k2", [P, T, KV, 2, HD], f32, U_AT + 53248)
    sinks = place("sinks", [P, HEADS], f32, F_AT)
    qk_gain = place("qk_gain", [P, 2, HD], f32, F_AT + 64)
    relb = place("relb", [BUCKETS + 1, HEADS], f32, F_AT + 576)
    table = place("table", [BUCKETS + 1, 3 * P], f32, F_AT + 640)
    reltab = place("reltab", [HEADS, 3 * P], f32, F_AT + 2176)
    NQK = HEADS + KV
    qk_ss = place("qk_ss", [P, T, NQK], f32, F_AT + 3712)
    stat = place("stat", [P, 2, 4, GQ], f32, F_AT + 3872)
    z_s = place("z_s", [P, T, DI], f32, U_AT)
    xbc = place("xbc", [P, T, XBC], f32, U_AT + 16384)
    b_t = place("b_t", [P, SG, SEQ], f32, U_AT + 40960)
    c_t = place("c_t", [P, SG, SEQ], f32, U_AT + 45056)
    u_pad = place("u_pad", [P, 2, 2, SEQ + TAPS], f32, S_AT)
    cv = place("cv", [P, 2, 2, SEQ], f32, U_AT + 49152)
    dec = place("dec", [P, 2, HG * P], f32, U_AT + 49152)
    xd = place("xd", [P, 2, HG * SHD], f32, A_AT)
    xde = place("xde", [P, 2, HG * SHD], f32, A_AT + 4096)
    y_tmp = place("y_tmp", [P, HG * SHD], f32, S_AT)
    y_sq = place("y_sq", [P, HG * SHD], f32, S_AT + 2048)
    state = place("state", [P, SG, HG * SHD], f32, A_AT + 8192)
    w_dt = place("w_dt", [P, KD, SH], f32, F_AT)
    w_dt_hi = place("w_dt_hi", [P, KD, SH], f32r, S_AT + 4160)
    w_dt_lo = place("w_dt_lo", [P, KD, SH], f32r, S_AT + 5184)
    srow = place("srow", [P, 3, SH], f32, F_AT + 1024)
    dt = place("dt", [P, T, SH], f32, F_AT + 1408)
    dt_rows = place("dt_rows", [SH, SEQ], f32, S_AT + 6208)
    dt_a = place("dt_a", [P, T, SH], f32, F_AT + 1664)
    dt_e = place("dt_e", [P, T, SH], f32, F_AT + 1920)
    acs = place("acs", [P, 2 * T, SH], f32, F_AT + 2176)
    acs_e = place("acs_e", [P, T, SH], f32, F_AT + 2688)
    end_e = place("end_e", [P, T, SH], f32, F_AT + 2944)
    cbm = place("cbm", [P, P], f32, F_AT + 3200)
    yss = place("yss", [P, T, SG], f32, F_AT + 3712)
    y_hi = place("y_hi", [P, DI // P, SEQ], f32r, A_AT)
    y_lo = place("y_lo", [P, DI // P, SEQ], f32r, U_AT)
    EH = FK * P * 4
    e_hi = place("e_hi", [P, FK, P], f32r, U_AT)
    e_lo = place("e_lo", [P, FK, P], f32r, U_AT + EH)
    t_hi = place("t_hi", [P, T, D], f32r, U_AT + 2 * EH)
    t_lo = place("t_lo", [P, T, D], f32r, U_AT + 2 * EH + 8192)
    y_sum = place("y_sum", [P, T, D], f32, U_AT + 2 * EH + 16384)
    pick = place("pick", [P, T, P], f32r, U_AT + 2 * EH + 24576)
    put = place("put", [P, T, P], f32r, U_AT + 2 * EH + 25600)
    g_hi = place("g_hi", [P, KD, P], f32r, A_AT)
    g_lo = place("g_lo", [P, KD, P], f32r, A_AT + 4096)
    yd_hi = place("yd_hi", [P, D], f32r, A_AT + 8192)
    yd_lo = place("yd_lo", [P, D], f32r, A_AT + 12288)
    w_r_hi = place("w_r_hi", [P, KD, EXPERTS], f32r, F_AT + 2816)
    w_r_lo = place("w_r_lo", [P, KD, EXPERTS], f32r, F_AT + 3072)
    lg_rows = place("lg_rows", [EXPERTS, SEQ], f32, F_AT)
    lg = place("lg", [P, T, EXPERTS], f32, F_AT + 2304)
    mx = place("mx", [P, T, 8], f32, F_AT + 2368)
    mi = place("mi", [P, T, 8], u32, F_AT + 2432)
    mif = place("mif", [P, T, 8], f32, F_AT + 2496)
    oh = place("oh", [P, T, 2, EXPERTS], f32, F_AT + 2560)
    tw = place("tw", [P, T, 3], f32, F_AT + 2688)
    msk = place("msk", [P, T, EXPERTS], f32, F_AT + 2720)
    cmax = place("cmax", [P, 1], f32, F_AT + 2784)

    acc = [nc.alloc_psum_tensor(f"acc{n}", [P, 2 * HALF], f32) for n in range(3)]
    xb = [nc.alloc_psum_tensor(f"xb{n}", [P, HALF], f32) for n in range(2)]
    rel_dram = nc.dram_tensor("rel_scratch", (HEADS, 3 * P), f32, kind="Internal").ap()

    def r32(ap):
        return ap.bitcast(f32)

    sem = nc.alloc_semaphore
    raw_ready = [sem(f"raw_ready{n}") for n in range(RAW)]
    raw_used = sem("raw_used")
    hi_ready = sem("hi_ready")
    w_used = sem("w_used")
    acc_full = sem("acc_full")
    acc_done = [sem(f"acc_done{n}") for n in range(3)]
    rows_full = sem("rows_full")
    xb_full = sem("xb_full")
    xb_done = [sem(f"xb_done{n}") for n in range(2)]
    xb_hi = sem("xb_hi")
    dve_step = sem("dve_step")
    act_step = sem("act_step")
    ld_square, ld_rows, ld_vecs, ld_x, ld_tab, ld_att, ld_mix, ld_norm, ld_router, st_rel, st_out = (
        sem(n) for n in ("ld_square", "ld_rows", "ld_vecs", "ld_x", "ld_tab", "ld_att", "ld_mix",
                         "ld_norm", "ld_router", "st_rel", "st_out"))
    relb_set, cond_ready, ada_ready, ld_gain = (
        sem(n) for n in ("relb_set", "cond_ready", "ada_ready", "ld_gain"))
    ss_ready, ms_ready, root_ready, hm_ready, x_ready = (
        sem(n) for n in ("ss_ready", "ms_ready", "root_ready", "hm_ready", "x_ready"))
    qk_sq, qk_ms, qk_root, qk_ready, max_ready, exp_ready, p_ready = (
        sem(n) for n in ("qk_sq", "qk_ms", "qk_root", "qk_ready", "max_ready",
                         "exp_ready", "p_ready"))
    ld_bias = [sem(f"ld_bias{n}") for n in range(2)]
    small_hi, small_lo = sem("small_hi"), sem("small_lo")
    gate_ready = sem("gate_ready")
    u_ready, cv_ready, cs_ready, norm_free = (
        sem(n) for n in ("u_ready", "cv_ready", "cs_ready", "norm_free"))
    dtv_ready, dte_ready, dta_ready, acs_ready, acse_ready = (
        sem(n) for n in ("dtv_ready", "dte_ready", "dta_ready", "acs_ready", "acse_ready"))
    state_ready, e_ready, mt_ready, y_ready, yss_ready, yms_ready, yroot, yn_ready = (
        sem(n) for n in ("state_ready", "e_ready", "mt_ready", "y_ready", "yss_ready", "yms_ready",
                         "yroot", "yn_ready"))
    t_hi_ready, t_lo_ready, tw_in, tw_exp, mask_ready, route_ready = (
        sem(n) for n in ("t_hi_ready", "t_lo_ready", "tw_in", "tw_exp", "mask_ready", "route_ready"))
    pick_ready, yd_hi_ready, yd_lo_ready, final_step = (
        sem(n) for n in ("pick_ready", "yd_hi_ready", "yd_lo_ready", "final_step"))

    def ada_before(s):
        return min(n_ada, s * n_ada // (BODY - KD))

    def ada_after(s):
        return ada_before(s + 1) != ada_before(s)

    n_ada = 6 * KD
    raw0, spl0, pc0, pr0 = {}, {}, {}, {}
    at = [0, 0, 0, 0]
    for stage, raws, splits, pieces, pairs in (
        ("start", 0, 0, 2, 0), ("ada", 2 * KD, 2 * KD, 0, 2), ("norm0", 0, 0, 4, 0),
        ("qkv", 12, 12, 0, 4), ("heads", 0, 0, 6 + 2, 0), ("attend", 4 * KD, 0, 20 + 6, 12),
        ("wo", KD, KD, 0, 2), ("norm1", 0, 0, 4, 0),
        ("ffn", BODY + n_ada, BODY, 2 * FJ + 12, 2 * FJ + 2), ("norm2", 0, 0, 4, 0),
        ("proj", 5 * KD, 5 * KD, 2 + 22 + 1, 10),
        ("ssd", 0, 0, 8, 16), ("ynorm", 0, 0, 8, 0), ("wout", 2 * KD, 2 * KD, 0, 2),
        ("norm3", 0, 0, 4, 0), ("route", 0, 0, 3, 0), ("moe", 0, 0, 0, 0),
    ):
        raw0[stage], spl0[stage], pc0[stage], pr0[stage] = at
        at = [a + b for a, b in zip(at, (raws, splits, pieces, pairs))]

    def body_pieces(mixture):
        after = {}
        for j in range(FJ):
            after.setdefault(KD * (j + 1) + 3, []).extend(("h", j, t) for t in range(1 if mixture else T))
        if mixture:
            for n in range(2 * T):
                after.setdefault(2 * KD + 4 + 2 * n, []).append(("scatter", n // 2, n % 2))
            after.setdefault(3 * KD + 4, []).append(("put",))
            for n in range(4):
                after.setdefault(FJ * KD + 8 + 4 * n, []).append(("gather", n // 2, n % 2))
        else:
            done = 0
            for s in range(BODY):
                if ada_after(s):
                    done += 1
                    if done % KD == 0:
                        c = done // KD - 1
                        after.setdefault(min(s + 1, BODY - 1), []).extend(("ada", c, n) for n in range(2))
        order, n = {}, 0
        for s in sorted(after):
            order[s] = [(n + m, *what) for m, what in enumerate(after[s])]
            n += len(after[s])
        return order

    PIECES = {False: body_pieces(False), True: body_pieces(True)}
    assert sum(len(v) for v in PIECES[True].values()) == 16
    assert sum(len(v) for v in PIECES[False].values()) == 2 * FJ + 12

    def pieces_read_after(mixture, s):
        last = s == BODY - 1
        found = list(PIECES[mixture].get(s - LEAD, []))
        if last:
            for later in range(s - LEAD + 1, BODY):
                found += PIECES[mixture].get(later, [])
        return found

    UNITS = [(g, b) for g in range(KV) for b in range(T)]
    PER_UNIT = 4 * KD // len(UNITS)

    def score_pair(u):
        return pr0["attend"] + 3 * (u // 2) + u % 2

    def ada_pair(c):
        return pr0["ada"] + c if c < 2 else pr0["attend"] + 3 * (c - 2) + 2

    att_piece, out_piece, bias_piece, n = {}, {}, {0: pc0["heads"] + 2 * T}, pc0["attend"]
    for u, (g, b) in enumerate(UNITS):
        if u:
            out_piece[u - 1] = n
            n += 1
        att_piece[u] = n
        n += b + 1
        if u < KV - 1:
            bias_piece[u + 1] = n
            n += 2
    out_piece[len(UNITS) - 1] = n
    assert n + 1 == pc0["wo"]

    def turn_piece(t, part):
        return pc0["heads"] + (2 * T + 2 + t if part == 2 else 2 * t + part)

    SUNITS = [(c, g) for c in range(T) for g in range(SG)]
    ssd_pair, n = {}, pr0["ssd"]
    for what in [("a", 0), ("a", 1)] + [w for u in range(8) for w in ([("y", u)] + ([("a", u + 2)] if u < 6 else []))]:
        ssd_pair[what] = n
        n += 1
    def full_no(n):
        return len(UNITS) + n - pr0["ssd"] + 1

    PROJ_GROUPS = (2, 3, 4, 0, 1)
    NCV = CH // 2
    CBACK = 10

    def conv_in_at(q):
        return KD + 2 + 2 * q

    def conv_back_at(q):
        return conv_in_at(q) + 4

    DT_AT = 6
    DT_TURN_AT = KD + 3
    SUMS_AT = KD + 9
    proj_piece, n = {}, pc0["proj"]
    for i in range(5 * KD):
        for what, at_ in ([("dt", DT_AT), ("dt_turn", DT_TURN_AT), ("sums", SUMS_AT)]
                          + [(("b", q), conv_back_at(q)) for q in range(CBACK)] + [(("f", q), conv_in_at(q)) for q in range(NCV)]):
            if i == at_:
                proj_piece[what] = n
                n += 1
    cv_piece = proj_piece
    assert n == pc0["ssd"]

    moe_uses = [(FJ + 1) // 2, FJ // 2, 1]
    pair_uses0 = [len([m for m in range(pr0["moe"]) if m % 3 == q]) for q in range(3)]
    ROUND_PIECES = 4 + 16 * EXPERTS + 4

    class Body:

        def __init__(self, mixture, e=0, rnd=0):
            self.mixture, self.e = mixture, e
            self.tiles = 1 if mixture else T
            if mixture:
                self.raw = raw0["moe"] + rnd * EXPERTS * BODY
                self.spl = spl0["moe"] + rnd * EXPERTS * BODY
                self.pc = pc0["moe"] + rnd * ROUND_PIECES + 4
                self.pr = pr0["moe"] + rnd * EXPERTS * (FJ + 1)
                self.rnd = rnd
            else:
                self.raw, self.spl, self.pc, self.pr, self.rnd = raw0["ffn"], spl0["ffn"], pc0["ffn"], pr0["ffn"], 0

        def raw_no(self, s):
            extra = 0 if self.mixture else ada_before(s)
            return self.raw + s + extra

        def pair(self, j, t):
            if not self.mixture:
                n = self.pr + T * j + t
                return n % 3, n // 3
            q = 2 if j == FJ else j % 2
            used = pair_uses0[q] + self.rnd * EXPERTS * moe_uses[q] + (0 if j == FJ else j // 2)
            return q, used + self.e * moe_uses[q]

        def full(self, j):
            return self.spl + KD * (j + 1) + self.e * BODY

    def rep(e, per):
        return e * per

    def swiglu_source(w_gu, w_down, s):
        if s < FJ * KD:
            j, k = divmod(s, KD)
            return w_gu[k * P:(k + 1) * P, :].rearrange("p (h n) -> p h n", h=2)[:, :, j * HALF:(j + 1) * HALF]
        k = s - FJ * KD
        return w_down[k * P:(k + 1) * P, :]

    block = nc.Block()
    with block:

        @block.sync
        def _(sp):
            def load(no, src, e=0):
                if no >= RAW:
                    sp.wait_ge(raw_used, no - RAW + 1 + rep(e, BODY))
                dst = raw[:, no % RAW, :]
                if len(src.shape) == 3:
                    dst = dst.rearrange("p (h n) -> p h n", h=src.shape[1])
                sp.dma_start(dst, src).then_inc(raw_ready[no % RAW], 16)

            def row(src, n):
                return bass.AP(src.tensor, src.offset, [[0, P], [1, n]])

            sp.dma_start(square[:, :, :], square_in[:, 0:5 * P].rearrange("p (n m) -> p n m", n=5)).then_inc(ld_square, 16)
            sp.dma_start(reversal, square_in[:, 5 * P:6 * P]).then_inc(ld_square, 16)
            sp.dma_start(vec_rows[0:KD, :], A["c"].rearrange("b (k p) -> (b k) p", p=P)).then_inc(ld_vecs, 16)
            sp.dma_start(vec_rows[KD:KD + TAPS * CH, :], A["ssm_conv_w"][0].rearrange("t (k p) -> (t k) p", p=P)).then_inc(ld_vecs, 16)
            sp.dma_start(vec_rows[KD + TAPS * CH:P, :], A["ssm_conv_b"].rearrange("b (k p) -> (b k) p", p=P)).then_inc(ld_vecs, 16)
            sp.dma_start(table[:, :], table_in).then_inc(ld_tab, 16)
            sp.dma_start(rel_rows[:, :], A["rel_bias"]).then_inc(ld_tab, 16)
            sp.dma_start(bias_rows[:, :], A["ada_b"].rearrange("l (g n) -> (l g) n", n=D)).then_inc(ld_rows, 16)
            sp.dma_start(x[:, :, :], A["x"][0].rearrange("(t p) n -> p t n", p=P)).then_inc(ld_x, 16)
            sp.dma_start(w_r[:, :, :], A["moe_w_router"][0].rearrange("(k p) n -> p k n", p=P)).then_inc(ld_router, 16)
            sp.dma_start(sinks[:, :], row(A["attn_sinks"], HEADS)).then_inc(ld_att, 16)
            sp.dma_start(qk_gain[:, 0, :], row(A["attn_q_gain"], HD)).then_inc(ld_att, 16)
            sp.dma_start(qk_gain[:, 1, :], row(A["attn_k_gain"], HD)).then_inc(ld_att, 16)

            def ada_load(layer, no, i):
                c, k = divmod(i, KD)
                load(no, A["ada_w"][layer, k * P:(k + 1) * P, c * D:(c + 1) * D])

            no = 0
            for i in range(2 * KD):
                ada_load(0, no, i)
                no += 1
                if i == KD:
                    for half in range(2):
                        sp.dma_start(mod[:, 1 + 3 * half, :], row(A["norm_gain"][0, half:half + 1, :], D)).then_inc(ld_gain, 16)
                    sp.wait_ge(xb_done[1], 1)
                    sp.dma_start(rel_dram, reltab[:, :]).then_inc(st_rel, 16)
            w = A["attn_w_qkv"][0]
            for k in range(KD):
                load(no, w[k * P:(k + 1) * P, 0:D])
                no += 1
            for k in range(0, KD, 2):
                load(no, w[k * P:(k + 2) * P, D:QKV].rearrange("(h p) n -> p h n", h=2))
                no += 1
            def bias_load(g):
                sp.dma_start(bias_rev[g][:, :, :],
                             bass.AP(rel_dram.tensor, g * GQ * 3 * P, [[1, P], [3 * P, GQ], [1, 2 * P]])).then_inc(ld_bias[g // 2], 16)

            sp.wait_ge(st_rel, 16)
            sp.wait_ge(xb_full, pc0["qkv"])
            for g in (0, 1):
                bias_load(g)
            for i in range(2 * KD, 6 * KD):
                if i == 2 * KD + RAW:
                    sp.wait_ge(w_used, spl0["heads"])
                    for g in (2, 3):
                        bias_load(g)
                ada_load(0, no, i)
                no += 1
            for k in range(KD):
                load(no, A["attn_w_o"][0, k * P:(k + 1) * P, :])
                no += 1
            n = 0
            for s in range(BODY):
                load(no, swiglu_source(A["ffn_w_gu"][0], A["ffn_w_down"][0], s))
                no += 1
                if s == RAW:
                    sp.wait_ge(hm_ready, 4 * T)
                    for c in range(6):
                        src = A["norm_gain"][1, c // 3:c // 3 + 1, :] if IS_SCALE[c] else A["ada_b"][1:2, c * D:(c + 1) * D]
                        sp.dma_start(mod[:, MOD_SLOT[1][c], :], row(src, D)).then_inc(ld_gain, 16)
                if ada_after(s):
                    ada_load(1, no, n)
                    n += 1
                    no += 1
            w = A["ssm_w_in"][0]
            for i in range(5 * KD):
                g, k = PROJ_GROUPS[i // KD], i % KD
                load(no, w[k * P:(k + 1) * P, g * TW:(g + 1) * TW])
                no += 1
                if i == KD - 1:
                    sp.wait_ge(x_ready, 2 * T)
                    sp.dma_start(w_dt[:, :, :], w[:, 5 * TW:NPROJ].rearrange("(k p) n -> p k n", p=P)).then_inc(ld_mix, 16)
                    for r, name in enumerate(("ssm_dt_bias", "ssm_a_log", "ssm_d")):
                        sp.dma_start(srow[:, r, :], row(A[name], SH)).then_inc(ld_mix, 16)
            sp.wait_ge(norm_free, 1)
            sp.dma_start(mod[:, 0:2, :], bass.AP(A["ssm_norm_w"].tensor, 0, [[0, P], [1, DI]])).then_inc(ld_norm, 16)
            for k in range(2 * KD):
                load(no, A["ssm_w_out"][0, k * P:(k + 1) * P, :])
                no += 1
            assert no == raw0["moe"]

            def experts(rnd):
                with sp.Fori(0, EXPERTS) as e:
                    for s in range(BODY):
                        load(raw0["moe"] + rnd * EXPERTS * BODY + s,
                             swiglu_source(A["moe_w_gu"][0, e], A["moe_w_down"][0, e], s), e)

            experts(0)
            sp.wait_ge(route_ready, 1)
            most = sp.value_load(flag[0:1, 0:1], min_val=0, max_val=SEQ)
            with sp.If(most > overflow_at):
                experts(1)
            sp.wait_ge(x_ready, 3 * T + 1)
            sp.dma_start(out[0].rearrange("(t p) n -> p t n", p=P), x[:, :, :]).then_inc(st_out, 16)
            sp.wait_ge(st_out, 16)

        @block.scalar
        def _(act):
            steps = [0]

            def own(ins):
                steps[0] += 1
                ins.then_inc(act_step, 1)
                act.wait_ge(act_step, steps[0])

            def split_hi(no, w, e=0, per=0, per_raw=0):
                act.wait_ge(raw_ready[no % RAW], 16 * (no // RAW + 1) + rep(e, 16 * per_raw // RAW))
                if w >= SPLIT:
                    act.wait_ge(w_used, w - SPLIT + 1 + rep(e, per))
                act.activation(w_hi[:, w % SPLIT, :], raw[:, no % RAW, :], ACT.Copy).then_inc(hi_ready, 1)

            def early_hi(stage):
                for i in range(EARLY[stage]):
                    split_hi(raw0[stage] + i, spl0[stage] + i)

            def warm(function):
                warmed[0] += 1
                act.activation(spare[:, warmed[0]:warmed[0] + 1], ones[:, 0:1], function)

            warmed = [-1]

            def piece(c):
                act.wait_ge(xb_full, c + 1)
                return xb[c % 2]

            def gemm(stage, evacuate, groups, after=None):
                i = 0
                pr = pr0[stage]
                early = EARLY.get(stage, 0)

                def out_of(gi):
                    act.wait_ge(w_used, spl0[stage] + sum(groups[:gi + 1]))
                    evacuate(gi, pr + T * gi)

                for gi, n_tiles in enumerate(groups):
                    for k in range(n_tiles):
                        if i >= early:
                            split_hi(raw0[stage] + i, spl0[stage] + i)
                        i += 1
                        if evacuate and gi and k == 1:
                            out_of(gi - 1)
                        if after:
                            after(i - 1)
                if evacuate:
                    out_of(len(groups) - 1)

            def norm_root(n):
                warm(ACT.Sqrt)
                if n == 0:
                    act.wait_ge(ld_x, 16)
                for t in range(T):
                    if n:
                        act.wait_ge(x_ready, T * (n - 1) + t + 1)
                    act.activation(hm[:, t, :], x[:, t, :], ACT.Square, accum_out=ss[:, t:t + 1]).then_inc(ss_ready, 1)
                act.wait_ge(ms_ready, n + 1)
                act.activation(rs[:, :], ms[:, :], ACT.Sqrt).then_inc(root_ready, 1)

            def norm(n, stage):
                if n:
                    norm_root(n)
                for hf in range(2):
                    for t in range(T):
                        b = piece(pc0[stage] + T * hf + t)
                        act.activation(a_hi[:, 4 * hf:4 * hf + 4, t * P:(t + 1) * P],
                                       b[:, :].rearrange("p (k m) -> p k m", k=4), ACT.Copy).then_inc(xb_hi, 1)

            b = piece(0)
            act.activation(vecs[:, :], b[:, 0:P], ACT.Copy).then_inc(xb_done[0], 1)
            act.wait_ge(xb_done[0], 1)
            act.activation(cond[:, :], vecs[:, 0:KD], ACT.Silu).then_inc(cond_ready, 1)
            act.wait_ge(cond_ready, 1)
            act.activation(cond_hi[:, :], cond[:, :], ACT.Copy).then_inc(cond_ready, 1)
            b = piece(1)
            act.activation(reltab[:, :], b[0:HEADS, 0:3 * P], ACT.Copy).then_inc(xb_done[1], 1)
            norm_root(0)

            def ada_hi(first, n):
                for i in range(first, first + n):
                    split_hi(raw0["ada"] + i, spl0["ada"] + i)

            ada_hi(0, 2 * KD)
            early_hi("qkv")
            norm(0, "norm0")

            def qkv_out(g, pr):
                lo, n = (0, D) if g == 0 else (D, QKV - D)
                for t in range(T):
                    act.activation(qkv[:, t, lo:lo + n], acc[(pr + t) % 3][:, 0:n], ACT.Copy).then_inc(acc_done[(pr + t) % 3], 1)

            QK_PARTS = ((slice(0, HEADS), slice(0, D)), (slice(HEADS, NQK), slice(D, NQK * HD)))

            def qk_squares(part):
                for n in range(pr0["qkv"] + T * part, pr0["qkv"] + T * (part + 1)):
                    act.wait_ge(acc_done[n % 3], n // 3 + 1)
                if part:
                    act.wait_ge(qk_ms, 1)
                cols = QK_PARTS[part][1]
                act.activation(qk_square[:, :, 0:cols.stop - cols.start], qkv[:, :, cols], ACT.Square).then_inc(qk_sq, 1)

            def qk_roots(part):
                act.wait_ge(qk_ms, part + 1)
                heads = QK_PARTS[part][0]
                act.activation(qk_ss[:, :, heads], qk_ss[:, :, heads], ACT.Sqrt).then_inc(qk_root, 1)

            def qk_steps(i):
                if i == KD + 1:
                    qk_squares(0)
                if i == KD + 2:
                    qk_roots(0)

            gemm("qkv", qkv_out, (KD, KD // 2), qk_steps)
            qk_squares(1)

            def bias_in(g):
                for m in range(2):
                    n, c = 2 * g + m, bias_piece[g] + m
                    b = piece(c)
                    act.activation(bias[:, 2 * n:2 * n + 2, :], b[:, :].rearrange("p (k m) -> p k m", k=2), ACT.Copy).then_inc(xb_done[c % 2], 1)

            def turns_out(t, part):
                c = turn_piece(t, part)
                b = piece(c)
                dst = k_t[:, :, t * P:(t + 1) * P] if part == 2 else q_t[:, 4 * part:4 * part + 4, t * P:(t + 1) * P]
                act.activation(dst, b[:, :].rearrange("p (k m) -> p k m", k=4), ACT.Copy).then_inc(xb_done[c % 2], 1)

            for n in range(2 * T):
                turns_out(n // 2, n % 2)
            qk_roots(1)
            warm(ACT.Exp)
            bias_in(0)
            for t in range(T):
                turns_out(t, 2)

            def exps(u):
                g, blk = UNITS[u]
                w = P * (blk + 1)
                act.wait_ge(max_ready, u + 1)
                for i in range(GQ):
                    act.activation(sc[:, u % 2, i * w:(i + 1) * w], sc[:, u % 2, i * w:(i + 1) * w], ACT.Exp,
                                   bias=stat[:, u % 2, 1, i:i + 1], accum_out=stat[:, u % 2, 2, i:i + 1])
                act.activation(stat[:, u % 2, 3, :], stat[:, u % 2, 3, :], ACT.Exp).then_inc(exp_ready, 1)

            def probs_out(u):
                g, blk = UNITS[u]
                for kc in range(blk + 1):
                    c = att_piece[u] + kc
                    b = piece(c)
                    act.activation(p_t[blk][:, kc, :], b[:, :], ACT.Copy).then_inc(xb_done[c % 2], 1)

            def heads_hi(u):
                g, blk = UNITS[u]
                b = piece(out_piece[u])
                act.activation(a_hi[:, 2 * g:2 * g + 2, blk * P:(blk + 1) * P],
                               b[:, 0:2 * P].rearrange("p (k m) -> p k m", k=2), ACT.Copy).then_inc(xb_hi, 1)

            exps(0)
            for u in range(8):
                if u:
                    heads_hi(u - 1)
                if u < 7:
                    exps(u + 1)
                probs_out(u)
                if u < KV - 1:
                    bias_in(u + 1)
            early_hi("wo")
            heads_hi(7)

            gemm("wo", None, (KD,))
            early_hi("ffn")
            norm(1, "norm1")

            def body(B):
                e = B.e
                for s in range(BODY):
                    if B.mixture or s >= EARLY["ffn"]:
                        split_hi(B.raw_no(s), B.spl + s, e, BODY, BODY)
                    if B.mixture and s == 2:
                        act.wait_ge(w_used, B.full(-1))
                        act.activation(yd_hi[:, :], acc[2][:, :], ACT.Copy).then_inc(yd_hi_ready, 1)
                    j, k = divmod(s, KD)
                    if 1 <= j <= FJ and k == 2:
                        act.wait_ge(w_used, B.full(j - 1))
                        for t in range(B.tiles):
                            act.activation(h[:, t, :], acc[B.pair(j - 1, t)[0]][:, 0:HALF], ACT.Silu).then_inc(gate_ready, 1)
                    for c, kind, *which in pieces_read_after(B.mixture, s):
                        c += B.pc
                        if kind == "h":
                            act.wait_ge(xb_full, c + 1 + rep(e, 16))
                            j, t = which
                            dst = (e_hi if B.mixture else h_hi)[:, 4 * j:4 * j + 4, t * P:(t + 1) * P]
                            act.activation(dst, xb[c % 2][:, :].rearrange("p (k m) -> p k m", k=4), ACT.Copy).then_inc(xb_hi, 1)
                        elif kind == "put":
                            act.wait_ge(xb_full, c + 1 + rep(e, 16))
                            act.activation(put[:, :, :], xb[c % 2][:, 0:T * P].rearrange("p (t m) -> p t m", t=T),
                                           ACT.Copy).then_inc(xb_done[c % 2], 1)
                        elif kind == "gather" and which[0] == 0:
                            act.wait_ge(xb_full, c + 1 + rep(e, 16))
                            q = which[1]
                            act.activation(g_hi[:, 4 * q:4 * q + 4, :], xb[c % 2][:, :].rearrange("p (k m) -> p k m", k=4),
                                           ACT.Copy).then_inc(xb_done[c % 2], 1)

            body(Body(False))
            early_hi("proj")
            norm(2, "norm2")

            def proj_out(gi, pr):
                g = PROJ_GROUPS[gi]
                for t in range(T):
                    n = pr + t
                    if g < 2:
                        act.activation(z_s[:, t, g * TW:(g + 1) * TW], acc[n % 3][:, :], ACT.Silu).then_inc(acc_done[n % 3], 1)
                    else:
                        act.activation(xbc[:, t, (g - 2) * TW:(g - 1) * TW], acc[n % 3][:, :], ACT.Copy).then_inc(acc_done[n % 3], 1)

            def rows_out(c, rows_, n):
                b = piece(c)
                act.activation(rows_[:, :], b[0:n, 0:SEQ], ACT.Copy).then_inc(xb_done[c % 2], 1)

            def mixer_steps(i):
                if i == DT_AT - 1:
                    act.wait_ge(ld_mix, 64)
                    act.activation(w_dt_hi[:, :, :], w_dt[:, :, :], ACT.Copy).then_inc(small_hi, 1)
                if i == DT_AT + LEAD:
                    rows_out(proj_piece["dt"], dt_rows, SH)
                if i == DT_TURN_AT + LEAD:
                    act.wait_ge(dtv_ready, 1)
                    own(act.activation(dt_e[:, :, :], dt[:, :, :], ACT.Abs))
                    own(act.activation(dt_e[:, :, :], dt_e[:, :, :], ACT.Exp, scale=-1.0))
                    own(act.activation(srow[:, 1, :], srow[:, 1, :], ACT.Exp))
                    act.activation(dt_e[:, :, :], dt_e[:, :, :], ACT.Ln, bias=ones[:, 0:1]).then_inc(dte_ready, 1)
                for q in range(NCV):
                    if q < CBACK and i == conv_back_at(q) + LEAD:
                        c = cv_piece["b", q]
                        b = piece(c)
                        act.activation(xbc[:, :, 2 * P * q:2 * P * (q + 1)], b[:, :].rearrange("p (t m) -> p t m", t=T),
                                       ACT.Copy).then_inc(xb_done[c % 2], 1)
                for q in range(NCV):
                    if i == conv_in_at(q) + LEAD:
                        b = piece(cv_piece["f", q])
                        if q < 2:
                            act.wait_ge(u_ready, 1)
                        act.activation(u_pad[:, q % 2, :, TAPS - 1:TAPS - 1 + SEQ], b[:, :].rearrange("p (k m) -> p k m", k=2),
                                       ACT.Copy).then_inc(xb_done[cv_piece["f", q] % 2], 1)
                    if i == conv_in_at(q) + LEAD + 1:
                        act.wait_ge(cv_ready, q + 1)
                        dst = cv[:, q % 2] if q < 8 else (b_t if q < CBACK else c_t)[:, 2 * (q % 2):2 * (q % 2) + 2, :]
                        act.activation(dst, cv[:, q % 2], ACT.Silu).then_inc(cs_ready, 1)

            def unit_decays(u):
                c, g = SUNITS[u]
                n = ssd_pair["a", u]
                act.wait_ge(acc_full, full_no(n))
                if u >= 2:
                    act.wait_ge(acc_full, full_no(ssd_pair["y", u - 2]))
                for i in range(HG):
                    cols = slice(i * P, (i + 1) * P)
                    ins = act.activation(dec[:, u % 2, cols], acc[n % 3][:, cols], ACT.Relu, scale=-1.0,
                                         bias=acs[:, c, HG * g + i:HG * g + i + 1])
                ins.then_inc(acc_done[n % 3], 1)
                act.wait_ge(acc_done[n % 3], n // 3 + 1)
                act.activation(dec[:, u % 2, :], dec[:, u % 2, :], ACT.Exp, scale=-1.0).then_inc(e_ready, 1)

            def state_out(u):
                c, g = SUNITS[u]
                if c == 0:
                    n = ssd_pair["y", u]
                    act.wait_ge(acc_full, full_no(n))
                    act.activation(state[:, g, :], acc[n % 3][:, HALF:2 * HALF], ACT.Copy).then_inc(state_ready, 1)

            gemm("proj", proj_out, (KD,) * 5, mixer_steps)
            act.wait_ge(acs_ready, 1)
            unit_decays(0)
            act.activation(acs_e[:, :, :], acs[:, 0:T, :], ACT.Exp).then_inc(acse_ready, 1)
            act.activation(end_e[:, :, :], end_e[:, :, :], ACT.Exp).then_inc(acse_ready, 1)

            def y_square(u):
                c, g = SUNITS[u]
                act.wait_ge(y_ready, u + 1)
                act.wait_ge(yss_ready, u)
                act.activation(y_sq[:, :], xbc[:, c, 512 * g:512 * (g + 1)], ACT.Square, accum_out=yss[:, c, g:g + 1]).then_inc(yss_ready, 1)

            for u in range(1, 8):
                unit_decays(u)
                state_out(u - 1)
                if u >= 2:
                    y_square(u - 2)
            early_hi("wout")
            warm(ACT.Sqrt)
            y_square(6)
            y_square(7)
            act.wait_ge(yms_ready, 1)
            act.activation(rs[:, :], ms[:, :], ACT.Sqrt).then_inc(yroot, 1)
            act.wait_ge(ld_router, 16)
            act.activation(w_r_hi[:, :, :], w_r[:, :, :], ACT.Copy).then_inc(small_hi, 1)

            def y_turned(q):
                for t in range(T):
                    b = piece(pc0["ynorm"] + T * q + t)
                    act.activation(y_hi[:, 4 * q:4 * q + 4, t * P:(t + 1) * P], b[:, :].rearrange("p (k m) -> p k m", k=4),
                                   ACT.Copy).then_inc(xb_hi, 1)

            y_turned(0)
            gemm("wout", None, (2 * KD,), lambda i: y_turned(i // 4 + 1) if i % 4 == 3 and i < 12 else None)
            norm(3, "norm3")

            rows_out(pc0["route"], lg_rows, EXPERTS)
            warm(ACT.Exp)
            act.wait_ge(tw_in, 1)
            act.activation(tw[:, :, 0], tw[:, :, 0], ACT.Exp).then_inc(tw_exp, 1)
            for t in range(T):
                act.activation(t_hi[:, t, :], hm[:, t, :], ACT.Copy).then_inc(t_hi_ready, 1)
            warm(ACT.Silu)

            def first_gather(rnd):
                for q in range(2):
                    c = pc0["moe"] + rnd * ROUND_PIECES + q
                    b = piece(c)
                    act.activation(g_hi[:, 4 * q:4 * q + 4, :], b[:, :].rearrange("p (k m) -> p k m", k=4),
                                   ACT.Copy).then_inc(xb_done[c % 2], 1)

            def experts(rnd):
                first_gather(rnd)
                with act.Fori(0, EXPERTS) as e:
                    body(Body(True, e, rnd))
                act.wait_ge(w_used, spl0["moe"] + (rnd + 1) * EXPERTS * BODY)
                act.activation(yd_hi[:, :], acc[2][:, :], ACT.Copy).then_inc(yd_hi_ready, 1)

            experts(0)
            most = act.value_load(flag[0:1, 0:1], min_val=0, max_val=SEQ)
            with act.If(most > overflow_at):
                experts(1)

        @block.vector
        def _(dve):
            steps = [0]

            def own(ins):
                steps[0] += 1
                ins.then_inc(dve_step, 1)
                dve.wait_ge(dve_step, steps[0])

            def split_lo(no, w, e=0):
                dve.wait_ge(hi_ready, w + 1 + rep(e, BODY))
                dve.tensor_tensor(w_lo[:, w % SPLIT, :], raw[:, no % RAW, :], r32(w_hi[:, w % SPLIT, :]), ALU.subtract).then_inc(raw_used, 1)

            def early_lo(stage, first=0, end=None):
                for i in range(first, end or EARLY[stage]):
                    split_lo(raw0[stage] + i, spl0[stage] + i)

            def step(ins):
                steps[0] += 1
                ins.then_inc(dve_step, 1)
                return steps[0]

            first_half = [0]

            def ada_half(no, k, buf, hf):
                cols = slice(hf * HALF, (hf + 1) * HALF)
                dst, src = ada[:, buf, cols], raw[:, no % RAW, cols]
                dve.wait_ge(raw_ready[no % RAW], 16 * (no // RAW + 1))
                if k == 0:
                    ins = dve.tensor_scalar(dst, src, cond[:, 0:1], None, ALU.mult)
                else:
                    if hf:
                        dve.wait_ge(raw_used, no)
                    else:
                        dve.wait_ge(dve_step, first_half[0])
                    ins = dve.scalar_tensor_tensor(dst, src, cond[:, k:k + 1], dst, ALU.mult, ALU.add)
                if hf:
                    ins.then_inc(raw_used, 1)
                else:
                    first_half[0] = step(ins)

            def ada_piece(c, n, pc):
                dve.wait_ge(xb_full, pc + 1)
                dve.wait_ge(ld_gain, 16 * 8)
                dst = mod[:, MOD_SLOT[1][c], n * HALF:(n + 1) * HALF]
                if IS_SCALE[c]:
                    dve.scalar_tensor_tensor(dst, xb[pc % 2][:, :], 1.0, dst, ALU.add, ALU.mult).then_inc(xb_done[pc % 2], 1)
                else:
                    dve.tensor_tensor(dst, xb[pc % 2][:, :], dst, ALU.add).then_inc(xb_done[pc % 2], 1)

            lows = [0]

            def piece_lo(c, dst, m=4):
                lows[0] += 1
                dve.wait_ge(xb_hi, lows[0])
                d_hi, d_lo = dst
                dve.tensor_tensor(d_lo, xb[c % 2][:, :].rearrange("p (k m) -> p k m", k=m), r32(d_hi), ALU.subtract).then_inc(xb_done[c % 2], 1)

            def norm_root(n):
                dve.wait_ge(ss_ready, T * (n + 1))
                dve.tensor_scalar(ms[:, :], ss[:, :], 1.0 / D, EPS, ALU.mult, ALU.add).then_inc(ms_ready, 1)
                dve.wait_ge(root_ready, n + 1)
                own(dve.reciprocal(rs[:, :], rs[:, :]))

            def norm(n, stage):
                if n:
                    dve.wait_ge(x_ready, T * n)
                layer, half = divmod(n, 2)
                sh, g = (mod[:, MOD_SLOT[layer][3 * half + q], :] for q in range(2))
                if n:
                    norm_root(n)

                def rows(hf):
                    cols = slice(hf * HALF, (hf + 1) * HALF)
                    for t in range(T):
                        done = step(dve.scalar_tensor_tensor(hm[:, t, cols], x[:, t, cols], rs[:, t:t + 1], g[:, cols], ALU.mult, ALU.mult))
                    for t in range(T):
                        dve.wait_ge(dve_step, done - T + 1 + t)
                        dve.tensor_tensor(hm[:, t, cols], hm[:, t, cols], sh[:, cols], ALU.add).then_inc(hm_ready, 1)

                def turned_lo(m):
                    hf, t = divmod(m, T)
                    part = (slice(None), slice(4 * hf, 4 * hf + 4), slice(t * P, (t + 1) * P))
                    piece_lo(pc0[stage] + m, (a_hi[part], a_lo[part]))

                for hf in range(2):
                    rows(hf)
                    for t in range(T):
                        turned_lo(T * hf + t)
            def residual(stage, groups_before, gate):
                first = pr0[stage] + T * groups_before
                after = {"wo": "norm1", "ffn": "norm2", "wout": "norm3"}[stage]
                for t in range(T):
                    if t == 0:
                        dve.wait_ge(rows_full, ("wo", "ffn", "wout").index(stage) + 1)
                    else:
                        dve.wait_ge(w_used, spl0[after])
                    n = first + t
                    dve.tensor_tensor(hm[:, t, :], acc[n % 3][:, :], gate, ALU.mult).then_inc(acc_done[n % 3], 1)
                    dve.wait_ge(acc_done[n % 3], n // 3 + 1)
                    dve.tensor_tensor(x[:, t, :], x[:, t, :], hm[:, t, :], ALU.add).then_inc(x_ready, 1)

            def gemm(stage, groups, after=None):
                for i in range(sum(groups)):
                    if i >= EARLY.get(stage, 0):
                        split_lo(raw0[stage] + i, spl0[stage] + i)
                    if after:
                        after(i)

            dve.memset(relb[BUCKETS:BUCKETS + 1, :], MASKED).then_inc(relb_set, 1)
            dve.wait_ge(ld_tab, 32)
            for o in range(2):
                dve.tensor_copy(relb[0:BUCKETS, :].rearrange("b (g o i) -> b g o i", o=2, i=2)[:, :, o, :],
                                rel_rows[:, :].rearrange("b (g i o) -> b g i o", o=2, i=2)[:, :, :, o]).then_inc(relb_set, 1)
            dve.wait_ge(cond_ready, 1)
            dve.wait_ge(cond_ready, 2)
            dve.tensor_tensor(cond_lo[:, :], cond[:, :], r32(cond_hi[:, :]), ALU.subtract).then_inc(cond_ready, 1)

            def ada_row(c):
                n = ada_pair(c)
                if c < 2:
                    dve.wait_ge(w_used, spl0["ada"] + (c + 1) * KD)
                else:
                    dve.wait_ge(ada_ready, c - 1)
                dst = mod[:, MOD_SLOT[0][c], :]
                if IS_SCALE[c]:
                    dve.wait_ge(ld_gain, 32)
                    dve.scalar_tensor_tensor(dst, acc[n % 3][:, :], 1.0, dst, ALU.add, ALU.mult).then_inc(acc_done[n % 3], 1)
                else:
                    dve.tensor_copy(dst, acc[n % 3][:, :]).then_inc(acc_done[n % 3], 1)

            def ada_rows_stand(*groups):
                for c in groups:
                    n = ada_pair(c)
                    dve.wait_ge(acc_done[n % 3], n // 3 + 1)

            norm_root(0)
            for i in range(2 * KD):
                split_lo(raw0["ada"] + i, spl0["ada"] + i)
                if i == KD + 1:
                    ada_row(0)
            early_lo("qkv")
            ada_row(1)
            ada_rows_stand(0, 1)
            norm(0, "norm0")

            qk_heads = qkv[:, :, 0:NQK * HD].rearrange("p t (h d) -> p t h d", d=HD)

            def qk_means(heads):
                n = heads.stop - heads.start
                own(dve.reduce_sum(qk_ss[:, :, heads], qk_square[:, :, 0:n * HD].rearrange("p t (h d) -> p t h d", d=HD), axis=AX.X))
                dve.tensor_scalar(qk_ss[:, :, heads], qk_ss[:, :, heads], 1.0 / HD, EPS, ALU.mult, ALU.add).then_inc(qk_ms, 1)

            def qk_scale(heads):
                n = heads.stop - heads.start
                own(dve.reciprocal(qk_ss[:, :, heads], qk_ss[:, :, heads]))
                for t in range(T):
                    v = qk_heads[:, t, heads, :]
                    own(dve.tensor_tensor(v, v, qk_ss[:, t, heads].unsqueeze(2).to_broadcast([P, n, HD]), ALU.mult))

            def qk_steps(i):
                if i == KD + 1:
                    dve.wait_ge(qk_sq, 1)
                    qk_means(slice(0, HEADS))
                if i == KD + 2:
                    dve.wait_ge(qk_root, 1)
                    qk_scale(slice(0, HEADS))
                if i == KD + 3:
                    dve.wait_ge(ld_att, 48)
                    for t in range(T):
                        v = qk_heads[:, t, 0:HEADS, :]
                        dve.tensor_tensor(v, v, qk_gain[:, 0:1, :].to_broadcast([P, HEADS, HD]), ALU.mult).then_inc(qk_ready, 1)

            gemm("qkv", (KD, KD // 2), qk_steps)
            dve.wait_ge(qk_sq, 2)
            qk_means(slice(HEADS, NQK))
            dve.wait_ge(qk_root, 2)
            qk_scale(slice(HEADS, NQK))
            for t in range(T):
                for twice in range(2):
                    dve.tensor_tensor(k2[:, t, :, twice, :], qk_heads[:, t, HEADS:NQK, :],
                                      qk_gain[:, 1:2, :].to_broadcast([P, KV, HD]), ALU.mult).then_inc(qk_ready, 1)

            def ada_beside(u, *halves):
                for m in halves:
                    if u >= 0:
                        c, k = divmod(PER_UNIT * u + m // 2, KD)
                        ada_half(raw0["attend"] + PER_UNIT * u + m // 2, k, c % 2, m % 2)

            def unit_scores(u, beside):
                g, blk = UNITS[u]
                w = P * (blk + 1)
                n = score_pair(u)
                if blk == 0:
                    for c in (bias_piece[g], bias_piece[g] + 1):
                        dve.wait_ge(xb_done[c % 2], c // 2 + 1)
                dve.wait_ge(acc_full, u + 1)
                s3 = sc[:, u % 2, 0:GQ * w].rearrange("p (i m) -> p i m", i=GQ)
                sink = sinks[:, GQ * g:GQ * (g + 1)].rearrange("p (i o) -> p o i", o=2)
                top_, exit_ = (stat[:, u % 2, q, :].rearrange("p (o i) -> p o i", o=2) for q in (0, 3))
                for o in range(2):
                    done = step(dve.scalar_tensor_tensor(s3[:, 2 * o:2 * o + 2, :],
                                                         acc[n % 3][:, o * HALF:o * HALF + 2 * w].rearrange("p (i m) -> p i m", i=2), HD ** -0.5,
                                                         bias[:, GQ * g + 2 * o:GQ * g + 2 * o + 2, (1 - blk) * P:2 * P], ALU.mult, ALU.add))
                ada_beside(beside, 0)
                dve.wait_ge(dve_step, done)
                dve.sem_inc(acc_done[n % 3], 1)
                done = step(dve.reduce_max(stat[:, u % 2, 0, :], s3, axis=AX.X))
                ada_beside(beside, 1)
                dve.wait_ge(dve_step, done)
                done = step(dve.tensor_tensor(top_, top_, sink, ALU.max))
                ada_beside(beside, 2)
                dve.wait_ge(dve_step, done)
                done = step(dve.tensor_scalar(stat[:, u % 2, 1, :], stat[:, u % 2, 0, :], -1.0, None, ALU.mult))
                dve.tensor_tensor(exit_, sink, top_, ALU.subtract).then_inc(max_ready, 1)
                return done

            def unit_probs(u):
                g, blk = UNITS[u]
                w = P * (blk + 1)
                dve.wait_ge(exp_ready, u + 1)
                s3 = sc[:, u % 2, 0:GQ * w].rearrange("p (i m) -> p i m", i=GQ)
                total = stat[:, u % 2, 0, :]
                done = step(dve.tensor_tensor(total, stat[:, u % 2, 2, :], stat[:, u % 2, 3, :], ALU.add))
                ada_beside(u, 3)
                dve.wait_ge(dve_step, done)
                done = step(dve.reciprocal(total, total))
                ada_beside(u, 4)
                dve.wait_ge(dve_step, done)
                dve.tensor_tensor(s3, s3, total.unsqueeze(2).to_broadcast([P, GQ, w]), ALU.mult).then_inc(p_ready, 1)

            def heads_lo(u):
                g, blk = UNITS[u]
                c = out_piece[u]
                lows[0] += 1
                dve.wait_ge(xb_hi, lows[0])
                part = (slice(None), slice(2 * g, 2 * g + 2), slice(blk * P, (blk + 1) * P))
                dve.tensor_tensor(a_lo[part], xb[c % 2][:, 0:2 * P].rearrange("p (k m) -> p k m", k=2), r32(a_hi[part]),
                                  ALU.subtract).then_inc(xb_done[c % 2], 1)

            unit_scores(0, -1)
            for u in range(8):
                if u < 7:
                    if u:
                        dve.wait_ge(xb_full, att_piece[u - 1] + UNITS[u - 1][1] + 1)
                    unit_scores(u + 1, u)
                else:
                    ada_beside(u, 0, 1, 2)
                unit_probs(u)
                if u:
                    heads_lo(u - 1)
                ada_beside(u, 5, 6, 7)
                if u >= 3 and u % 2:
                    ada_row((u + 1) // 2)
            early_lo("wo")
            heads_lo(7)

            gemm("wo", (KD,))
            ada_row(5)
            ada_rows_stand(2, 3, 4, 5)
            early_lo("ffn")
            residual("wo", 0, mod[:, MOD_SLOT[0][2], :])
            norm(1, "norm1")

            def body(B):
                e = B.e
                ada_n = 0
                for s in range(BODY):
                    if B.mixture or s >= EARLY["ffn"]:
                        split_lo(B.raw_no(s), B.spl + s, e)
                    if B.mixture and s == 2:
                        dve.wait_ge(yd_hi_ready, B.rnd * (EXPERTS + 1) + 1 + rep(e, 1))
                        dve.tensor_tensor(yd_lo[:, :], acc[2][:, :], r32(yd_hi[:, :]), ALU.subtract).then_inc(acc_done[2], 1)
                    j, k = divmod(s, KD)
                    if 1 <= j <= FJ and k == 2:
                        for t in range(B.tiles):
                            q, _ = B.pair(j - 1, t)
                            dve.wait_ge(gate_ready, gates(B, j - 1, t))
                            dve.tensor_tensor(h[:, t, :], h[:, t, :], acc[q][:, HALF:2 * HALF], ALU.mult).then_inc(acc_done[q], 1)
                    if not B.mixture and ada_after(s):
                        c, k = divmod(ada_n, KD)
                        if k == 0 and c >= 2:
                            dve.wait_ge(ada_ready, 4 + c - 1)
                        for hf in range(2):
                            ada_half(B.raw_no(s) + 1, k, c % 2, hf)
                        ada_n += 1
                    if B.mixture and s == FJ * KD + 4:
                        build_pick(e + 1, B.rnd)
                    for c, kind, *which in pieces_read_after(B.mixture, s):
                        c += B.pc
                        if kind == "h":
                            j, t = which
                            part = (slice(None), slice(4 * j, 4 * j + 4), slice(t * P, (t + 1) * P))
                            d_hi, d_lo = (e_hi, e_lo) if B.mixture else (h_hi, h_lo)
                            dve.wait_ge(xb_hi, h_highs(B, j, t))
                            dve.tensor_tensor(d_lo[part], xb[c % 2][:, :].rearrange("p (k m) -> p k m", k=4), r32(d_hi[part]),
                                              ALU.subtract).then_inc(xb_done[c % 2], 1)
                        elif kind == "ada":
                            ada_piece(which[0], which[1], c)
                        elif kind == "scatter":
                            scatter_sum(c, which[0], which[1], e, e)
                        elif kind == "gather" and which[0] == 1:
                            dve.wait_ge(xb_full, c + 1 + rep(e, 16))
                            q = which[1]
                            dve.tensor_copy(g_lo[:, 4 * q:4 * q + 4, :], xb[c % 2][:, :].rearrange("p (k m) -> p k m", k=4)).then_inc(xb_done[c % 2], 1)

            def gates(B, j, t):
                if not B.mixture:
                    return T * j + t + 1
                return T * FJ + B.rnd * EXPERTS * FJ + j + 1 + rep(B.e, FJ)

            def h_highs(B, j, t):
                if not B.mixture:
                    return highs_ffn + T * j + t + 1
                return highs_moe + B.rnd * EXPERTS * FJ + j + 1 + rep(B.e, FJ)

            def build_pick(col, rnd):
                for t in range(T):
                    dve.tensor_scalar(pick[:, t, :], column, slot_of[:, t, bass.ds(col, 1)],
                                      None, ALU.is_equal).then_inc(pick_ready, 1)

            def scatter_sum(c, t, hf, col, e=0):
                dve.wait_ge(xb_full, c + 1 + rep(e, 16))
                dve.wait_ge(xb_done[c % 2], c // 2 + rep(e, 8))
                dst = y_sum[:, t, hf * HALF:(hf + 1) * HALF]
                dve.scalar_tensor_tensor(dst, xb[c % 2][:, :], comb[:, t, bass.ds(col, 1)], dst, ALU.mult, ALU.add).then_inc(xb_done[c % 2], 1)

            highs_ffn = lows[0]
            body(Body(False))
            lows[0] += T * FJ
            early_lo("proj")
            residual("ffn", FJ, mod[:, MOD_SLOT[0][5], :])
            norm(2, "norm2")
            dve.wait_ge(hm_ready, 6 * T)
            dve.sem_inc(norm_free, 1)

            def dt_sum():
                dve.wait_ge(ld_mix, 64)
                c = proj_piece["dt_turn"]
                dve.wait_ge(xb_full, c + 1)
                own(dve.tensor_tensor(dt[:, :, :], xb[c % 2][:, 0:T * SH].rearrange("p (t m) -> p t m", t=T),
                                      srow[:, 0:1, :].to_broadcast([P, T, SH]), ALU.add))
                dve.sem_inc(xb_done[c % 2], 1)
                dve.sem_inc(dtv_ready, 1)

            def dt_parts():
                dve.wait_ge(dte_ready, 1)
                own(dve.scalar_tensor_tensor(dt[:, :, :], dt[:, :, :], 0.0, dt_e[:, :, :], ALU.max, ALU.add))
                dve.scalar_tensor_tensor(dt_a[:, :, :], dt[:, :, :], -1.0, srow[:, 1:2, :].to_broadcast([P, T, SH]),
                                         ALU.mult, ALU.mult).then_inc(dta_ready, 1)

            def run_sums():
                c = proj_piece["sums"]
                dve.wait_ge(xb_full, c + 1)
                own(dve.tensor_copy(acs[:, :, :], xb[c % 2][:, 0:2 * T * SH].rearrange("p (t m) -> p t m", t=2 * T)))
                dve.sem_inc(xb_done[c % 2], 1)
                own(dve.tensor_tensor(end_e[:, :, :], acs[:, T:2 * T, :], acs[:, 0:T, :], ALU.subtract))
                dve.sem_inc(acs_ready, 1)

            def convolve(q):
                c = cv_piece["f", q]
                dve.wait_ge(xb_done[c % 2], c // 2 + 1)
                if q >= 2:
                    dve.wait_ge(cs_ready, q - 1)
                    if q - 2 < 8:
                        dve.wait_ge(xb_full, cv_piece["b", q - 2] + 1)
                for tap in range(TAPS):
                    for m in range(2):
                        k = 2 * q + m
                        src = u_pad[:, q % 2, m, tap:tap + SEQ]
                        wt = vecs[:, KD + tap * CH + k:KD + tap * CH + k + 1]
                        if tap == 0:
                            ins = dve.tensor_scalar(cv[:, q % 2, m, :], src, wt, vecs[:, KD + TAPS * CH + k:KD + TAPS * CH + k + 1],
                                                    ALU.mult, ALU.add)
                        else:
                            ins = dve.scalar_tensor_tensor(cv[:, q % 2, m, :], src, wt, cv[:, q % 2, m, :], ALU.mult, ALU.add)
                        steps[0] += 1
                        ins.then_inc(dve_step, 1)
                        if tap or m:
                            dve.wait_ge(dve_step, steps[0] - 1)
                dve.wait_ge(dve_step, steps[0])
                dve.sem_inc(cv_ready, 1)

            def mixer_steps(i):
                if i == DT_AT - 1:
                    dve.wait_ge(small_hi, 1)
                    dve.tensor_tensor(w_dt_lo[:, :, :], w_dt[:, :, :], r32(w_dt_hi[:, :, :]), ALU.subtract).then_inc(small_lo, 1)
                if i == DT_TURN_AT + LEAD:
                    dt_sum()
                if i == DT_TURN_AT + LEAD + 2:
                    dt_parts()
                if i == SUMS_AT + LEAD:
                    run_sums()
                for q in range(NCV):
                    if i == conv_in_at(q) + LEAD:
                        convolve(q)

            own(dve.memset(u_pad[:, :, :, 0:TAPS - 1], 0.0))
            dve.sem_inc(u_ready, 1)
            gemm("proj", (KD,) * 5, mixer_steps)
            for q in range(2):
                dve.wait_ge(xb_done[q], (pc0["ssd"] + 1 - q) // 2)

            def heads_of(row_, g):
                return row_[:, HG * g:HG * (g + 1)].unsqueeze(2)

            def unit_in(u):
                c, g = SUNITS[u]
                xs3 = xbc[:, c, 512 * g:512 * (g + 1)].rearrange("p (h m) -> p h m", h=HG)
                xd3 = xd[:, u % 2, :].rearrange("p (h m) -> p h m", h=HG)
                own(dve.tensor_tensor(xd3, xs3, heads_of(dt[:, c, :], g).to_broadcast([P, HG, SHD]), ALU.mult))

            def unit_mid(u):
                c, g = SUNITS[u]
                if u == 0:
                    dve.wait_ge(acse_ready, 2)
                pc = pc0["ssd"] + u
                dve.wait_ge(xb_full, pc + 1)
                if c == 0:
                    own(dve.tensor_tensor(xde[:, u % 2, :].rearrange("p (h m) -> p h m", h=HG), xd[:, u % 2, :].rearrange("p (h m) -> p h m", h=HG),
                                          heads_of(end_e[:, 0, :], g).to_broadcast([P, HG, SHD]), ALU.mult))
                own(dve.tensor_tensor(cbm[:, :], xb[pc % 2][:, 0:P], tri, ALU.mult))
                dve.sem_inc(xb_done[pc % 2], 1)
                dve.wait_ge(e_ready, u + 1)
                d3 = dec[:, u % 2, :].rearrange("p (h m) -> p h m", h=HG)
                dve.tensor_tensor(d3, d3, cbm[:, :].unsqueeze(1).to_broadcast([P, HG, P]), ALU.mult).then_inc(mt_ready, 1)

            def unit_out(u):
                c, g = SUNITS[u]
                n = ssd_pair["y", u]
                y = xbc[:, c, 512 * g:512 * (g + 1)]
                y3 = y.rearrange("p (h m) -> p h m", h=HG)
                own(dve.tensor_tensor(y3, y3, heads_of(srow[:, 2, :], g).to_broadcast([P, HG, SHD]), ALU.mult))
                dve.wait_ge(acc_full, full_no(n))
                if c == 0:
                    dve.wait_ge(state_ready, u + 1)
                else:
                    own(dve.tensor_tensor(y_tmp[:, :].rearrange("p (h m) -> p h m", h=HG),
                                          acc[n % 3][:, HALF:2 * HALF].rearrange("p (h m) -> p h m", h=HG),
                                          heads_of(acs_e[:, c, :], g).to_broadcast([P, HG, SHD]), ALU.mult))
                    own(dve.tensor_tensor(y, y, y_tmp[:, :], ALU.add))
                own(dve.tensor_tensor(y, y, acc[n % 3][:, 0:HALF], ALU.add))
                dve.sem_inc(acc_done[n % 3], 1)
                dve.tensor_tensor(y, y, z_s[:, c, 512 * g:512 * (g + 1)], ALU.mult).then_inc(y_ready, 1)

            unit_in(0)
            unit_in(1)
            unit_mid(0)
            for q in range(3):
                dve.wait_ge(acc_done[q], len([m for m in range(pr0["ssd"]) if m % 3 == q]))
            for u in range(8):
                if u < 7:
                    unit_mid(u + 1)
                unit_out(u)
                if u < 6:
                    unit_in(u + 2)
            dve.wait_ge(yss_ready, 8)
            own(dve.reduce_sum(ss[:, :], yss[:, :, :], axis=AX.X))
            dve.tensor_scalar(ms[:, :], ss[:, :], 1.0 / DI, EPS, ALU.mult, ALU.add).then_inc(yms_ready, 1)
            dve.wait_ge(yroot, 1)
            own(dve.reciprocal(rs[:, :], rs[:, :]))
            dve.wait_ge(ld_norm, 16)
            def y_scaled(q):
                for t in range(T):
                    cols = slice(q * HALF, (q + 1) * HALF)
                    dve.scalar_tensor_tensor(xbc[:, t, cols], xbc[:, t, cols], rs[:, t:t + 1],
                                             mod[:, q // 2, (q % 2) * HALF:(q % 2 + 1) * HALF], ALU.mult, ALU.mult).then_inc(yn_ready, 1)

            def y_turned(q):
                for t in range(T):
                    part = (slice(None), slice(4 * q, 4 * q + 4), slice(t * P, (t + 1) * P))
                    piece_lo(pc0["ynorm"] + T * q + t, (y_hi[part], y_lo[part]))

            y_scaled(0)
            early_lo("wout", 0, 1)
            y_turned(0)
            early_lo("wout", 1, 2)
            y_scaled(1)
            early_lo("wout", 2)
            y_scaled(2)
            y_scaled(3)
            dve.wait_ge(small_hi, 2)
            dve.tensor_tensor(w_r_lo[:, :, :], w_r[:, :, :], r32(w_r_hi[:, :, :]), ALU.subtract).then_inc(small_lo, 1)
            gemm("wout", (2 * KD,), lambda i: y_turned(i // 4 + 1) if i % 4 == 3 and i < 12 else None)
            own(dve.memset(comb[:, :, :], 0.0))
            own(dve.memset(slot_of[:, :, :], -1.0))
            own(dve.memset(y_sum[:, :, :], 0.0))
            own(dve.memset(r32(put[:, :, :]), 0.0))
            residual("wout", 0, mod[:, MOD_SLOT[1][2], :])
            norm(3, "norm3")

            own(dve.memset(acc[2][:, :], 0.0))
            dve.wait_ge(xb_full, pc0["route"] + 2)
            b = xb[(pc0["route"] + 1) % 2]
            own(dve.tensor_copy(lg[:, :, :], b[:, 0:T * EXPERTS].rearrange("p (t m) -> p t m", t=T)))
            dve.sem_inc(xb_done[(pc0["route"] + 1) % 2], 1)
            for t in range(T):
                own(dve.max(mx[:, t, :], lg[:, t, :]))
                own(dve.max_index(mi[:, t, :], mx[:, t, :], lg[:, t, :]))
            own(dve.tensor_copy(mif[:, :, :], mi[:, :, :]))
            own(dve.tensor_tensor(tw[:, :, 0], mx[:, :, 1], mx[:, :, 0], ALU.subtract))
            dve.sem_inc(tw_in, 1)
            for q in range(2):
                own(dve.tensor_tensor(oh[:, :, q, :], column[:, 0:EXPERTS].unsqueeze(1).to_broadcast([P, T, EXPERTS]),
                                      mif[:, :, q:q + 1].to_broadcast([P, T, EXPERTS]), ALU.is_equal))
            own(dve.tensor_tensor(msk[:, :, :], oh[:, :, 0, :], oh[:, :, 1, :], ALU.add))
            dve.sem_inc(mask_ready, 1)
            dve.wait_ge(tw_exp, 1)
            own(dve.tensor_scalar(tw[:, :, 1], tw[:, :, 0], 1.0, None, ALU.add))
            own(dve.reciprocal(tw[:, :, 1], tw[:, :, 1]))
            own(dve.tensor_tensor(tw[:, :, 2], tw[:, :, 0], tw[:, :, 1], ALU.mult))
            for q, to in ((0, comb[:, :, 1:1 + EXPERTS]), (1, lg[:, :, :])):
                own(dve.tensor_tensor(to, oh[:, :, q, :], tw[:, :, 1 + q:2 + q].to_broadcast([P, T, EXPERTS]), ALU.mult))
            own(dve.tensor_tensor(comb[:, :, 1:1 + EXPERTS], comb[:, :, 1:1 + EXPERTS], lg[:, :, :], ALU.add))
            c = pc0["route"] + 2
            dve.wait_ge(xb_full, c + 1)
            b = xb[c % 2]
            own(dve.scalar_tensor_tensor(slot_of[:, :, 0:EXPERTS], b[:, 0:T * EXPERTS].rearrange("p (t m) -> p t m", t=T), 1.0, msk[:, :, :],
                                         ALU.add, ALU.mult))
            own(dve.tensor_scalar(slot_of[:, :, 0:EXPERTS], slot_of[:, :, 0:EXPERTS], -1.0, None, ALU.add))
            own(dve.reduce_max(cmax[:, :], b[:, 2 * EXPERTS:3 * EXPERTS], axis=AX.X))
            dve.sem_inc(xb_done[c % 2], 1)
            own(dve.tensor_copy(flag[:, :], cmax[0:1, :]))
            dve.sem_inc(route_ready, 1)

            highs_moe = lows[0]

            def experts(rnd):
                if rnd:
                    for q in range(2):
                        dve.wait_ge(xb_done[q], (pc0["moe"] + ROUND_PIECES + 1 - q) // 2)
                    own(dve.tensor_scalar(slot_of[:, :, :], slot_of[:, :, :], -float(P), None, ALU.add))
                    own(dve.memset(r32(put[:, :, :]), 0.0))
                    dve.sem_inc(route_ready, 1)
                build_pick(0, rnd)
                if not rnd:
                    for t in range(T):
                        dve.wait_ge(t_hi_ready, t + 1)
                        dve.tensor_tensor(t_lo[:, t, :], hm[:, t, :], r32(t_hi[:, t, :]), ALU.subtract).then_inc(t_lo_ready, 1)
                for q in range(2):
                    c = pc0["moe"] + rnd * ROUND_PIECES + 2 + q
                    dve.wait_ge(xb_full, c + 1)
                    dve.tensor_copy(g_lo[:, 4 * q:4 * q + 4, :], xb[c % 2][:, :].rearrange("p (k m) -> p k m", k=4)).then_inc(xb_done[c % 2], 1)
                with dve.Fori(0, EXPERTS) as e:
                    body(Body(True, e, rnd))
                dve.wait_ge(yd_hi_ready, (rnd + 1) * (EXPERTS + 1))
                dve.tensor_tensor(yd_lo[:, :], acc[2][:, :], r32(yd_hi[:, :]), ALU.subtract).then_inc(yd_lo_ready, 1)
                for n in range(4):
                    scatter_sum(pc0["moe"] + rnd * ROUND_PIECES + 4 + 16 * EXPERTS + n, n // 2, n % 2, EXPERTS)

            experts(0)
            most = dve.value_load(flag[0:1, 0:1], min_val=0, max_val=SEQ)
            with dve.If(most > overflow_at):
                experts(1)
            for q in range(2):
                dve.wait_ge(xb_done[q], (pc0["moe"] + ROUND_PIECES + 1 - q) // 2)
            for t in range(T):
                dve.tensor_tensor(y_sum[:, t, :], y_sum[:, t, :], mod[:, MOD_SLOT[1][5], :], ALU.mult).then_inc(final_step, 1)
                dve.wait_ge(final_step, 2 * t + 1)
                dve.tensor_tensor(x[:, t, :], x[:, t, :], y_sum[:, t, :], ALU.add).then_inc(final_step, 1)
            dve.wait_ge(final_step, 2 * T)
            dve.sem_inc(x_ready, 1)

        @block.tensor
        def _(pe):
            def open_piece(c, e=0, per=0):
                if c >= 2:
                    pe.wait_ge(xb_done[c % 2], c // 2 + rep(e, per // 2))
                return xb[c % 2]

            def open_pair(q, used):
                if not isinstance(used, int) or used:
                    pe.wait_ge(acc_done[q], used)
                return acc[q]

            def keep_warm(n, q):
                for _ in range(n):
                    pe.matmul(acc[q][:, 0:HALF], ident, square[:, 0:4, :].rearrange("p n m -> p (n m)"), start=True, stop=True)

            def weight_tile(w, parts, pairs, lhs, tiles, first, last, e=0, no=0, stage_end=False):
                l_hi, l_lo = lhs
                hi, lo = w_hi[:, w % SPLIT, :], w_lo[:, w % SPLIT, :]
                pe.wait_ge(hi_ready, w + 1 + rep(e, BODY))
                for t in range(tiles):
                    rows_ = slice(t * P, (t + 1) * P)
                    if first:
                        open_pair(*pairs[t])
                    for m, (k, to, col) in enumerate(parts):
                        o = acc[pairs[t][0]][:, to:to + HALF]
                        new = first and (m == 0 or parts[m][1] != parts[m - 1][1])
                        pe.matmul(o, l_hi[:, k, rows_], hi[:, col:col + HALF], start=new, stop=False)
                        pe.matmul(o, l_lo[:, k, rows_], hi[:, col:col + HALF], start=False, stop=False)
                    if t == 0:
                        pe.wait_ge(raw_used, no + 1 + rep(e, BODY))
                    for m, (k, to, col) in enumerate(parts):
                        o = acc[pairs[t][0]][:, to:to + HALF]
                        end = last and (m == len(parts) - 1 or parts[m][1] != parts[m + 1][1])
                        mm = pe.matmul(o, l_hi[:, k, rows_], lo[:, col:col + HALF], start=False, stop=end)
                    if stage_end and t < tiles - 1:
                        mm.then_inc(rows_full, 1)
                mm.then_inc(w_used, 1)

            def gemm(stage, groups, lhs, after=None, rows_of=None):
                i = 0
                for gi, tiles in enumerate(groups):
                    pr = pr0[stage] + T * gi
                    pairs = [((pr + t) % 3, (pr + t) // 3) for t in range(T)]
                    for n, parts in enumerate(tiles):
                        if rows_of and i == KD // 2:
                            turned(rows_of, 1)
                        weight_tile(spl0[stage] + i, parts, pairs, lhs, T, n == 0, n == len(tiles) - 1, no=raw0[stage] + i,
                                    stage_end=stage in ("wo", "wout") and n == len(tiles) - 1)
                        if rows_of and i == 0:
                            norm_rest(int(rows_of[-1]), rows_of)
                        if after:
                            after(i)
                        i += 1

            def wide(k):
                return [(k, 0, 0), (k, HALF, HALF)]

            def turn(c, src, n):
                b = open_piece(c)
                for m in range(n):
                    mm = pe.transpose(b[:, m * P:(m + 1) * P], src(m), ident)
                mm.then_inc(xb_full, 1)

            def norm(n, stage, free):
                open_pair(free % 3, pair_uses0[free % 3] if n == 3 else free // 3)
                keep_warm(WARM_NORM, free % 3)
                for t in range(T):
                    norm_turn(n, stage, t)
                turned(stage, 0)

            def norm_turn(n, stage, m):
                hf, t = divmod(m, T)
                pe.wait_ge(hm_ready, 2 * T * n + m + 1)
                turn(pc0[stage] + m, lambda m: hm[:, t, (4 * hf + m) * P:(4 * hf + m + 1) * P], 4)

            def norm_rest(n, stage):
                for t in range(T):
                    norm_turn(n, stage, T + t)

            def turned(stage, hf):
                for c in range(pc0[stage] + T * hf, pc0[stage] + T * (hf + 1)):
                    pe.wait_ge(xb_done[c % 2], c // 2 + 1)

            def pieces_on(q, c):
                return (c + 1 - q) // 2

            pe.wait_ge(ld_square, 32)
            pe.wait_ge(ld_vecs, 48)
            pe.transpose(xb[0][:, 0:P], vec_rows[:, :], ident).then_inc(xb_full, 1)
            pe.wait_ge(relb_set, 3)
            pe.wait_ge(ld_tab, 32)
            pe.matmul(xb[1][0:HEADS, 0:3 * P], relb[:, :], table[:, :], start=True, stop=True).then_inc(xb_full, 1)
            pe.wait_ge(ld_rows, 16)

            def one_ada(c, n, pc):
                b = open_piece(pc)
                cols = slice(n * HALF, (n + 1) * HALF)
                if IS_SCALE[c]:
                    pe.matmul(b[:, :], ident[0:12, 6 + c:7 + c].to_broadcast([12, P]), bias_rows[:, cols], start=True, stop=False)
                pe.matmul(b[:, :], ones, ada[:, c % 2, cols], start=not IS_SCALE[c], stop=True).then_inc(xb_full, 1)
                if n == 1:
                    pe.wait_ge(xb_full, pc + 1)
                    pe.sem_inc(ada_ready, 1)

            HALVES = (slice(0, HALF), slice(HALF, 2 * HALF))

            def ada_bias(c):
                pair = ada_pair(c)
                open_pair(pair % 3, pair // 3)
                for cols in HALVES:
                    pe.matmul(acc[pair % 3][:, cols], ident[0:12, c:c + 1].to_broadcast([12, P]), bias_rows[:, cols],
                              start=True, stop=False)

            def ada_sum(c):
                ada_bias(c)
                pe.wait_ge(raw_used, raw0["attend"] + (c - 1) * KD)
                for cols in HALVES:
                    mm = pe.matmul(acc[ada_pair(c) % 3][:, cols], ones, ada[:, c % 2, cols], start=False, stop=True)
                mm.then_inc(ada_ready, 1)

            def ada_tiles():
                for i in range(2 * KD):
                    c, k = divmod(i, KD)
                    no, w, pair = raw0["ada"] + i, spl0["ada"] + i, ada_pair(c)
                    if k == 0:
                        ada_bias(c)
                    pe.wait_ge(hi_ready, w + 1)
                    halves = [(acc[pair % 3][:, cols], w_hi[:, w % SPLIT, cols], w_lo[:, w % SPLIT, cols])
                              for cols in HALVES]
                    for part in (cond_hi, cond_lo):
                        for o, hi, lo in halves:
                            pe.matmul(o, part[:, k:k + 1].to_broadcast([P, P]), hi, start=False, stop=False)
                    pe.wait_ge(raw_used, no + 1)
                    for o, hi, lo in halves:
                        mm = pe.matmul(o, cond_hi[:, k:k + 1].to_broadcast([P, P]), lo, start=False, stop=k == KD - 1)
                    mm.then_inc(w_used, 1)

            pe.wait_ge(cond_ready, 3)
            ada_tiles()
            norm(0, "norm0", pr0["qkv"])
            gemm("qkv", [[wide(k) for k in range(KD)], [[(k, 0, 0), (k + 1, 0, HALF)] for k in range(0, KD, 2)]], (a_hi, a_lo), rows_of="norm0")
            def bias_turn(g):
                if g == 2:
                    pe.wait_ge(ld_bias[1], 16 * 2)
                for m in range(2):
                    pe.matmul(open_piece(bias_piece[g] + m)[:, :], reversal,
                              bias_rev[g][:, 2 * m:2 * m + 2, :].rearrange("p k m -> p (k m)"),
                              start=True, stop=True).then_inc(xb_full, 1)

            for t in range(T):
                pe.wait_ge(qk_ready, t + 1)
                for part in range(2):
                    turn(turn_piece(t, part), lambda m: qkv[:, t, (4 * part + m) * P:(4 * part + m + 1) * P], 4)
            pe.wait_ge(ld_bias[0], 16 * 2)
            bias_turn(0)
            for t in range(T):
                pe.wait_ge(qk_ready, T + 2 * t + 2)
                turn(turn_piece(t, 2), lambda m: k2[:, t, m].rearrange("p a d -> p (a d)"), 4)
            for q in range(2):
                pe.wait_ge(xb_done[q], pieces_on(q, pc0["attend"]))

            def scores(u):
                g, blk = UNITS[u]
                w = P * (blk + 1)
                n = score_pair(u)
                o = open_pair(n % 3, n // 3)
                for i in range(GQ):
                    hh = HD * (i % 2)
                    at_ = HALF * (i % 2) + w * (i // 2)
                    mm = pe.matmul(o[:, at_:at_ + w], q_t[hh:hh + HD, (GQ * g + i) // 2, blk * P:(blk + 1) * P],
                                   k_t[hh:hh + HD, g, 0:w], start=True, stop=True)
                mm.then_inc(acc_full, 1)

            def turn_probs(u):
                g, blk = UNITS[u]
                w = P * (blk + 1)
                pe.wait_ge(p_ready, u + 1)
                for kc in range(blk + 1):
                    turn(att_piece[u] + kc, lambda m: sc[:, u % 2, m * w + kc * P:m * w + (kc + 1) * P], GQ)

            def attend(u):
                g, blk = UNITS[u]
                for kc in range(blk + 1):
                    c = att_piece[u] + kc
                    pe.wait_ge(xb_done[c % 2], c // 2 + 1)
                o = open_piece(out_piece[u])
                for odd in range(2):
                    for kc in range(blk + 1):
                        probs = p_t[blk][:, kc, 2 * P * odd:2 * P * (odd + 1)].rearrange("p (i m) -> p i m", i=2)
                        mm = pe.matmul(o[HD * odd:HD * (odd + 1), 0:2 * P].rearrange("p (i m) -> p i m", i=2),
                                       qkv[:, kc, D + KV * HD + g * HD:D + KV * HD + (g + 1) * HD], probs,
                                       start=kc == 0, stop=kc == blk)
                mm.then_inc(xb_full, 1)

            scores(0)
            scores(1)
            for u in range(8):
                if u:
                    attend(u - 1)
                if u < 6:
                    scores(u + 2)
                turn_probs(u)
                if u < KV - 1:
                    bias_turn(u + 1)
                if u and u % 2 == 0:
                    ada_sum(1 + u // 2)
            attend(7)
            ada_sum(5)
            for q in range(2):
                pe.wait_ge(xb_done[q], pieces_on(q, pc0["wo"]))
            gemm("wo", [[wide(k) for k in range(KD)]], (a_hi, a_lo))
            norm(1, "norm1", pr0["ffn"])

            def body(B):
                e = B.e
                per = 16 if B.mixture else 0
                gu = (g_hi, g_lo) if B.mixture else (a_hi, a_lo)
                hid = (e_hi, e_lo) if B.mixture else (h_hi, h_lo)
                for s in range(BODY):
                    if s < FJ * KD:
                        j, k = divmod(s, KD)
                        first, last, lhs = k == 0, k == KD - 1, gu
                    else:
                        j, k = FJ, s - FJ * KD
                        first, last, lhs = k == 0, k == FK - 1, hid
                        if k % 4 == 0:
                            for c, *what in [w for v in PIECES[B.mixture].values() for w in v]:
                                if what[0] == "h" and what[1] == k // 4:
                                    c += B.pc
                                    pe.wait_ge(xb_done[c % 2], c // 2 + 1 + rep(e, per // 2))
                    if B.mixture and s == 0:
                        for c in (B.pc - 2, B.pc - 1):
                            pe.wait_ge(xb_done[c % 2], c // 2 + 1 + rep(e, per // 2))
                    if not B.mixture and s == KD // 2:
                        turned("norm1", 1)
                    if B.mixture and first and j == FJ:
                        pairs = [(2, B.pair(FJ, 0)[1] + 1)]
                    else:
                        pairs = [B.pair(j, t) for t in range(B.tiles)]
                    weight_tile(B.spl + s, wide(k), pairs, lhs, B.tiles, first, last, e, B.raw_no(s),
                                stage_end=not B.mixture and s == BODY - 1)
                    if not B.mixture and s == 0:
                        norm_rest(1, "norm1")
                    for c, kind, *which in PIECES[B.mixture].get(s, []):
                        c += B.pc
                        if kind == "h":
                            j, t = which
                            q, used = B.pair(j, t)
                            pe.wait_ge(acc_done[q], used + 1)
                            b = open_piece(c, e, per)
                            for m in range(4):
                                mm = pe.transpose(b[:, m * P:(m + 1) * P], h[:, t, m * P:(m + 1) * P], ident)
                            mm.then_inc(xb_full, 1)
                        elif kind == "ada":
                            cc, n = which
                            if n == 0:
                                pe.wait_ge(raw_used, ada_group_end[cc])
                            one_ada(cc, n, c)
                        elif kind == "scatter":
                            t, hf = which
                            pe.wait_ge(acc_done[2], B.pair(FJ, 0)[1] + 1)
                            scatter(c, t, hf, e, per)
                        elif kind == "put":
                            b = open_piece(c, e, per)
                            for t in range(T):
                                mm = pe.transpose(b[:, t * P:(t + 1) * P], r32(pick[:, t, :]), ident)
                            mm.then_inc(xb_full, 1)
                        elif kind == "gather":
                            gather(c, which[0], which[1], e, per, B.rnd)

            def scatter(c, t, hf, e, per):
                b = open_piece(c, e, per)
                cols = slice(hf * HALF, (hf + 1) * HALF)
                pe.matmul(b[:, :], put[:, t, :], yd_hi[:, cols], start=True, stop=False)
                pe.matmul(b[:, :], put[:, t, :], yd_lo[:, cols], start=False, stop=True).then_inc(xb_full, 1)

            def gather(c, low, hf, e, per, rnd):
                if low == 0 and hf == 0:
                    pe.wait_ge(pick_ready, rnd * T * (EXPERTS + 1) + T + rep(e, T) + (T if per else 0))
                b = open_piece(c, e, per)
                src = t_lo if low else t_hi
                for m in range(4):
                    for t in range(T):
                        mm = pe.matmul(b[:, m * P:(m + 1) * P], src[:, t, (4 * hf + m) * P:(4 * hf + m + 1) * P], pick[:, t, :],
                                       start=t == 0, stop=t == T - 1)
                mm.then_inc(xb_full, 1)

            ada_group_end, n = {}, 0
            for s in range(BODY):
                if ada_after(s):
                    n += 1
                    if n % KD == 0:
                        ada_group_end[n // KD - 1] = Body(False).raw_no(s) + 2
            body(Body(False))
            norm(2, "norm2", pr0["proj"])

            def narrow(c, w_hi_, w_lo_, n):
                b = open_piece(c)
                parts = [(w, a, k) for k in range(KD) for w, a in ((w_hi_, a_hi), (w_hi_, a_lo), (w_lo_, a_hi))]
                for m, (w, a, k) in enumerate(parts):
                    mm = pe.matmul(b[0:n, 0:SEQ], w[:, k, :], a[:, k, :], start=m == 0, stop=m == len(parts) - 1)
                mm.then_inc(xb_full, 1)

            def narrow_turn(c, source, rows_, n):
                pe.wait_ge(xb_done[source % 2], source // 2 + 1)
                b = open_piece(c)
                for t in range(T):
                    mm = pe.transpose(b[:, t * n:(t + 1) * n], rows_[:, t * P:(t + 1) * P], ident[0:n, 0:n])
                mm.then_inc(xb_full, 1)

            def dt_product():
                pe.wait_ge(small_hi, 1)
                pe.wait_ge(small_lo, 1)
                narrow(proj_piece["dt"], w_dt_hi, w_dt_lo, SH)

            def run_sums():
                pe.wait_ge(dta_ready, 1)
                b = open_piece(proj_piece["sums"])
                for n in range(2 * T):
                    mm = pe.matmul(b[:, n * SH:(n + 1) * SH], tri if n < T else ones, dt_a[:, n % T, :], start=True, stop=True)
                mm.then_inc(xb_full, 1)

            def mixer_steps(i):
                if i == DT_AT:
                    dt_product()
                if i == DT_TURN_AT:
                    narrow_turn(proj_piece["dt_turn"], proj_piece["dt"], dt_rows, SH)
                if i == SUMS_AT:
                    run_sums()
                for q in range(CBACK):
                    if i == conv_back_at(q):
                        pe.wait_ge(cs_ready, q + 1)
                        if q < 8:
                            turn(cv_piece["b", q], lambda m: cv[:, q % 2, m % 2, (m // 2) * P:(m // 2 + 1) * P], 4)
                        else:
                            turn(cv_piece["b", q], lambda m: b_t[:, 2 * (q % 2) + m % 2, (m // 2) * P:(m // 2 + 1) * P], 4)
                for q in range(NCV):
                    if i == conv_in_at(q):
                        for n in range(pr0["proj"] + T * (q // 4), pr0["proj"] + T * (q // 4 + 1)):
                            pe.wait_ge(acc_done[n % 3], n // 3 + 1)
                        turn(cv_piece["f", q], lambda m: xbc[:, m % 2, (2 * q + m // 2) * P:(2 * q + m // 2 + 1) * P], 4)

            gemm("proj", [[wide(k) for k in range(KD)]] * 5, (a_hi, a_lo), mixer_steps, "norm2")
            pe.wait_ge(cs_ready, NCV)

            def unit_in(u):
                c, g = SUNITS[u]
                n = ssd_pair["a", u]
                o = open_pair(n % 3, n // 3)
                for i in range(HG):
                    mm = pe.matmul(o[:, i * P:(i + 1) * P], dt_a[:, c, HG * g + i:HG * g + i + 1].to_broadcast([P, P]), tri,
                                   start=True, stop=True)
                mm.then_inc(acc_full, 1)
                pc = pc0["ssd"] + u
                b = open_piece(pc)
                pe.matmul(b[:, 0:P], b_t[:, g, c * P:(c + 1) * P], c_t[:, g, c * P:(c + 1) * P], start=True, stop=True).then_inc(xb_full, 1)

            def unit_out(u):
                c, g = SUNITS[u]
                n = ssd_pair["y", u]
                o = open_pair(n % 3, n // 3)
                if u == 0:
                    keep_warm(WARM_SSD, n % 3)
                pe.wait_ge(mt_ready, u + 1)
                if c == 0:
                    pe.matmul(o[:, HALF:2 * HALF], xbc[:, c, DI + g * NS:DI + (g + 1) * NS], xde[:, u % 2, :], start=True, stop=True)
                else:
                    pe.wait_ge(state_ready, g + 1)
                    pe.matmul(o[:, HALF:2 * HALF], c_t[:, g, c * P:(c + 1) * P], state[:, g, :], start=True, stop=True)
                for i in range(HG):
                    mm = pe.matmul(o[:, i * SHD:(i + 1) * SHD], dec[:, u % 2, i * P:(i + 1) * P],
                                   xd[:, u % 2, i * SHD:(i + 1) * SHD], start=True, stop=True)
                mm.then_inc(acc_full, 1)

            unit_in(0)
            unit_in(1)
            for u in range(8):
                unit_out(u)
                if u < 6:
                    unit_in(u + 2)
            def y_turn(q):
                for t in range(T):
                    pe.wait_ge(yn_ready, T * q + t + 1)
                    turn(pc0["ynorm"] + T * q + t, lambda m: xbc[:, t, (4 * q + m) * P:(4 * q + m + 1) * P], 4)

            def y_stands(q):
                for c in range(pc0["ynorm"] + T * q, pc0["ynorm"] + T * (q + 1)):
                    pe.wait_ge(xb_done[c % 2], c // 2 + 1)

            def wout_steps(i):
                if i % 4 == 0 and i < 12:
                    y_turn(i // 4 + 1)
                if i % 4 == 3 and i < 15:
                    y_stands(i // 4 + 1)

            open_pair(pr0["wout"] % 3, pr0["wout"] // 3)
            keep_warm(WARM_Y, pr0["wout"] % 3)
            y_turn(0)
            y_stands(0)
            gemm("wout", [[wide(k) for k in range(2 * KD)]], (y_hi, y_lo), wout_steps)
            norm(3, "norm3", 1)
            norm_rest(3, "norm3")

            pe.wait_ge(small_hi, 2)
            pe.wait_ge(small_lo, 2)
            turned("norm3", 1)
            narrow(pc0["route"], w_r_hi, w_r_lo, EXPERTS)
            narrow_turn(pc0["route"] + 1, pc0["route"], lg_rows, EXPERTS)
            keep_warm(WARM_MASK, 1)
            pe.wait_ge(mask_ready, 1)
            b = open_piece(pc0["route"] + 2)
            pe.matmul(b[:, 0:EXPERTS], tri_strict, msk[:, 0, :], start=True, stop=True)
            pe.matmul(b[:, EXPERTS:2 * EXPERTS], tri_strict, msk[:, 1, :], start=True, stop=False)
            pe.matmul(b[:, EXPERTS:2 * EXPERTS], ones, msk[:, 0, :], start=False, stop=True)
            pe.matmul(b[:, 2 * EXPERTS:3 * EXPERTS], ones, msk[:, 0, :], start=True, stop=False)
            pe.matmul(b[:, 2 * EXPERTS:3 * EXPERTS], ones, msk[:, 1, :], start=False, stop=True).then_inc(xb_full, 1)

            def experts(rnd):
                if not rnd:
                    keep_warm(WARM_ROUTE, 1)
                pe.wait_ge(route_ready, rnd + 1)
                pe.wait_ge(t_hi_ready, T)
                for n in range(4):
                    if n == 2:
                        pe.wait_ge(t_lo_ready, T)
                    gather(pc0["moe"] + rnd * ROUND_PIECES + n, n // 2, n % 2, 0, 0, rnd)
                with pe.Fori(0, EXPERTS) as e:
                    body(Body(True, e, rnd))
                pe.wait_ge(yd_lo_ready, rnd + 1)
                for n in range(4):
                    scatter(pc0["moe"] + rnd * ROUND_PIECES + 4 + 16 * EXPERTS + n, n // 2, n % 2, 0, 0)

            experts(0)
            most = pe.value_load(flag[0:1, 0:1], min_val=0, max_val=SEQ)
            with pe.If(most > overflow_at):
                experts(1)


_INS = ["x", "c", "ada_w", "ada_b", "norm_gain", "rel_bias", "attn_w_qkv", "attn_q_gain", "attn_k_gain",
        "attn_sinks", "attn_w_o", "ssm_w_in", "ssm_conv_w", "ssm_conv_b", "ssm_dt_bias", "ssm_a_log",
        "ssm_d", "ssm_norm_w", "ssm_w_out", "ffn_w_gu", "ffn_w_down", "moe_w_router", "moe_w_gu", "moe_w_down"]


def kernel(**inputs):
    import concourse.bacc as bacc
    from concourse.bass_utils import run_bass_kernel_spmd

    nc = bacc.Bacc("TRN2", target_bir_lowering=False, num_devices=1)
    f32 = mybir.dt.float32
    arrays = {name: np.ascontiguousarray(inputs[name]) for name in _INS}
    arrays["square"], arrays["table"] = shape_constants()
    A = {name: nc.dram_tensor(f"in_{name}", a.shape, f32, kind="ExternalInput").ap() for name, a in arrays.items()}
    out = nc.dram_tensor("out", (1, SEQ, D), f32, kind="ExternalOutput").ap()
    build(nc, A, out, A["square"], A["table"])
    r = run_bass_kernel_spmd(nc, [{f"in_{name}": a for name, a in arrays.items()}], core_ids=[0])
    return r.results[0]["out"]
```
